# Optimizing a Trainium2 kernel written in Bass

```python
import math
import jax, jax.numpy as jnp
from jax import lax
import numpy as np

D_MODEL = 2048
BATCH = 1
SEQ = 512
DEPTH = 1

N_MEM = 256
N_MIXERS = 2
EXPAND = 2
INNER = EXPAND * D_MODEL
XA_HEADS = 4
XA_WIDTH = INNER // 4
XA_DIM = XA_WIDTH // XA_HEADS
MIX_WIDTH = INNER - XA_WIDTH
DN_HEAD_DIM = 128
DN_V_HEADS = MIX_WIDTH // DN_HEAD_DIM
DN_QK_HEADS = DN_V_HEADS // 2
DN_QK_WIDTH = DN_QK_HEADS * DN_HEAD_DIM
DN_CONV = 4
DN_CHUNK = 64
DN_MIX_COLS = 2 * DN_QK_WIDTH + MIX_WIDTH + 2 * DN_V_HEADS
DN_PROJ = DN_MIX_COLS + XA_WIDTH + INNER
SB_HEAD_DIM = 128
SB_HEADS = MIX_WIDTH // SB_HEAD_DIM
SB_BLOCK = 128
SB_MIX_COLS = 3 * MIX_WIDTH
SB_PROJ = SB_MIX_COLS + XA_WIDTH + INNER
EPS = 1e-6


def rms_norm(x, g):
    xf = x.astype(jnp.float32)
    y = xf * lax.rsqrt(jnp.mean(xf * xf, axis=-1, keepdims=True) + EPS)
    return (y * g.astype(jnp.float32)).astype(x.dtype)

def l2_norm(x):
    xf = x.astype(jnp.float32)
    return (xf * lax.rsqrt(jnp.sum(xf * xf, axis=-1, keepdims=True) + EPS)).astype(x.dtype)

def causal_depthwise_conv(x, w):
    c = x.shape[-1]
    return lax.conv_general_dilated(
        x, w[:, None, :].astype(x.dtype), window_strides=(1,),
        padding=((w.shape[0] - 1, 0),), dimension_numbers=("NWC", "WIO", "NWC"),
        feature_group_count=c)

def gated_delta_rule(q, k, v, g, beta):
    f32 = jnp.float32
    B, H, S, dk = q.shape
    dv = v.shape[-1]
    C, N = DN_CHUNK, S // DN_CHUNK
    q, k, v = (t.astype(f32).reshape(B, H, N, C, t.shape[-1]) for t in (q, k, v))
    g = g.astype(f32).reshape(B, H, N, C)
    beta = beta.astype(f32).reshape(B, H, N, C)
    gc = jnp.cumsum(g, axis=-1)
    idx = jnp.arange(C)
    incl = idx[:, None] >= idx[None, :]
    strict = idx[:, None] > idx[None, :]
    decay = jnp.exp(jnp.where(incl, gc[..., :, None] - gc[..., None, :], -jnp.inf))
    kk = jnp.einsum("bhncd,bhnjd->bhncj", k, k)
    m = jnp.where(strict, beta[..., :, None] * kk * decay, 0.0) + jnp.eye(C, dtype=f32)
    rhs = jnp.concatenate([v * beta[..., None], k * (beta * jnp.exp(gc))[..., None]], axis=-1)
    sol = lax.linalg.triangular_solve(m, rhs, left_side=True, lower=True, unit_diagonal=True)
    u0, w = sol[..., :dv], sol[..., dv:]
    qk = jnp.einsum("bhncd,bhnjd->bhncj", q, k) * decay
    q_dec = q * jnp.exp(gc)[..., None]
    k_dec = k * jnp.exp(gc[..., -1:] - gc)[..., None]
    chunk_decay = jnp.exp(gc[..., -1])

    def step(state, inp):
        u0_c, w_c, qk_c, qd_c, kd_c, cd_c = inp
        u = u0_c - jnp.einsum("bhcd,bhde->bhce", w_c, state)
        o = jnp.einsum("bhcd,bhde->bhce", qd_c, state) + jnp.einsum("bhcj,bhje->bhce", qk_c, u)
        state = cd_c[..., None, None] * state + jnp.einsum("bhcd,bhce->bhde", kd_c, u)
        return state, o

    xs = tuple(jnp.moveaxis(t, 2, 0) for t in (u0, w, qk, q_dec, k_dec, chunk_decay))
    _, o = lax.scan(step, jnp.zeros((B, H, dk, dv), f32), xs)
    return jnp.moveaxis(o, 0, 2).reshape(B, H, S, dv)

def deltanet_branch(p, conv_w, a_log, dt_bias, out_g):
    B, S, _ = p.shape
    c_qkv = 2 * DN_QK_WIDTH + MIX_WIDTH
    qkv = jax.nn.silu(causal_depthwise_conv(p[..., :c_qkv], conv_w))
    q = qkv[..., :DN_QK_WIDTH].reshape(B, S, DN_QK_HEADS, DN_HEAD_DIM)
    k = qkv[..., DN_QK_WIDTH:2 * DN_QK_WIDTH].reshape(B, S, DN_QK_HEADS, DN_HEAD_DIM)
    v = qkv[..., 2 * DN_QK_WIDTH:].reshape(B, S, DN_V_HEADS, DN_HEAD_DIM)
    a = p[..., c_qkv:c_qkv + DN_V_HEADS].astype(jnp.float32)
    b = p[..., c_qkv + DN_V_HEADS:].astype(jnp.float32)
    rep = DN_V_HEADS // DN_QK_HEADS
    q = jnp.repeat(l2_norm(q), rep, axis=2) * DN_HEAD_DIM ** -0.5
    k = jnp.repeat(l2_norm(k), rep, axis=2)
    g = -jnp.exp(a_log.astype(jnp.float32)) * jax.nn.softplus(a + dt_bias.astype(jnp.float32))
    beta = jax.nn.sigmoid(b)
    o = gated_delta_rule(q.transpose(0, 2, 1, 3), k.transpose(0, 2, 1, 3), v.transpose(0, 2, 1, 3),
                         g.transpose(0, 2, 1), beta.transpose(0, 2, 1))
    o = rms_norm(o.astype(p.dtype), out_g)
    return o.transpose(0, 2, 1, 3).reshape(B, S, MIX_WIDTH)

def stick_breaking_attention(q, k, v):
    B, H, S, d = q.shape
    scale = d ** -0.5
    outs = []
    for blk in range(S // SB_BLOCK):
        q0 = blk * SB_BLOCK
        kv_len = q0 + SB_BLOCK
        qb = q[:, :, q0:kv_len]
        kb, vb = k[:, :, :kv_len], v[:, :, :kv_len]
        z = jnp.einsum("bhtd,bhsd->bhts", qb, kb).astype(jnp.float32) * scale
        t_pos = q0 + jnp.arange(SB_BLOCK)
        s_pos = jnp.arange(kv_len)
        mask = s_pos[None, :] < t_pos[:, None]
        log_rest = jnp.where(mask, jax.nn.log_sigmoid(-z), 0.0)
        later = lax.cumsum(log_rest, axis=3, reverse=True) - log_rest
        wts = jnp.where(mask, jnp.exp(jax.nn.log_sigmoid(z) + later), 0.0)
        outs.append(jnp.einsum("bhts,bhsd->bhtd", wts.astype(v.dtype), vb))
    return jnp.concatenate(outs, axis=2)

def stick_breaking_branch(p, qn_g, kn_g):
    B, S, _ = p.shape
    q, k, v = (t.reshape(B, S, SB_HEADS, SB_HEAD_DIM) for t in jnp.split(p, 3, axis=-1))
    q, k = rms_norm(q, qn_g), rms_norm(k, kn_g)
    o = stick_breaking_attention(q.transpose(0, 2, 1, 3), k.transpose(0, 2, 1, 3), v.transpose(0, 2, 1, 3))
    return o.transpose(0, 2, 1, 3).reshape(B, S, MIX_WIDTH)

def memory_cross_attention(xq, mem_n, w_kv, qn_g, kn_g):
    B, S, _ = xq.shape
    q = rms_norm(xq.reshape(B, S, XA_HEADS, XA_DIM), qn_g)
    kv = jnp.einsum("bmd,de->bme", mem_n, w_kv)
    k = rms_norm(kv[..., :XA_WIDTH].reshape(B, -1, XA_HEADS, XA_DIM), kn_g)
    v = kv[..., XA_WIDTH:].reshape(B, -1, XA_HEADS, XA_DIM)
    s = jnp.einsum("bthd,bmhd->bhtm", q, k).astype(jnp.float32) * XA_DIM ** -0.5
    p = jax.nn.softmax(s, axis=-1).astype(v.dtype)
    return jnp.einsum("bhtm,bmhd->bthd", p, v).reshape(B, S, XA_WIDTH)

def first_inputs(seed: int = 0) -> dict:
    key = jax.random.key(seed)
    ks = jax.random.split(key, 20)
    f32 = jnp.float32
    n_dn = (DEPTH + N_MIXERS - 1) // N_MIXERS
    n_sb = DEPTH // N_MIXERS

    def dense(k, shape, fan_in):
        return jax.random.normal(k, shape, f32) * fan_in ** -0.5

    def gain(k, shape):
        return 1.0 + 0.02 * jax.random.normal(k, shape, f32)

    dt = jnp.exp(jax.random.uniform(ks[10], (n_dn, DN_V_HEADS), f32,
                                    minval=math.log(1e-3), maxval=math.log(1e-1)))
    return {
        "x": jax.random.normal(ks[0], (BATCH, SEQ, D_MODEL), f32),
        "mem": jax.random.normal(ks[1], (BATCH, N_MEM, D_MODEL), f32),
        "norm_g": gain(ks[2], (DEPTH, D_MODEL)),
        "mem_norm_g": gain(ks[3], (D_MODEL,)),
        "mem_w_kv": dense(ks[4], (DEPTH, D_MODEL, 2 * XA_WIDTH), D_MODEL),
        "xa_q_norm_g": gain(ks[5], (DEPTH, XA_DIM)),
        "xa_k_norm_g": gain(ks[6], (DEPTH, XA_DIM)),
        "w_out": dense(ks[7], (DEPTH, INNER, D_MODEL), INNER),
        "dn_w_in": dense(ks[8], (n_dn, D_MODEL, DN_PROJ), D_MODEL),
        "dn_conv_w": dense(ks[9], (n_dn, DN_CONV, 2 * DN_QK_WIDTH + MIX_WIDTH), DN_CONV),
        "dn_a_log": jnp.log(jax.random.uniform(ks[11], (n_dn, DN_V_HEADS), f32, minval=1.0, maxval=16.0)),
        "dn_dt_bias": dt + jnp.log(-jnp.expm1(-dt)),
        "dn_out_norm_g": gain(ks[12], (n_dn, DN_HEAD_DIM)),
        "sb_w_in": dense(ks[13], (n_sb, D_MODEL, SB_PROJ), D_MODEL),
        "sb_q_norm_g": gain(ks[14], (n_sb, SB_HEAD_DIM)),
        "sb_k_norm_g": gain(ks[15], (n_sb, SB_HEAD_DIM)),
    }

def first_block(x, mem, norm_g, mem_norm_g, mem_w_kv, xa_q_norm_g, xa_k_norm_g, w_out,
              dn_w_in, dn_conv_w, dn_a_log, dn_dt_bias, dn_out_norm_g,
              sb_w_in, sb_q_norm_g, sb_k_norm_g):
    mem_n = rms_norm(mem, mem_norm_g)
    for i in range(DEPTH):
        h = rms_norm(x, norm_g[i])
        j = i // N_MIXERS
        if i % N_MIXERS == 0:
            proj = jnp.einsum("bsd,de->bse", h, dn_w_in[j])
            mix = deltanet_branch(proj[..., :DN_MIX_COLS], dn_conv_w[j], dn_a_log[j],
                                  dn_dt_bias[j], dn_out_norm_g[j])
        else:
            proj = jnp.einsum("bsd,de->bse", h, sb_w_in[j])
            mix = stick_breaking_branch(proj[..., :SB_MIX_COLS], sb_q_norm_g[j], sb_k_norm_g[j])
        xq = proj[..., -(XA_WIDTH + INNER):-INNER]
        z = proj[..., -INNER:]
        xa = memory_cross_attention(xq, mem_n, mem_w_kv[i], xa_q_norm_g[i], xa_k_norm_g[i])
        y = jnp.concatenate([mix, xa], axis=-1) * jax.nn.silu(z)
        x = x + jnp.einsum("bse,ed->bsd", y, w_out[i])
    return x


PE_DIM = 256
MIX_WIDTH_2 = D_MODEL
ML_WIDTH = MIX_WIDTH_2 // 2
ML_HEADS = 4
ML_DV = ML_WIDTH // ML_HEADS
ML_DQK = ML_DV // 2
ML_QK = ML_HEADS * ML_DQK
ML_CONV = 4
ML_CHUNK = 64
HG_WIDTH = MIX_WIDTH_2 - ML_WIDTH
HG_EXPAND = 128
HG_HEADS = HG_WIDTH // HG_EXPAND
HG_DV = HG_WIDTH // HG_HEADS
HG_FDIM = HG_HEADS * HG_EXPAND
HG_CHUNK = 64

SPLIT_SIZES = (ML_QK, ML_QK, ML_WIDTH, ML_WIDTH, ML_WIDTH, ML_HEADS, ML_HEADS,
               HG_FDIM, HG_FDIM, HG_WIDTH, HG_WIDTH)
IN_COLS = sum(SPLIT_SIZES)


def rmsnorm(x, w):
    xf = x.astype(jnp.float32)
    return xf * lax.rsqrt(jnp.mean(xf * xf, axis=-1, keepdims=True) + EPS) * w.astype(jnp.float32)

def causal_dwconv(x, w, b):
    K = w.shape[0]
    S = x.shape[1]
    xp = jnp.pad(x, ((0, 0), (K - 1, 0), (0, 0)))
    y = xp[:, 0:S, :] * w[0]
    for k in range(1, K):
        y = y + xp[:, k:k + S, :] * w[k]
    return y + b

def to_chunks(x, L):
    Bn, S = x.shape[0], x.shape[1]
    x = x.reshape((Bn, S // L, L) + x.shape[2:])
    perm = (1, 0, 3, 2) + tuple(range(4, x.ndim))
    return x.transpose(perm)

def from_chunks(y):
    NC, Bn, H, L, d = y.shape
    return y.transpose(1, 0, 3, 2, 4).reshape(Bn, NC * L, H, d)

def mlstm_chunkwise(q, k, v, i_pre, f_pre):
    L = ML_CHUNK
    Bn, S, H, dqk = q.shape
    dv = v.shape[-1]
    k = k * (dqk ** -0.5)
    logf = jax.nn.log_sigmoid(f_pre)
    xs = (to_chunks(q, L), to_chunks(k, L), to_chunks(v, L), to_chunks(i_pre, L), to_chunks(logf, L))
    causal = jnp.tril(jnp.ones((L, L), dtype=bool))

    def step(carry, inp):
        C, n, m = carry
        qc, kc, vc, ig, lf = inp
        b = jnp.cumsum(lf, axis=-1)
        logD = jnp.where(causal, b[..., :, None] - b[..., None, :] + ig[..., None, :], -jnp.inf)
        inter_log = b + m[..., None]
        m_t = jnp.maximum(inter_log, jnp.max(logD, axis=-1))
        scores = jnp.einsum('bhtd,bhjd->bhtj', qc, kc) * jnp.exp(logD - m_t[..., None])
        w_inter = jnp.exp(inter_log - m_t)
        num = (jnp.einsum('bhtj,bhjv->bhtv', scores, vc)
               + w_inter[..., None] * jnp.einsum('bhtd,bhdv->bhtv', qc, C))
        den = jnp.sum(scores, axis=-1) + w_inter * jnp.einsum('bhtd,bhd->bht', qc, n)
        h = num / jnp.maximum(jnp.abs(den), jnp.exp(-m_t))[..., None]
        g = b[..., -1]
        a = g[..., None] - b + ig
        m_new = jnp.maximum(g + m, jnp.max(a, axis=-1))
        wa = jnp.exp(a - m_new[..., None])
        ws = jnp.exp(g + m - m_new)
        C_new = ws[..., None, None] * C + jnp.einsum('bhj,bhjd,bhjv->bhdv', wa, kc, vc)
        n_new = ws[..., None] * n + jnp.einsum('bhj,bhjd->bhd', wa, kc)
        return (C_new, n_new, m_new), h

    init = (jnp.zeros((Bn, H, dqk, dv), jnp.float32),
            jnp.zeros((Bn, H, dqk), jnp.float32),
            jnp.zeros((Bn, H), jnp.float32))
    _, hs = lax.scan(step, init, xs)
    return from_chunks(hs)

def hgrn2_chunkwise(q, k, logf, iv):
    L = HG_CHUNK
    Bn, S, H, E = q.shape
    dv = iv.shape[-1]
    xs = (to_chunks(q, L), to_chunks(k, L), to_chunks(logf, L), to_chunks(iv, L))
    causal = jnp.tril(jnp.ones((L, L), dtype=bool))[:, :, None]

    def step(Sst, inp):
        qc, kc, lf, vc = inp
        b = jnp.cumsum(lf, axis=2)
        decay = jnp.exp(jnp.where(causal, b[:, :, :, None, :] - b[:, :, None, :, :], -jnp.inf))
        A = jnp.einsum('bhte,bhje,bhtje->bhtj', qc, kc, decay)
        o = (jnp.einsum('bhtj,bhjv->bhtv', A, vc)
             + jnp.einsum('bhte,bhev->bhtv', qc * jnp.exp(b), Sst))
        g = b[:, :, -1, :]
        S_new = (jnp.exp(g)[..., None] * Sst
                 + jnp.einsum('bhje,bhjv->bhev', kc * jnp.exp(g[:, :, None, :] - b), vc))
        return S_new, o

    _, os_ = lax.scan(step, jnp.zeros((Bn, H, E, dv), jnp.float32), xs)
    return from_chunks(os_)

def second_inputs(seed: int = 0) -> dict:
    key = jax.random.key(seed)
    ks = jax.random.split(key, 16)
    f32 = jnp.float32
    nrm = lambda k, shape, s: jax.random.normal(k, shape, f32) * s
    x = jax.random.normal(ks[0], (BATCH, SEQ, D_MODEL), f32)
    p = jax.random.normal(ks[1], (DEPTH, BATCH, SEQ, PE_DIM), f32)
    norm_w = 1.0 + nrm(ks[2], (DEPTH, D_MODEL), 0.05)
    w_in = nrm(ks[3], (DEPTH, D_MODEL, IN_COLS), D_MODEL ** -0.5)
    conv_w = nrm(ks[4], (DEPTH, ML_CONV, 2 * ML_QK), ML_CONV ** -0.5)
    conv_b = nrm(ks[5], (DEPTH, 2 * ML_QK), 0.02)
    ml_b_i = nrm(ks[6], (DEPTH, ML_HEADS), 0.1)
    ml_b_f = jnp.linspace(3.0, 6.0, ML_HEADS, dtype=f32)[None, :] + nrm(ks[7], (DEPTH, ML_HEADS), 0.1)
    ml_norm_w = 1.0 + nrm(ks[8], (DEPTH, ML_WIDTH), 0.05)
    hg_lb = nrm(ks[9], (DEPTH + 1, HG_FDIM), 0.1)
    hg_norm_w = 1.0 + nrm(ks[10], (DEPTH, HG_WIDTH), 0.05)
    w_out = nrm(ks[11], (DEPTH, MIX_WIDTH_2, D_MODEL), MIX_WIDTH_2 ** -0.5)
    pe_norm_w = 1.0 + nrm(ks[12], (DEPTH, D_MODEL), 0.05)
    w_pg = nrm(ks[13], (DEPTH, D_MODEL, D_MODEL), D_MODEL ** -0.5)
    w_pe = nrm(ks[14], (DEPTH, PE_DIM, D_MODEL), PE_DIM ** -0.5)
    final_norm_w = 1.0 + nrm(ks[15], (D_MODEL,), 0.05)
    return {"x": x, "p": p, "norm_w": norm_w, "w_in": w_in, "conv_w": conv_w,
            "conv_b": conv_b, "ml_b_i": ml_b_i, "ml_b_f": ml_b_f, "ml_norm_w": ml_norm_w,
            "hg_lb": hg_lb, "hg_norm_w": hg_norm_w, "w_out": w_out, "pe_norm_w": pe_norm_w,
            "w_pg": w_pg, "w_pe": w_pe, "final_norm_w": final_norm_w}

def second_block(x, p, norm_w, w_in, conv_w, conv_b, ml_b_i, ml_b_f, ml_norm_w,
              hg_lb, hg_norm_w, w_out, pe_norm_w, w_pg, w_pe, final_norm_w):
    Bn, S, _ = x.shape
    split_points = [int(s) for s in np.cumsum(SPLIT_SIZES)[:-1]]
    lb_all = jnp.cumsum(jax.nn.softmax(hg_lb.astype(jnp.float32), axis=0), axis=0)
    h = x.astype(jnp.float32)
    for l in range(DEPTH):
        u = rmsnorm(h, norm_w[l])
        proj = jnp.einsum('bsd,dc->bsc', u, w_in[l].astype(jnp.float32))
        (ml_q, ml_k, ml_v, ml_o, ml_z, ml_i, ml_f,
         hg_q, hg_f, hg_i, hg_g) = jnp.split(proj, split_points, axis=-1)

        qk = jax.nn.silu(causal_dwconv(jnp.concatenate([ml_q, ml_k], axis=-1),
                                       conv_w[l].astype(jnp.float32), conv_b[l].astype(jnp.float32)))
        q_a = qk[..., :ML_QK].reshape(Bn, S, ML_HEADS, ML_DQK)
        k_a = qk[..., ML_QK:].reshape(Bn, S, ML_HEADS, ML_DQK)
        v_a = ml_v.reshape(Bn, S, ML_HEADS, ML_DV)
        i_pre = ml_i + ml_b_i[l].astype(jnp.float32)
        f_pre = ml_f + ml_b_f[l].astype(jnp.float32)
        h_a = mlstm_chunkwise(q_a, k_a, v_a, i_pre, f_pre)
        h_a = rmsnorm(h_a, ml_norm_w[l].reshape(ML_HEADS, ML_DV)).reshape(Bn, S, ML_WIDTH)
        y_a = jax.nn.sigmoid(ml_o) * h_a * jax.nn.silu(ml_z)

        lb = lb_all[l]
        f_b = lb + (1.0 - lb) * jax.nn.sigmoid(hg_f)
        logf_b = jnp.log(f_b).reshape(Bn, S, HG_HEADS, HG_EXPAND)
        k_b = ((1.0 - lb) * jax.nn.sigmoid(-hg_f)).reshape(Bn, S, HG_HEADS, HG_EXPAND)
        q_b = hg_q.reshape(Bn, S, HG_HEADS, HG_EXPAND)
        i_b = hg_i.reshape(Bn, S, HG_HEADS, HG_DV)
        h_b = hgrn2_chunkwise(q_b, k_b, logf_b, i_b)
        h_b = rmsnorm(h_b, hg_norm_w[l].reshape(HG_HEADS, HG_DV)).reshape(Bn, S, HG_WIDTH)
        y_b = h_b * jax.nn.silu(hg_g)

        y = jnp.concatenate([y_a, y_b], axis=-1)
        h = h + jnp.einsum('bsc,cd->bsd', y, w_out[l].astype(jnp.float32))

        e = jnp.einsum('bsr,rd->bsd', p[l].astype(jnp.float32), w_pe[l].astype(jnp.float32))
        gate = jax.nn.sigmoid(jnp.einsum('bsd,de->bse', rmsnorm(h, pe_norm_w[l]), w_pg[l].astype(jnp.float32)))
        h = h + gate * e
    out = rmsnorm(h, final_norm_w)
    return out.astype(x.dtype)


def setup_inputs(seed=0):
    out = dict(first_inputs(seed))
    for name, value in second_inputs(seed + 1).items():
        if name != "x":
            out[name + "_2"] = value
    return out


def reference(
    x, mem, norm_g, mem_norm_g, mem_w_kv, xa_q_norm_g, xa_k_norm_g, w_out, dn_w_in, dn_conv_w,
    dn_a_log, dn_dt_bias, dn_out_norm_g, sb_w_in, sb_q_norm_g, sb_k_norm_g, p_2, norm_w_2,
    w_in_2, conv_w_2, conv_b_2, ml_b_i_2, ml_b_f_2, ml_norm_w_2, hg_lb_2, hg_norm_w_2, w_out_2,
    pe_norm_w_2, w_pg_2, w_pe_2, final_norm_w_2,
):
    x = first_block(
        x, mem, norm_g, mem_norm_g, mem_w_kv, xa_q_norm_g, xa_k_norm_g, w_out, dn_w_in,
        dn_conv_w, dn_a_log, dn_dt_bias, dn_out_norm_g, sb_w_in, sb_q_norm_g, sb_k_norm_g,
    )
    return second_block(
        x, p_2, norm_w_2, w_in_2, conv_w_2, conv_b_2, ml_b_i_2, ml_b_f_2, ml_norm_w_2, hg_lb_2,
        hg_norm_w_2, w_out_2, pe_norm_w_2, w_pg_2, w_pe_2, final_norm_w_2,
    )


_drawn_inputs = setup_inputs


def setup_inputs(seed=0):
    import zlib

    import numpy as np

    out = dict(_drawn_inputs(seed))
    spreads = {}
    factors = {'norm_g': 3.185,
     'mem_norm_g': 8.0,
     'xa_q_norm_g': 8.0,
     'xa_k_norm_g': 8.0,
     'dn_out_norm_g': 20.991,
     'conv_b_2': 40.007,
     'ml_b_i_2': 64.0,
     'ml_norm_w_2': 49.296,
     'hg_norm_w_2': 28.896,
     'pe_norm_w_2': 200.0,
     'norm_w_2': 3.724,
     'hg_lb_2': 5.308,
     'p_2': 7.054,
     'w_pg_2': 8.0,
     'w_pe_2': 7.05}
    for name, (base, spread) in spreads.items():
        noise = np.random.default_rng([zlib.crc32(name.encode()), seed]).standard_normal(out[name].shape)
        drawn = base * np.exp(spread * noise) if base else spread * noise
        out[name] = __import__('jax').numpy.asarray(drawn.astype(out[name].dtype))
    for name, factor in factors.items():
        out[name] = (out[name] * factor).astype(out[name].dtype)
    return out
```

```python
from contextlib import ExitStack

import numpy as np
import concourse.bass as bass
from concourse import mybir

F32 = mybir.dt.float32
F32R = mybir.dt.float32r
U32 = mybir.dt.uint32
ALU = mybir.AluOpType
ACT = mybir.ActivationFunctionType
AX = mybir.AxisListType

P = 128
T = 512
D = 2048
KT = D // P
NB = T // P
M = 256
EPS = 1e-6
QKH = 12
VH = 2 * QKH
XH = 4
MLH = 4
HGH = 8
LEVELS = 7

W_MEM = 0
W_AB = 2 * (XH * 256) // P
W_XA = W_AB + 1
W_DN = W_XA + 4 * XH
W_OUT = W_DN + 6 * QKH
W_GATE = W_OUT + 2 * KT
W_ML = W_GATE + 1
W_HG = W_ML + 8 * MLH
W_OUT2 = W_HG + 4 * HGH
W_PE = W_OUT2 + KT
W_PG = W_PE + 2
W_END = W_PG + KT

_o = [0]


def _cols(n):
    _o[0] += n
    return _o[0] - n


C_NORM, C_MEMN = _cols(KT), _cols(KT)
C_XQ, C_XK = _cols(2), _cols(2)
C_DNOUT = _cols(1)
C_ALOG, C_DT = _cols(1), _cols(1)
C_DNCONV = _cols(QKH * 16)
C_NORM2 = _cols(KT)
C_IFB = _cols(1)
C_ML = _cols(MLH * 12)
C_HGL = _cols(2 * HGH)
C_HGN = _cols(HGH)
C_PEN, C_FIN = _cols(KT), _cols(KT)
NPAR = _o[0]


class Steps:

    def __init__(self, eng, sem, pad):
        self.eng, self.sem, self.pad = eng, sem, pad
        self.start, self.loop, self.k, self.last = 0, 0, 0, None

    def did(self, ins, sem=None, value=None):
        if sem is None:
            self.k += 1
            sem, value = self.sem, self.start + self.loop + self.k
        ins.then_inc(sem, 1)
        self.last = (sem, value)

    def wait(self):
        if self.last is not None:
            self.eng.wait_ge(*self.last)

    def settle(self):
        self.eng.sem_inc(self.pad, 1)

    def enter(self, i, per):
        self.start, self.k, self.per, self.last = self.start + self.k, 0, per, None
        self.loop = i * per
        if self.start > 0:
            self.last = (self.sem, self.start + self.loop)

    def leave(self, trips):
        assert self.k == self.per, ("steps in a trip", self.k)
        self.start, self.loop, self.k = self.start + trips * self.per, 0, 0


def tile_at(base, c, i=0, per=0):
    return (base + c) % 2, (base + c) // 2 + (per // 2) * i


def interleave(tiles, steps):
    parts = [("gemm", c, k) for c in range(tiles) for k in range(KT)]
    order, done = [], 0
    for n, part in enumerate(parts):
        order.append(part)
        if part[2] == KT - 1:
            order.append(("evict", part[1]))
        while done < len(steps) and (done + 1) * len(parts) <= (n + 1) * (len(steps) + 1):
            order.append(steps[done])
            done += 1
    return order + steps[done:]


DN_STEPS = ([("qk_norm",), ("natural",), ("transposed",)]
            + [(s, l) for l in range(1, LEVELS) for s in ("half", "whole")]
            + [(s, n) for n in range(NB) for s in ("rest", "update", "output")]
            + [("head_out",)])


ML_STEPS = [("ml_scores",), ("ml_sums",), ("ml_out",)]
HG_STEPS = ([("hg_prep",), ("hg_diagonal",)] + [("hg_level", l) for l in range(LEVELS)]
            + [("hg_state",), ("hg_mix",), ("hg_out",)])
ML_VECTOR_STEPS = 24
HG_VECTOR_STEPS = 26


def build(nc, weights, xT, memT, peT, params, consts, out):
    ctx = ExitStack()

    def sb(name, shape, dt=F32):
        return ctx.enter_context(nc.sbuf_tensor(name, shape, dt))

    def sem(name):
        return ctx.enter_context(nc.semaphore(name))

    with ctx:
        w_raw = sb("w_raw", [P, 2, KT, P])
        w_hi = sb("w_hi", [P, 2, KT, P], F32R)
        w_lo = sb("w_lo", [P, 2, KT, P], F32R)
        a_hi = sb("a_hi", [P, KT, T], F32R)
        a_lo = sb("a_lo", [P, KT, T], F32R)
        par = sb("par", [P, NPAR])
        con = sb("con", [P, 4 + 2 * LEVELS, P])
        ones, ident, incl, reset = (con[:, n, :] for n in range(4))
        low = con[:, 4:4 + LEVELS, :].bitcast(U32)
        lowT = con[:, 4 + LEVELS:4 + 2 * LEVELS, :].bitcast(U32)
        eps = sb("eps", [P, 1])
        nul = sb("nul", [P, 1])
        arena = sb("arena", [P, 21504])

        def at(start, n=T):
            assert start + n <= 21504
            return arena[:, start:start + n]

        def halves(start, n=T):
            return at(start, 2 * n).rearrange("p (a t) -> p a t", a=2)

        stage = at(0, 4 * T).rearrange("p (s t) -> p s t", s=4)
        sqr = halves(2048)
        root, rstd = at(3072), at(3584)
        BASE = 4096
        kv = at(BASE, 16 * M).rearrange("p (c m) -> p c m", c=16)
        vmem = at(BASE + 4096, 2048).rearrange("p (m c) -> p m c", m=2)
        src0 = at(BASE + 6144, 8192).rearrange("p (k t) -> p k t", k=KT)
        src_mem = src0[:, :, 0:M]
        xq = halves(BASE + 6144)
        xz = halves(BASE + 7168)
        xp = at(BASE + 8192, 1024).rearrange("p (b m) -> p b m", b=NB)
        xpT = halves(BASE + 9216)
        xy = halves(BASE + 10240)
        xsm = at(BASE + 11264, 3 * NB).rearrange("p (s b) -> p s b", s=3)
        xrt = halves(BASE + 11776)
        ab = at(18432, 5 * T).rearrange("p (s t) -> p s t", s=5)
        cols = at(20992).rearrange("p (b q h) -> p b q h", b=NB, q=4)
        o_ = BASE
        raw = at(o_, T + 3)
        o_ += 520
        cv = at(o_, 4 * T).rearrange("p (c t) -> p c t", c=4)
        o_ += 4 * T
        z_in, z_g = halves(o_), halves(o_ + 1024)
        o_ += 2048
        gcb = halves(o_)
        o_ += 1024
        qn, kn = at(o_), at(o_ + T)
        o_ += 1024

        def units(start):
            return at(start, 1024).rearrange("p (a n t) -> p a n t", a=2, n=NB)

        Nm, dT, NmT, X, XT, T1, kd, vn = (units(o_ + 1024 * k) for k in range(8))
        ke, qd = halves(o_ + 2 * 1024), halves(o_ + 3 * 1024)
        ort, yo = halves(o_), halves(o_ + 5 * 1024)
        o_ += 8 * 1024
        St, rr, uu = (at(o_ + 256 * k, 256).rearrange("p (a t) -> p a t", a=2) for k in range(3))
        o_ += 768
        cb = at(o_, 32).rearrange("p (b q a) -> p b q a", b=NB, q=4)
        cw = at(o_ + 32, 16)
        assert o_ + 48 <= 20992
        xt = at(BASE, 8192).rearrange("p (k t) -> p k t", k=KT)
        ys = at(BASE + 8192, 8192).rearrange("p (k t) -> p k t", k=KT)

        o_ = BASE
        m_raw = at(o_, T + 3)
        mc, mv, m_o, m_z, m_g, m_rows, m_h, m_y = (halves(o_ + 520 + 1024 * k) for k in range(8))
        o_ += 520 + 8192
        m_s = at(o_, NB * T).rearrange("p (n t) -> p n t", n=NB)
        m_vn = at(o_ + 2048, 1024).rearrange("p (a n t) -> p a n t", a=2, n=NB)
        m_den = at(o_ + 3072)
        m_conv = at(o_ + 3584, 12)
        m_gain = at(o_ + 3600, 2)
        m_cb = at(o_ + 3604, NB)
        mcols = at(20992, NB * MLH).rearrange("p (n h) -> p n h", n=NB)
        h_par = at(21024, 3 * HGH).rearrange("p (h c) -> p h c", c=3)
        h_tmp = at(21056, HGH)
        o_ = BASE
        (hg_in, hq_in, hf_in, hi_in, h_gate, h_q, h_k, h_b, h_eb, h_d, h_w0, h_w1, h_a, h_vn, h_kdt, h_kd, h_qe,
         h_s, h_rt, h_y) = (at(o_ + T * k) for k in range(20))
        h_hp = at(o_ + T * 20, 3)
        ets = ys
        pe_src = at(20480, 1024).rearrange("p (k t) -> p k t", k=2)

        gemm_ps = [ctx.enter_context(nc.psum_tensor(f"gemm_ps{i}", [P, T], F32)) for i in range(2)]
        bankA, bankB, bankC = (ctx.enter_context(nc.psum_tensor(f"bank{x}", [P, 2, T], F32)) for x in "ABC")

        def quad(bank):
            return bank[:, :, :].rearrange("p a (n t) -> p a n t", n=NB)

        y_dram = nc.dram_tensor("y_scratch", [2 * KT, P, T], F32)
        x2_dram = nc.dram_tensor("x2_scratch", [P, KT, T], F32)
        y2_dram = nc.dram_tensor("y2_scratch", [KT, P, T], F32)
        ml_dram = nc.dram_tensor("ml_scratch", [MLH, 2, T], F32)
        gc_dram = nc.dram_tensor("gc_scratch", [VH, T], F32)

        dve_step, act_step, pool_step, pad = sem("dve_step"), sem("act_step"), sem("pool_step"), sem("pad")
        const_loaded, filled = sem("const_loaded"), sem("filled")
        raw_loaded = [sem("raw_loaded0"), sem("raw_loaded1")]
        cut = [sem("cut0"), sem("cut1")]
        gemm_done = [sem("gemm_done0"), sem("gemm_done1")]
        evicted = [sem("evicted0"), sem("evicted1")]
        names = ("src_loaded src_used staged act_hi act_lo squared sq_summed sums root_ready rstd_ready "
                 "kv_sq kv_sum kv_root kv_norm vT_done v_done "
                 "ab_exp ab_x ab_ln ab_x2 rows_ready colsT cols_ready gc_stored "
                 "q_sq q_sum q_root q_norm s_done max_ready p_exp p_norm pT_done pT_sbuf o_done z_ready z_silu y_ready y_stored "
                 "conv silu dq_sq dq_sum dq_root dq_norm nat nat_v pair vn_sbuf diff expd n_ready nT nT_sbuf x_ready "
                 "t1 t1_sbuf dd lvl rk r_ready u u_sbuf o s_ready o_sq o_sum o_root dy_ready dy_stored gate gc_loaded "
                 "ys_loaded out_ready out_stored "
                 "g_x g_exp g_rowsT mcols_ready ml_stored h_lb h_lbexp x2_stored "
                 "m_conv m_silu m_gated m_gate ml_loaded mvT m_vn m_diff m_expd m_sc m_scd m_den m_num m_dencp m_hd m_sq "
                 "m_sum m_root m_yr m_yst "
                 "h_cut h_sig h_fb h_ln h_vT h_vns h_qk h_diag h_dr h_ex h_wr h_pr h_pred h_ebx h_kx h_kxe h_kdr h_kT "
                 "h_kds h_st h_sr h_o h_osq h_osum h_ort h_yr h_yst h_gs "
                 "e_done e_out sg_in sg_out").split()
        s = {n: sem(n) for n in names}
        act_hi, act_lo = s["act_hi"], s["act_lo"]
        block = ctx.enter_context(nc.Block())

        def gains(c, n=1):
            return par[:, c:c + n]

        def used_before(tile, slot):
            return (tile + 1 - slot) // 2

        FILLS = [W_MEM, W_AB, W_OUT, W_OUT + KT, W_GATE, W_OUT2, W_PE, W_PG]
        CUT_AT = [0, KT, 2 * KT, 3 * KT, 4 * KT, 5 * KT, 6 * KT, 6 * KT + 2]
        GAINED = {0: 0, 1: 1, 4: 2, 7: 3}

        @block.sync
        def _(sp):
            for w in range(2):
                sp.dma_start(w_raw[:, w, :, :], weights[w]).then_inc(raw_loaded[w], 16)
            with sp.Fori(0, (W_END + 1) // 2 - 1) as i:
                for w in range(2):
                    sp.wait_ge(cut[w], i + 1)
                    sp.dma_start(w_raw[:, w, :, :], weights[bass.ds(2 * i + 2 + w, 1)].rearrange(
                        "a p k c -> p (a k) c")).then_inc(raw_loaded[w], 16)
            for w in range(2):
                sp.wait_ge(raw_loaded[w], 16 * ((W_END + 1) // 2))

        @block.gpsimd
        def _(pool):
            def cut_tile(w, n, first=False):
                pool.wait_ge(raw_loaded[w], 16 * n + 16)
                if not first:
                    pool.wait_ge(gemm_done[w], n)
                pool.tensor_tensor(w_hi[:, w, :, :].rearrange("p k c -> p (k c)"),
                                   w_raw[:, w, :, :].rearrange("p k c -> p (k c)"),
                                   nul[:, 0:1].to_broadcast([P, KT * P]), ALU.add).then_inc(pool_step, 1)
                pool.wait_ge(pool_step, 2 * n + w + 1)
                pool.tensor_tensor(w_lo[:, w, :, :], w_raw[:, w, :, :], w_hi[:, w, :, :].bitcast(F32),
                                   ALU.subtract).then_inc(cut[w], 1)

            pool.wait_ge(filled, 2)
            for w in range(2):
                cut_tile(w, 0, True)
            with pool.Fori(0, (W_END + 1) // 2 - 1) as i:
                for w in range(2):
                    cut_tile(w, i + 1)

        @block.tensor
        def _(pe):
            def gemm(base, c, k, fill=None, i=0, per=0, width=T):
                slot, n = tile_at(base, c, i, per)
                if k == 0:
                    pe.wait_ge(cut[slot], n + 1)
                    if not (isinstance(n, int) and n == 0):
                        pe.wait_ge(evicted[slot], n)
                if fill is not None:
                    pe.wait_ge(act_lo, CUT_AT[fill] + k + 1)
                o = gemm_ps[slot][:, 0:width]
                hi, lo = w_hi[:, slot, k, :], w_lo[:, slot, k, :]
                pe.matmul(o, hi, a_hi[:, k, 0:width], start=(k == 0), stop=False)
                pe.matmul(o, hi, a_lo[:, k, 0:width], start=False, stop=False)
                last = pe.matmul(o, lo, a_hi[:, k, 0:width], start=False, stop=(k == KT - 1))
                if k == KT - 1:
                    last.then_inc(gemm_done[slot], 1)

            def square_sums(q, width=T):
                for k in range(KT):
                    pe.wait_ge(s["squared"], KT * q + k + 1)
                    pe.matmul(bankA[:, 0, 0:width], ones, sqr[:, k % 2, 0:width], start=(k == 0),
                              stop=(k == KT - 1)).then_inc(s["sq_summed"], 1)

            pe.wait_ge(const_loaded, 48)
            square_sums(0, M)
            for c in range(W_AB):
                for k in range(KT):
                    gemm(W_MEM, c, k, 0 if c == 0 else None, width=M)
            for h in range(XH):
                pe.wait_ge(s["kv_sq"], h + 1)
                for d in range(2):
                    last = pe.matmul(bankA[:, h // 2, h % 2 * M:h % 2 * M + M], ones,
                                     sqr[:, h % 2, d * M:d * M + M], start=(d == 0), stop=(d == 1))
                last.then_inc(s["kv_sum"], 1)
            pe.wait_ge(evicted[1], W_AB // 2)
            for c in range(8):
                bank = bankB if c < 4 else bankC
                for m in range(2):
                    last = pe.transpose(bank[:, m, c % 4 * P:c % 4 * P + P], kv[:, 8 + c, m * P:m * P + P],
                                        ident)
            last.then_inc(s["vT_done"], 1)

            pe.wait_ge(s["kv_root"], XH)
            square_sums(1)
            for k in range(KT):
                gemm(W_AB, 0, k, 1)
            pe.wait_ge(s["rows_ready"], 1)
            for n in range(NB):
                last = pe.transpose(bankB[:, 0, n * P:n * P + P], ab[:, 3, n * P:n * P + P], ident)
            last.then_inc(s["colsT"], 1)

            for h in range(XH):
                for step in XA_ORDER:
                    if step[0] == "gemm":
                        gemm(W_XA + 4 * h, step[1], step[2])
                    elif step[0] == "q_norm":
                        pe.wait_ge(s["q_sq"], h + 1)
                        for d in range(2):
                            last = pe.matmul(bankA[:, 0, :], ones, sqr[:, d, :], start=(d == 0), stop=(d == 1))
                        last.then_inc(s["q_sum"], 1)
                    elif step[0] == "scores":
                        pe.wait_ge(s["q_norm"], h + 1)
                        if h == 0:
                            pe.wait_ge(s["kv_norm"], XH)
                            pe.wait_ge(s["cols_ready"], 1)
                        else:
                            pe.wait_ge(s["y_ready"], 2 * h)
                        for n in range(NB):
                            o = bankB[:, n // 2, n % 2 * M:n % 2 * M + M]
                            for d in range(2):
                                last = pe.matmul(o, xq[:, d, n * P:n * P + P], kv[:, 2 * h + d, :],
                                                 start=(d == 0), stop=(d == 1))
                        last.then_inc(s["s_done"], 1)
                    elif step[0] == "weights":
                        pe.wait_ge(s["p_norm"], h + 1)
                        if h == 0:
                            pe.wait_ge(s["v_done"], 2)
                        for n in range(NB):
                            for m in range(2):
                                last = pe.transpose(bankC[:, m, n * P:n * P + P], xp[:, n, m * P:m * P + P], ident)
                        last.then_inc(s["pT_done"], 1)
                    elif step[0] == "values":
                        pe.wait_ge(s["pT_sbuf"], h + 1)
                        for d in range(2):
                            for m in range(2):
                                last = pe.matmul(bankB[:, d, :], vmem[:, m, (2 * h + d) * P:(2 * h + d) * P + P],
                                                 xpT[:, m, :], start=(m == 0), stop=(m == 1))
                        last.then_inc(s["o_done"], 1)

            def dn_mix(step, j):
                if step[0] == "qk_norm":
                    for a in range(2):
                        pe.wait_ge(s["dq_sq"], 2 * j + a + 1)
                        pe.matmul(bankA[:, a, :], ones, sqr[:, a, :], start=True, stop=True).then_inc(s["dq_sum"], 1)
                elif step[0] == "natural":
                    pe.wait_ge(s["dq_norm"], 2 * j + 2)
                    for n in range(NB):
                        last = pe.transpose(bankB[:, 0, n * P:n * P + P], kn[:, n * P:n * P + P], ident)
                    last.then_inc(s["nat"], 1)
                    for a in range(2):
                        for n in range(NB):
                            last = pe.transpose(bankC[:, a, n * P:n * P + P], cv[:, 2 + a, n * P:n * P + P], ident)
                    last.then_inc(s["nat_v"], 1)
                    for n in range(NB):
                        b = slice(n * P, n * P + P)
                        pe.matmul(bankA[:, 0, b], kn[:, b], kn[:, b], start=True, stop=True)
                        last = pe.matmul(bankA[:, 1, b], kn[:, b], qn[:, b], start=True, stop=True)
                    last.then_inc(s["pair"], 1)
                elif step[0] == "transposed":
                    pe.wait_ge(s["n_ready"], j + 1)
                    for a in range(2):
                        for n in range(NB):
                            last = pe.transpose(quad(bankB)[:, a, n, :], Nm[:, a, n, :], ident)
                    last.then_inc(s["nT"], 1)
                elif step[0] == "half":
                    pe.wait_ge(s["x_ready"], j + 1)
                    if step[1] > 1:
                        pe.wait_ge(s["lvl"], (LEVELS - 1) * j + step[1] - 1)
                    else:
                        pe.wait_ge(s["nT_sbuf"], j + 1)
                    for a in range(2):
                        for n in range(NB):
                            last = pe.matmul(quad(bankA)[:, a, n, :], NmT[:, a, n, :], X[:, a, n, :],
                                             start=True, stop=True)
                    last.then_inc(s["t1"], 1)
                elif step[0] == "whole":
                    pe.wait_ge(s["t1_sbuf"], (LEVELS - 1) * j + step[1])
                    for a in range(2):
                        for n in range(NB):
                            if step[1] < LEVELS - 1:
                                pe.matmul(quad(bankB)[:, a, n, :], XT[:, a, n, :], T1[:, a, n, :],
                                          start=True, stop=True)
                            last = pe.matmul(quad(bankC)[:, a, n, :], T1[:, a, n, :], XT[:, a, n, :],
                                             start=True, stop=True)
                    last.then_inc(s["dd"], 1)
                elif step[0] == "rest":
                    if step[1] > 0:
                        pe.wait_ge(s["s_ready"], 3 * j + step[1])
                        for a in range(2):
                            last = pe.matmul(bankA[:, 0, a * P:a * P + P], ke[:, a, step[1] * P:step[1] * P + P],
                                             St[:, a, :], start=True, stop=True)
                        last.then_inc(s["rk"], 1)
                elif step[0] == "update":
                    pe.wait_ge(s["r_ready"], NB * j + step[1] + 1)
                    for a in range(2):
                        last = pe.matmul(bankB[:, 0, a * P:a * P + P], XT[:, a, step[1], :], rr[:, a, :],
                                         start=True, stop=True)
                    last.then_inc(s["u"], 1)
                elif step[0] == "output":
                    n = step[1]
                    pe.wait_ge(s["u_sbuf"], NB * j + n + 1)
                    for a in range(2):
                        o = bankC[:, a, n * P:n * P + P]
                        if n > 0:
                            pe.matmul(o, St[:, a, :], qd[:, a, n * P:n * P + P], start=True, stop=False)
                        last = pe.matmul(o, uu[:, a, :], dT[:, a, n, :], start=(n == 0), stop=True)
                    if n < NB - 1:
                        for a in range(2):
                            last = pe.matmul(bankA[:, 1, a * P:a * P + P], kd[:, a, n, :], uu[:, a, :],
                                             start=True, stop=True)
                    last.then_inc(s["o"], 1)
                elif step[0] == "head_out":
                    for a in range(2):
                        pe.wait_ge(s["o_sq"], 2 * j + a + 1)
                        pe.matmul(bankB[:, a, :], ones, sqr[:, a, :], start=True, stop=True).then_inc(s["o_sum"], 1)

            def dn_trip(g, j, tiles=True, mix=True):
                for step in interleave(6 if tiles else 0, DN_STEPS if mix else []):
                    if step[0] == "gemm":
                        gemm(W_DN, step[1], step[2], None, g, 6)
                    elif step[0] != "evict":
                        dn_mix(step, j)

            dn_trip(0, None, mix=False)
            with pe.Fori(0, QKH - 1) as j:
                dn_trip(j + 1, j)
            dn_trip(None, QKH - 1, tiles=False)

            for half in range(2):
                for k in range(KT):
                    gemm(W_OUT + KT * half, 0, k, 2 + half)
                for k in range(KT):
                    gemm(W_OUT + KT * half, 1, k)
                with pe.Fori(0, KT // 2 - 1) as i:
                    for c in range(2):
                        for k in range(KT):
                            gemm(W_OUT + KT * half + 2, c, k, None, i, 2)

            pe.wait_ge(s["o_root"], 2 * QKH)
            square_sums(2)
            for k in range(KT):
                gemm(W_GATE, 0, k, 4)
            pe.wait_ge(s["g_x"], 4)
            for n in range(NB):
                last = pe.transpose(bankB[:, 0, n * MLH:n * MLH + MLH], ab[0:MLH, 1, n * P:n * P + P],
                                    ident[0:MLH, 0:MLH])
            last.then_inc(s["g_rowsT"], 1)

            def ml_mix(step, j):
                if step[0] == "ml_scores":
                    for a in range(2):
                        slot, n = tile_at(W_ML, 6 + a, j, 8)
                        pe.wait_ge(evicted[slot], n + 1)
                    for a in range(2):
                        for n in range(NB):
                            last = pe.transpose(bankB[:, a, n * P:n * P + P], mv[:, a, n * P:n * P + P], ident)
                    last.then_inc(s["mvT"], 1)
                    pe.wait_ge(s["m_silu"], 2 * j + 2)
                    for n in range(NB):
                        o = (bankA, bankC)[n // 2][:, n % 2, n * P:T]
                        last = pe.matmul(o, mc[:, 1, n * P:n * P + P], mc[:, 0, n * P:T], start=True, stop=True)
                    last.then_inc(s["m_sc"], 1)
                elif step[0] == "ml_sums":
                    pe.wait_ge(s["m_scd"], j + 1)
                    pe.wait_ge(s["m_vn"], j + 1)
                    for n in range(NB):
                        last = pe.matmul(bankB[:, 0, n * P:T], ones, m_s[:, n, n * P:T], start=(n == 0),
                                         stop=(n == NB - 1))
                    last.then_inc(s["m_den"], 1)
                    for a in range(2):
                        for n in range(NB):
                            last = pe.matmul(bankC[:, a, n * P:T], m_vn[:, a, n, :], m_s[:, n, n * P:T],
                                             start=(n == 0), stop=(n == NB - 1))
                    last.then_inc(s["m_num"], 1)
                elif step[0] == "ml_out":
                    pe.wait_ge(s["m_sq"], j + 1)
                    for a in range(2):
                        last = pe.matmul(bankA[:, 0, :], ones, sqr[:, a, :], start=(a == 0), stop=(a == 1))
                    last.then_inc(s["m_sum"], 1)

            def ml_trip(g, j, tiles=True, mix=True):
                for step in interleave(8 if tiles else 0, ML_STEPS if mix else []):
                    if step[0] == "gemm":
                        gemm(W_ML, step[1], step[2], None, g, 8)
                    elif step[0] != "evict":
                        ml_mix(step, j)

            ml_trip(0, None, mix=False)
            with pe.Fori(0, MLH - 1) as j:
                ml_trip(j + 1, j)
            ml_trip(None, MLH - 1, tiles=False)

            def hg_mix(step, j):
                if step[0] == "hg_prep":
                    pe.wait_ge(s["h_cut"], j + 1)
                    for n in range(NB):
                        last = pe.transpose(bankB[:, 0, n * P:n * P + P], hi_in[:, n * P:n * P + P], ident)
                    last.then_inc(s["h_vT"], 1)
                elif step[0] == "hg_diagonal":
                    pe.wait_ge(s["h_qk"], j + 1)
                    pe.matmul(bankB[:, 1, :], ones, h_w1, start=True, stop=True).then_inc(s["h_diag"], 1)
                elif step[0] == "hg_level":
                    l = step[1]
                    pe.wait_ge(s["h_wr"], LEVELS * j + l + 1)
                    w = (h_w0, h_w1)[l % 2]
                    for n in range(NB):
                        b = slice(n * P, n * P + P)
                        last = pe.matmul(bankA[:, l % 2, b], w[:, b], w[:, b], start=True, stop=True)
                    last.then_inc(s["h_pr"], 1)
                elif step[0] == "hg_state":
                    pe.wait_ge(s["h_kdr"], j + 1)
                    for n in range(NB):
                        last = pe.transpose(bankB[:, 0, n * P:n * P + P], h_kdt[:, n * P:n * P + P], ident)
                    last.then_inc(s["h_kT"], 1)
                elif step[0] == "hg_mix":
                    pe.wait_ge(s["h_kds"], j + 1)
                    for n in range(NB - 1):
                        b = slice(n * P, n * P + P)
                        last = pe.matmul(bankB[:, 1, b], h_kd[:, b], h_vn[:, b], start=True, stop=True)
                    last.then_inc(s["h_st"], 1)
                elif step[0] == "hg_out":
                    pe.wait_ge(s["h_sr"], j + 1)
                    pe.wait_ge(s["h_pred"], LEVELS * j + LEVELS)
                    for n in range(NB):
                        b = slice(n * P, n * P + P)
                        last = pe.matmul(bankC[:, 0, b], h_vn[:, b], h_a[:, b], start=True, stop=(n == 0))
                        if n > 0:
                            last = pe.matmul(bankC[:, 0, b], h_s[:, (n - 1) * P:n * P], h_qe[:, b],
                                             start=False, stop=True)
                    last.then_inc(s["h_o"], 1)
                    pe.wait_ge(s["h_osq"], j + 1)
                    pe.matmul(bankC[:, 1, :], ones, sqr[:, 0, :], start=True, stop=True).then_inc(s["h_osum"], 1)

            def hg_trip(g, j, tiles=True, mix=True):
                for step in interleave(4 if tiles else 0, HG_STEPS if mix else []):
                    if step[0] == "gemm":
                        gemm(W_HG, step[1], step[2], None, g, 4)
                    elif step[0] != "evict":
                        hg_mix(step, j)

            hg_trip(0, None, mix=False)
            with pe.Fori(0, HGH - 1) as j:
                hg_trip(j + 1, j)
            hg_trip(None, HGH - 1, tiles=False)

            for c in range(2):
                for k in range(KT):
                    gemm(W_OUT2, c, k, 5 if c == 0 else None)
            with pe.Fori(0, KT // 2 - 1) as i:
                for c in range(2):
                    for k in range(KT):
                        gemm(W_OUT2 + 2, c, k, None, i, 2)

            for t in range(2):
                slot, n = tile_at(W_PE, t)
                pe.wait_ge(cut[slot], n + 1)
                for c in range(8):
                    e = 8 * t + c
                    if t == 0 and c < 2:
                        pe.wait_ge(act_lo, CUT_AT[6] + 2)
                        pe.wait_ge(evicted[c], used_before(W_PE, c))
                    else:
                        pe.wait_ge(s["e_out"], e - 1)
                    o = gemm_ps[e % 2][:, :]
                    for k in range(2):
                        hi, lo = w_hi[:, slot, 2 * c + k, :], w_lo[:, slot, 2 * c + k, :]
                        pe.matmul(o, hi, a_hi[:, k, :], start=(k == 0), stop=False)
                        pe.matmul(o, hi, a_lo[:, k, :], start=False, stop=False)
                        last = pe.matmul(o, lo, a_hi[:, k, :], start=False, stop=(k == 1))
                    if c < 7:
                        last.then_inc(s["e_done"], 1)
                    else:
                        last.then_inc(gemm_done[slot], 1)

            pe.wait_ge(s["h_yr"], HGH)
            square_sums(3)
            pe.wait_ge(s["e_out"], 16)
            for c in range(2):
                for k in range(KT):
                    gemm(W_PG, c, k, 7 if c == 0 else None)
            with pe.Fori(0, KT // 2 - 1) as i:
                for c in range(2):
                    for k in range(KT):
                        gemm(W_PG + 2, c, k, None, i, 2)
            square_sums(4)

        @block.vector
        def _(v):
            d = Steps(v, dve_step, pad)

            def op(make, *args, sem=None, value=None):
                d.wait()
                d.did(make(*args), sem, value)

            def copy_after(make, *args, sem=None, value=None):
                d.wait()
                d.settle()
                d.did(make(*args), sem, value)

            def scaled(dst, base, c, i=0, per=0, width=T, rows=P):
                slot, n = tile_at(base, c, i, per)
                v.wait_ge(gemm_done[slot], n + 1)
                op(v.tensor_tensor, dst, gemm_ps[slot][0:rows, 0:width], rstd[0:rows, 0:width], ALU.mult,
                   sem=evicted[slot], value=n + 1)

            def reciprocal_root(q, width=T):
                v.wait_ge(s["root_ready"], q + 1)
                op(v.reciprocal, rstd[:, 0:width], root[:, 0:width], sem=s["rstd_ready"], value=q + 1)

            def fill(f, src, gain, width=T, blocks=KT):
                for w in range(2):
                    if used_before(FILLS[f], w):
                        v.wait_ge(gemm_done[w], used_before(FILLS[f], w))

                def product(k):
                    op(v.tensor_scalar, stage[:, k % 4, 0:width], src[:, k, :], gains(gain + k), None, ALU.mult,
                       sem=s["staged"], value=KT * GAINED[f] + k + 1)

                for k in range(blocks):
                    if gain is not None:
                        for kk in ((0, 1, 2) if k == 0 else (k + 2,)):
                            if kk < KT:
                                product(kk)
                    v.wait_ge(act_hi, CUT_AT[f] + k + 1)
                    op(v.tensor_tensor, a_lo[:, k, 0:width],
                       stage[:, k % 4, 0:width] if gain is not None else src[:, k, :],
                       a_hi[:, k, 0:width].bitcast(F32), ALU.subtract, sem=act_lo, value=CUT_AT[f] + k + 1)

            op(v.memset, eps[:, :], EPS, sem=filled, value=1)
            op(v.memset, nul[:, :], 0.0, sem=filled, value=2)
            op(v.memset, ab[:, 3, :], 0.0)
            v.wait_ge(const_loaded, 48)

            v.wait_ge(s["src_loaded"], 16)
            fill(0, src_mem, C_MEMN, M)
            reciprocal_root(0, M)
            for c in range(W_AB):
                scaled(kv[:, c, :], W_MEM, c, width=M)
            for h in range(XH):
                v.wait_ge(s["kv_root"], h + 1)
                op(v.reciprocal, stage[:, h, 0:M], stage[:, h, 0:M])
                for e in range(2):
                    op(v.scalar_tensor_tensor, kv[:, 2 * h + e, :], kv[:, 2 * h + e, :], gains(C_XK + e),
                       stage[:, h, 0:M], ALU.mult, ALU.mult, sem=s["kv_norm"] if e else None, value=h + 1)

            v.wait_ge(s["src_loaded"], 32)
            fill(1, src0, C_NORM)
            reciprocal_root(1)
            scaled(ab[0:64, 0, :], W_AB, 0, rows=64)
            op(v.tensor_scalar, ab[0:64, 0, :], ab[0:64, 0, :], par[0:64, C_DT:C_DT + 1], None, ALU.add,
               sem=s["ab_x"], value=1)
            op(v.scalar_tensor_tensor, ab[0:VH, 1, :], ab[0:VH, 0, :], -1.0, ab[0:VH, 0, :], ALU.mult, ALU.max,
               sem=s["ab_x"], value=2)
            v.wait_ge(s["ab_exp"], 1)
            op(v.tensor_scalar, ab[0:VH, 1, :], ab[0:VH, 1, :], 1.0, None, ALU.add, sem=s["ab_x"], value=3)
            v.wait_ge(s["ab_exp"], 4)
            op(v.scalar_tensor_tensor, ab[0:VH, 0, :], ab[0:VH, 0, :], 0.0, ab[0:VH, 1, :], ALU.max, ALU.add)
            op(v.tensor_scalar, ab[0:VH, 0, :], ab[0:VH, 0, :], ab[0:VH, 4, 0:1], -1.0, ALU.mult, ALU.mult)
            for n in range(NB):
                b = slice(n * P, n * P + P)
                op(v.tensor_tensor_scan, ab[0:VH, 3, b], ones[0:VH, :], ab[0:VH, 0, b], 0.0, ALU.mult, ALU.add)
            gc_rows = ab[0:VH, 3, :].rearrange("p (n t) -> p n t", n=NB)
            op(v.tensor_tensor, ab[0:VH, 1, :].rearrange("p (n t) -> p n t", n=NB),
               gc_rows[:, :, P - 1:P].to_broadcast([VH, NB, P]), gc_rows, ALU.subtract, sem=s["ab_x"], value=4)
            op(v.tensor_scalar, ab[32:32 + VH, 3, :], ab[32:32 + VH, 2, :], -1.0, None, ALU.mult)
            op(v.tensor_copy, ab[96:96 + VH, 3, :], ab[32:32 + VH, 2, :])
            v.wait_ge(s["ab_exp"], 5)
            op(v.tensor_copy, ab[64:64 + VH, 3, :], ab[0:VH, 1, :], sem=s["rows_ready"], value=1)
            v.wait_ge(s["colsT"], 1)
            op(v.tensor_copy, at(20992), bankB[:, 0, :], sem=s["cols_ready"], value=1)

            for h in range(XH):
                for step in XA_ORDER:
                    if step[0] == "evict":
                        c = step[1]
                        if c >= 2 and h > 0:
                            v.wait_ge(s["y_ready"], 2 * h)
                        scaled((xq, xz)[c // 2][:, c % 2, :], W_XA + 4 * h, c)
                    elif step[0] == "q_norm":
                        v.wait_ge(s["q_root"], h + 1)
                        op(v.reciprocal, xrt[:, 0, :], xrt[:, 0, :])
                        for e in range(2):
                            op(v.scalar_tensor_tensor, xq[:, e, :], xq[:, e, :], gains(C_XQ + e), xrt[:, 0, :],
                               ALU.mult, ALU.mult, sem=s["q_norm"] if e else None, value=h + 1)
                    elif step[0] == "scores":
                        v.wait_ge(s["s_done"], h + 1)
                        op(v.tensor_reduce, xsm[:, 0, :], bankB[:, :, :].rearrange("p a (b m) -> p (a b) m", m=M),
                           AX.X, ALU.max)
                        op(v.tensor_scalar, xsm[:, 1, :], xsm[:, 0, :], -1.0 / 16, None, ALU.mult,
                           sem=s["max_ready"], value=h + 1)
                        v.wait_ge(s["p_exp"], NB * (h + 1))
                        op(v.reciprocal, xsm[:, 2, :], xsm[:, 2, :])
                        for n in range(NB):
                            op(v.tensor_scalar, xp[:, n, :], xp[:, n, :], xsm[:, 2, n:n + 1], None, ALU.mult,
                               sem=s["p_norm"] if n == NB - 1 else None, value=h + 1)
                    elif step[0] == "values":
                        v.wait_ge(s["o_done"], h + 1)
                        v.wait_ge(s["z_silu"], 2 * h + 2)
                        if h > 0:
                            v.wait_ge(s["y_stored"], 16 * h)
                        for e in range(2):
                            op(v.tensor_tensor, xy[:, e, :], bankB[:, e, :], xz[:, e, :], ALU.mult,
                               sem=s["y_ready"], value=2 * h + e + 1)

            def dn_evict(c, g):
                if c < 2:
                    if not (isinstance(g, int) and g == 0):
                        v.wait_ge(s["gate"], 2 * g)
                    scaled(z_in[:, c, :], W_DN, c, g, 6)
                    return
                if c == 2:
                    v.wait_ge(evicted[1], 1)
                    if not isinstance(g, int):
                        d.wait()
                        d.settle()
                    v.tensor_copy(cw, par[:, bass.ds(C_DNCONV + 16 * g, 16)] if not isinstance(g, int)
                                  else par[:, C_DNCONV + 16 * g:C_DNCONV + 16 * g + 16]).then_inc(dve_step, 1)
                    d.k += 1
                    d.last = (dve_step, d.start + d.loop + d.k)
                scaled(raw[:, 3:T + 3], W_DN, c, g, 6)
                o = cv[:, c - 2, :]
                tap = 4 * (c - 2)
                op(v.tensor_scalar, o, raw[:, 0:T], cw[:, tap:tap + 1], None, ALU.mult)
                for t in range(1, 4):
                    op(v.scalar_tensor_tensor, o, raw[:, t:t + T], cw[:, tap + t:tap + t + 1], o, ALU.mult, ALU.add,
                       sem=s["conv"] if t == 3 else None, value=4 * g + c - 1)

            def dn_mix(step, j):
                if step[0] == "qk_norm":
                    d.wait()
                    d.settle()
                    d.did(v.tensor_copy(cb, cols[:, :, :, bass.ds(2 * j, 2)] if not isinstance(j, int)
                                        else cols[:, :, :, 2 * j:2 * j + 2]))
                    for a, (dst, scale) in enumerate(((qn, P ** -0.5), (kn, 1.0))):
                        v.wait_ge(s["dq_root"], 2 * j + a + 1)
                        op(v.reciprocal, T1[:, a, 0:NB, :].rearrange("p n t -> p (n t)"),
                           T1[:, a, 0:NB, :].rearrange("p n t -> p (n t)"))
                        op(v.scalar_tensor_tensor, dst, cv[:, a, :], scale,
                           T1[:, a, 0:NB, :].rearrange("p n t -> p (n t)"), ALU.mult, ALU.mult,
                           sem=s["dq_norm"], value=2 * j + a + 1)
                elif step[0] == "natural":
                    v.wait_ge(s["gc_loaded"], 16 * j + 16)
                    for a in range(2):
                        for n in range(NB):
                            g_row = gcb[:, a, n * P:n * P + P]
                            op(v.tensor_scalar, dT[:, a, n, :], g_row, cb[:, n, 0, a:a + 1], 0.0,
                               ALU.subtract, ALU.min)
                            op(v.tensor_scalar, Nm[:, a, n, :], g_row, cb[:, n, 0, a:a + 1], 0.0,
                               ALU.subtract, ALU.max,
                               sem=s["diff"] if (a, n) == (1, NB - 1) else None, value=j + 1)
                    v.wait_ge(s["nat"], j + 1)
                    for a in range(2):
                        for n in range(NB):
                            op(v.tensor_scalar, kd[:, a, n, :], bankB[:, 0, n * P:n * P + P],
                               cb[:, n, 2, a:a + 1], None, ALU.mult)
                    v.wait_ge(s["pair"], j + 1)
                    v.wait_ge(s["expd"], 3 * j + 2)
                    for a in range(2):
                        for n in range(NB):
                            op(v.scalar_tensor_tensor, Nm[:, a, n, :], bankA[:, 0, n * P:n * P + P],
                               cb[:, n, 1, a:a + 1], Nm[:, a, n, :], ALU.mult, ALU.mult,
                               sem=s["n_ready"] if (a, n) == (1, NB - 1) else None, value=j + 1)
                    for a in range(2):
                        op(v.tensor_tensor, dT[:, a, :, :], dT[:, a, :, :], quad(bankA)[:, 1, :, :], ALU.mult)
                    op(v.tensor_tensor, dT[:, :, :, :].rearrange("p a n t -> p (a n) t"),
                       dT[:, :, :, :].rearrange("p a n t -> p (a n) t"),
                       incl[:, None, :].to_broadcast([P, 8, P]), ALU.mult)
                elif step[0] == "transposed":
                    flat = "p a n t -> p (a n) t"
                    for dst in (X, XT):
                        op(v.tensor_copy, dst[:, :, :, :].rearrange(flat), ident[:, None, :].to_broadcast([P, 8, P]))
                    copy_after(v.copy_predicated, X[:, :, :, :].rearrange(flat),
                               low[:, 0:1, :].to_broadcast([P, 8, P]), Nm[:, :, :, :].rearrange(flat))
                    v.wait_ge(s["nT_sbuf"], j + 1)
                    copy_after(v.copy_predicated, XT[:, :, :, :].rearrange(flat),
                               lowT[:, 0:1, :].to_broadcast([P, 8, P]), quad(bankB).rearrange(flat),
                               sem=s["x_ready"], value=j + 1)
                elif step[0] == "whole":
                    flat = "p a n t -> p (a n) t"
                    v.wait_ge(s["dd"], (LEVELS - 1) * j + step[1])
                    if step[1] < LEVELS - 1:
                        copy_after(v.copy_predicated, X[:, :, :, :].rearrange(flat),
                                   low[:, step[1]:step[1] + 1, :].to_broadcast([P, 8, P]), quad(bankB).rearrange(flat))
                    copy_after(v.copy_predicated, XT[:, :, :, :].rearrange(flat),
                               lowT[:, step[1]:step[1] + 1, :].to_broadcast([P, 8, P]), quad(bankC).rearrange(flat),
                               sem=s["lvl"], value=(LEVELS - 1) * j + step[1])
                elif step[0] == "rest":
                    n = step[1]
                    if n == 0:
                        v.wait_ge(s["expd"], 3 * j + 3)
                        for a in range(2):
                            op(v.tensor_tensor, ke[:, a, :], kn, gcb[:, a, :], ALU.mult)
                            op(v.tensor_tensor, qd[:, a, :], qn, gcb[:, a, :], ALU.mult)
                        v.wait_ge(s["vn_sbuf"], 2 * j + 2)
                        for a in range(2):
                            op(v.tensor_scalar, rr[:, a, :], vn[:, a, 0, :], cb[:, 0, 3, a:a + 1], None, ALU.mult,
                               sem=s["r_ready"] if a else None, value=NB * j + 1)
                    else:
                        v.wait_ge(s["rk"], 3 * j + n)
                        op(v.tensor_tensor, rr[:, :, :], vn[:, :, n, :],
                           bankA[:, 0, 0:2 * P].rearrange("p (a t) -> p a t", a=2), ALU.subtract)
                        for a in range(2):
                            op(v.tensor_scalar, rr[:, a, :], rr[:, a, :], cb[:, n, 3, a:a + 1], None, ALU.mult,
                               sem=s["r_ready"] if a else None, value=NB * j + n + 1)
                elif step[0] == "output":
                    n = step[1]
                    if n < NB - 1:
                        v.wait_ge(s["o"], NB * j + n + 1)
                        for a in range(2):
                            dS = bankA[:, 1, a * P:a * P + P]
                            mark = dict(sem=s["s_ready"] if a else None, value=3 * j + n + 1)
                            if n == 0:
                                op(v.tensor_copy, St[:, a, :], dS, **mark)
                            else:
                                op(v.scalar_tensor_tensor, St[:, a, :], St[:, a, :],
                                   gcb[:, a, n * P + P - 1:n * P + P], dS, ALU.mult, ALU.add, **mark)
                elif step[0] == "head_out":
                    v.wait_ge(s["gate"], 2 * j + 2)
                    for a in range(2):
                        v.wait_ge(s["o_root"], 2 * j + a + 1)
                        op(v.reciprocal, ort[:, a, :], ort[:, a, :])
                        op(v.scalar_tensor_tensor, yo[:, a, :], bankC[:, a, :], gains(C_DNOUT), ort[:, a, :],
                           ALU.mult, ALU.mult)
                        op(v.tensor_tensor, yo[:, a, :], yo[:, a, :], z_g[:, a, :], ALU.mult,
                           sem=s["dy_ready"], value=2 * j + a + 1)

            def dn_trip(g, j, tiles=True, mix=True):
                for step in interleave(6 if tiles else 0, DN_STEPS if mix else []):
                    if step[0] == "evict":
                        dn_evict(step[1], g)
                    elif step[0] != "gemm":
                        dn_mix(step, j)

            op(v.memset, raw[:, 0:3], 0.0)
            dn_trip(0, None, mix=False)
            with v.Fori(0, QKH - 1) as j:
                d.enter(j, DN_VECTOR_STEPS)
                dn_trip(j + 1, j)
            d.leave(QKH - 1)
            dn_trip(None, QKH - 1, tiles=False)

            def add_tile(dst, base, c, i=0, per=0):
                slot, n = tile_at(base, c, i, per)
                v.wait_ge(gemm_done[slot], n + 1)
                op(v.tensor_tensor, dst, gemm_ps[slot][:, :], dst, ALU.add, sem=evicted[slot], value=n + 1)

            for half in range(2):
                v.wait_ge(s["ys_loaded"], 16 * (half + 1))
                fill(2 + half, ys, None)
                if half == 0:
                    v.wait_ge(s["src_loaded"], 48)
                for c in range(2):
                    add_tile(xt[:, c, :], W_OUT + KT * half, c)
                with v.Fori(0, KT // 2 - 1) as i:
                    d.enter(i, 0)
                    for c in range(2):
                        add_tile(xt[:, bass.ds(2 * i + 2 + c, 1), :].rearrange("p k t -> p (k t)"),
                                 W_OUT + KT * half + 2, c, i, 2)
                d.leave(KT // 2 - 1)

            fill(4, xt, C_NORM2)
            reciprocal_root(2)
            op(v.tensor_tensor, h_tmp, par[:, C_HGL + HGH:C_HGL + 2 * HGH], par[:, C_HGL:C_HGL + HGH], ALU.subtract,
               sem=s["h_lb"], value=1)
            v.wait_ge(s["h_lbexp"], 1)
            op(v.tensor_scalar, h_tmp, h_tmp, 1.0, None, ALU.add)
            op(v.reciprocal, h_par[:, :, 0], h_tmp)
            op(v.tensor_scalar, h_par[:, :, 1], h_par[:, :, 0], -1.0, 1.0, ALU.mult, ALU.add)
            op(v.tensor_copy, h_par[:, :, 2], par[:, C_HGN:C_HGN + HGH])
            scaled(ab[0:64, 0, :], W_GATE, 0, rows=64)
            op(v.tensor_scalar, ab[0:64, 0, :], ab[0:64, 0, :], par[0:64, C_IFB:C_IFB + 1], None, ALU.add)
            f_ = ab[32:32 + MLH, 0, :]
            f1 = ab[32:32 + MLH, 1, :]
            op(v.scalar_tensor_tensor, f1, f_, -1.0, f_, ALU.mult, ALU.max, sem=s["g_x"], value=1)
            v.wait_ge(s["g_exp"], 1)
            op(v.tensor_scalar, f1, f1, 1.0, None, ALU.add, sem=s["g_x"], value=2)
            v.wait_ge(s["g_exp"], 2)
            op(v.scalar_tensor_tensor, f1, f_, 0.0, f1, ALU.min, ALU.subtract)
            op(v.tensor_copy, ab[0:MLH, 2, :], f1)
            for n in range(NB):
                b = slice(n * P, n * P + P)
                op(v.tensor_tensor_scan, ab[0:MLH, 3, b], ones[0:MLH, :], ab[0:MLH, 2, b],
                   0.0 if n == 0 else ab[0:MLH, 3, n * P - 1:n * P], ALU.mult, ALU.add)
            op(v.tensor_tensor, ab[0:MLH, 1, :], ab[0:MLH, 0, :], ab[0:MLH, 3, :], ALU.subtract)
            for n in range(NB):
                b = slice(n * P, n * P + P)
                op(v.tensor_tensor_scan, ab[0:MLH, 4, b], ones[0:MLH, :], ab[0:MLH, 1, b],
                   0.0 if n == 0 else ab[0:MLH, 4, n * P - 1:n * P], ALU.mult, ALU.max)
            op(v.tensor_tensor, ab[0:MLH, 2, :], ab[0:MLH, 3, :], ab[0:MLH, 4, :], ALU.add, sem=s["g_x"], value=3)
            op(v.tensor_scalar, ab[0:MLH, 3, :], ab[0:MLH, 4, :], -1.0, None, ALU.mult, sem=s["g_x"], value=4)
            v.wait_ge(s["g_rowsT"], 1)
            op(v.tensor_copy, at(20992, NB * MLH), bankB[:, 0, 0:NB * MLH], sem=s["mcols_ready"], value=1)

            v.wait_ge(s["x2_stored"], 16)
            v.wait_ge(s["squared"], 3 * KT)
            op(v.memset, m_raw[:, 0:3], 0.0)

            def head_copy(dst, src, at0, i, n):
                d.wait()
                d.settle()
                d.did(v.tensor_copy(dst, src[:, at0 + n * i:at0 + n * i + n] if isinstance(i, int)
                                    else src[:, bass.ds(at0 + n * i, n)]))

            def ml_evict(c, g):
                if c < 4:
                    if not (isinstance(g, int) and g == 0):
                        v.wait_ge(s["m_gated"], g)
                    scaled((m_o, m_z)[c // 2][:, c % 2, :], W_ML, c, g, 8)
                    return
                if c == 4:
                    head_copy(m_conv, par, C_ML, g, 12)
                if c >= 6:
                    scaled(mv[:, c - 6, :], W_ML, c, g, 8)
                    return
                scaled(m_raw[:, 3:T + 3], W_ML, c, g, 8)
                o, tap = mc[:, c - 4, :], 4 * (c - 4)
                op(v.tensor_scalar, o, m_raw[:, 0:T], m_conv[:, tap:tap + 1], m_conv[:, 8 + c - 4:9 + c - 4],
                   ALU.mult, ALU.add)
                for t in range(1, 4):
                    op(v.scalar_tensor_tensor, o, m_raw[:, t:t + T], m_conv[:, tap + t:tap + t + 1], o,
                       ALU.mult, ALU.add, sem=s["m_conv"] if t == 3 else None, value=2 * g + c - 3)

            def ml_mix(step, j):
                if step[0] == "ml_scores":
                    d.wait()
                    d.settle()
                    d.did(v.tensor_copy(m_cb, mcols[:, :, j] if isinstance(j, int)
                                        else mcols[:, :, bass.ds(j, 1)].rearrange("p n h -> p (n h)")))
                    d.wait()
                    d.settle()
                    d.did(v.tensor_copy(m_gain, par[:, C_ML + 12 * j + 10:C_ML + 12 * j + 12] if isinstance(j, int)
                                        else par[:, bass.ds(C_ML + 10 + 12 * j, 2)]))
                    v.wait_ge(s["ml_loaded"], 16 * j + 16)
                    for n in range(NB):
                        op(v.tensor_scalar, m_s[:, n, n * P:T], m_rows[:, 0, n * P:T], m_cb[:, n:n + 1], 0.0,
                           ALU.add, ALU.min, sem=s["m_diff"], value=NB * j + n + 1)
                    v.wait_ge(s["m_sc"], j + 1)
                    for n in range(NB):
                        v.wait_ge(s["m_expd"], NB * j + n + 1)
                        op(v.scalar_tensor_tensor, m_s[:, n, n * P:T], (bankA, bankC)[n // 2][:, n % 2, n * P:T],
                           P ** -0.5, m_s[:, n, n * P:T], ALU.mult, ALU.mult)
                        b = slice(n * P, n * P + P)
                        op(v.tensor_tensor, m_s[:, n, b], m_s[:, n, b], incl, ALU.mult,
                           sem=s["m_scd"] if n == NB - 1 else None, value=j + 1)
                elif step[0] == "ml_sums":
                    v.wait_ge(s["m_dencp"], j + 1)
                    op(v.scalar_tensor_tensor, m_den, m_den, -1.0, m_den, ALU.mult, ALU.max)
                    op(v.tensor_tensor, m_den, m_den, m_rows[:, 1, :], ALU.max)
                    op(v.reciprocal, m_den, m_den)
                    v.wait_ge(s["m_num"], j + 1)
                    for a in range(2):
                        op(v.tensor_tensor, m_h[:, a, :], bankC[:, a, :], m_den, ALU.mult,
                           sem=s["m_hd"] if a else None, value=j + 1)
                elif step[0] == "ml_out":
                    v.wait_ge(s["m_root"], j + 1)
                    op(v.reciprocal, m_den, m_den)
                    v.wait_ge(s["m_gated"], j + 1)
                    for a in range(2):
                        op(v.scalar_tensor_tensor, m_h[:, a, :], m_h[:, a, :], m_gain[:, a:a + 1], m_den,
                           ALU.mult, ALU.mult)
                        op(v.tensor_tensor, m_y[:, a, :], m_h[:, a, :], m_g[:, a, :], ALU.mult,
                           sem=s["m_yr"] if a else None, value=j + 1)

            def ml_trip(g, j, tiles=True, mix=True):
                for step in interleave(8 if tiles else 0, ML_STEPS if mix else []):
                    if step[0] == "evict":
                        ml_evict(step[1], g)
                    elif step[0] != "gemm":
                        ml_mix(step, j)
                if tiles:
                    v.wait_ge(s["m_gate"], g + 1)
                    op(v.tensor_tensor, m_g[:, :, :], m_o[:, :, :], m_z[:, :, :], ALU.mult,
                       sem=s["m_gated"], value=g + 1)
                d.wait()

            ml_trip(0, None, mix=False)
            with v.Fori(0, MLH - 1) as j:
                d.enter(j, ML_VECTOR_STEPS)
                ml_trip(j + 1, j)
            d.leave(MLH - 1)
            ml_trip(None, MLH - 1, tiles=False)

            v.wait_ge(s["m_yst"], 16 * MLH)

            def hg_evict(c, g):
                first = isinstance(g, int) and g == 0
                if c == 0 and not first:
                    v.wait_ge(s["h_gs"], g)
                if c == 3 and not first:
                    v.wait_ge(s["h_vT"], g)
                scaled((hg_in, hq_in, hf_in, hi_in)[c], W_HG, c, g, 4)
                if c == 3:
                    pass

            def by_pair(x, l):
                return x.rearrange("p (b t) -> p b t", t=2 << l)

            blocks = "p (n t) -> p n t"

            def hg_mix(step, j):
                if step[0] == "hg_prep":
                    d.wait()
                    d.settle()
                    d.did(v.tensor_copy(h_hp, h_par[:, j, :] if isinstance(j, int)
                                        else h_par[:, bass.ds(j, 1), :].rearrange("p h c -> p (h c)")))
                    op(v.tensor_copy, h_q, hq_in, sem=s["h_cut"], value=j + 1)
                    v.wait_ge(s["h_sig"], 2 * j + 2)
                    op(v.tensor_scalar, h_b, h_eb, h_hp[:, 1:2], h_hp[:, 0:1], ALU.mult, ALU.add,
                       sem=s["h_fb"], value=j + 1)
                    op(v.tensor_scalar, h_k, h_d, h_hp[:, 1:2], None, ALU.mult)
                    v.wait_ge(s["h_ln"], j + 1)
                    for n in range(NB):
                        b = slice(n * P, n * P + P)
                        op(v.tensor_tensor_scan, h_b[:, b], ones, h_eb[:, b], 0.0, ALU.mult, ALU.add)
                    op(v.tensor_tensor, h_w1, h_q, h_k, ALU.mult, sem=s["h_qk"], value=j + 1)
                elif step[0] == "hg_diagonal":
                    v.wait_ge(s["h_diag"], j + 1)
                    op(v.tensor_tensor, h_a.rearrange(blocks, n=NB), bankB[:, 1, :].rearrange(blocks, n=NB),
                       ident[:, None, :].to_broadcast([P, NB, P]), ALU.mult)
                elif step[0] == "hg_level":
                    l = step[1]
                    h = 1 << l
                    w = (h_w0, h_w1)[l % 2]
                    bv, dv = by_pair(h_b, l), by_pair(h_d, l)
                    ref = bv[:, :, h - 1:h].to_broadcast([P, T // (2 * h), h])
                    op(v.tensor_tensor, dv[:, :, h:2 * h], bv[:, :, h:2 * h], ref, ALU.subtract)
                    op(v.tensor_tensor, dv[:, :, 0:h], ref, bv[:, :, 0:h], ALU.subtract,
                       sem=s["h_dr"], value=LEVELS * j + l + 1)
                    v.wait_ge(s["h_ex"], LEVELS * j + l + 1)
                    op(v.tensor_tensor, by_pair(w, l)[:, :, h:2 * h], by_pair(h_q, l)[:, :, h:2 * h],
                       dv[:, :, h:2 * h], ALU.mult)
                    op(v.tensor_tensor, by_pair(w, l)[:, :, 0:h], by_pair(h_k, l)[:, :, 0:h],
                       dv[:, :, 0:h], ALU.mult, sem=s["h_wr"], value=LEVELS * j + l + 1)
                    v.wait_ge(s["h_pr"], LEVELS * j + l + 1)
                    d.wait()
                    d.settle()
                    d.did(v.copy_predicated(h_a.rearrange(blocks, n=NB), lowT[:, l:l + 1, :].to_broadcast([P, NB, P]),
                                            bankA[:, l % 2, :].rearrange(blocks, n=NB)),
                          s["h_pred"], LEVELS * j + l + 1)
                elif step[0] == "hg_state":
                    b3 = h_b.rearrange(blocks, n=NB)
                    op(v.tensor_tensor, h_d.rearrange(blocks, n=NB), b3[:, :, P - 1:P].to_broadcast([P, NB, P]), b3,
                       ALU.subtract, sem=s["h_kx"], value=j + 1)
                    v.wait_ge(s["h_kxe"], j + 1)
                    op(v.tensor_tensor, h_kdt, h_k, h_d, ALU.mult, sem=s["h_kdr"], value=j + 1)
                    v.wait_ge(s["h_ebx"], j + 1)
                    op(v.tensor_tensor, h_qe, h_q, h_eb, ALU.mult)
                elif step[0] == "hg_mix":
                    v.wait_ge(s["h_st"], j + 1)
                    op(v.tensor_copy, h_s[:, 0:P], bankB[:, 1, 0:P])
                    for n in range(1, NB - 1):
                        b = slice(n * P, n * P + P)
                        op(v.scalar_tensor_tensor, h_s[:, b], h_s[:, (n - 1) * P:n * P],
                           h_eb[:, n * P + P - 1:n * P + P], bankB[:, 1, b], ALU.mult, ALU.add,
                           sem=s["h_sr"] if n == NB - 2 else None, value=j + 1)
                elif step[0] == "hg_out":
                    v.wait_ge(s["h_ort"], j + 1)
                    v.wait_ge(s["h_gs"], j + 1)
                    op(v.reciprocal, h_rt, h_rt)
                    op(v.scalar_tensor_tensor, h_rt, bankC[:, 0, :], h_hp[:, 2:3], h_rt, ALU.mult, ALU.mult)
                    op(v.tensor_tensor, h_y, h_rt, h_gate, ALU.mult, sem=s["h_yr"], value=j + 1)

            def hg_trip(g, j, tiles=True, mix=True):
                for step in interleave(4 if tiles else 0, HG_STEPS if mix else []):
                    if step[0] == "evict":
                        hg_evict(step[1], g)
                    elif step[0] != "gemm":
                        hg_mix(step, j)

            hg_trip(0, None, mix=False)
            with v.Fori(0, HGH - 1) as j:
                d.enter(j, HG_VECTOR_STEPS)
                hg_trip(j + 1, j)
            d.leave(HGH - 1)
            hg_trip(None, HGH - 1, tiles=False)

            v.wait_ge(s["ys_loaded"], 48)
            fill(5, ys, None)
            v.wait_ge(s["src_loaded"], 64)
            for c in range(2):
                add_tile(xt[:, c, :], W_OUT2, c)
            with v.Fori(0, KT // 2 - 1) as i:
                d.enter(i, 0)
                for c in range(2):
                    add_tile(xt[:, bass.ds(2 * i + 2 + c, 1), :].rearrange("p k t -> p (k t)"),
                             W_OUT2 + 2, c, i, 2)
            d.leave(KT // 2 - 1)

            v.wait_ge(s["src_loaded"], 80)
            fill(6, pe_src, None, blocks=2)
            for e in range(16):
                slot, n = tile_at(W_PE, e // 8)
                if e % 8 < 7:
                    v.wait_ge(s["e_done"], 7 * (e // 8) + e % 8 + 1)
                else:
                    v.wait_ge(gemm_done[slot], n + 1)
                op(v.tensor_copy, ets[:, e, :], gemm_ps[e % 2][:, :], sem=s["e_out"], value=e + 1)

            for w in range(2):
                v.sem_inc(evicted[w], 1)

            fill(7, xt, C_PEN)
            reciprocal_root(3)

            def gated(c, base, i=0, per=0):
                slot, n = tile_at(base, c, i, per)
                k = c if per == 0 else 2 * i + 2 + c
                x_, e_ = ((xt[:, k, :], ets[:, k, :]) if isinstance(k, int) else
                          (a[:, bass.ds(k, 1), :].rearrange("p k t -> p (k t)") for a in (xt, ets)))
                v.wait_ge(gemm_done[slot], n + 1)
                op(v.tensor_tensor, stage[:, c, :], gemm_ps[slot][:, :], rstd, ALU.mult, sem=evicted[slot],
                   value=n + 1)
                v.wait_ge(s["sg_out"], k + 1)
                op(v.tensor_tensor, stage[:, c, :], stage[:, c, :], e_, ALU.mult)
                op(v.tensor_tensor, x_, x_, stage[:, c, :], ALU.add)

            for c in range(2):
                gated(c, W_PG)
            with v.Fori(0, KT // 2 - 1) as i:
                d.enter(i, 4)
                for c in range(2):
                    gated(c, W_PG + 2, i, 2)
            d.leave(KT // 2 - 1)
            d.wait()
            v.memset(nul[:, :], 0.0).then_inc(s["sg_in"], 1)

            reciprocal_root(4)
            for k in range(KT):
                op(v.scalar_tensor_tensor, xt[:, k, :], xt[:, k, :], gains(C_FIN + k), rstd, ALU.mult, ALU.mult,
                   sem=s["out_ready"], value=k + 1)

        @block.scalar
        def _(act):
            d = Steps(act, act_step, pad)

            def op(dst, src, func, sem=None, value=None, **kw):
                d.wait()
                d.did(act.activation(dst, src, func, **kw), sem, value)

            def squares_and_high(q, f, src, width=T, gain=True, blocks=KT):
                if f is not None:
                    for w in range(2):
                        if used_before(FILLS[f], w):
                            act.wait_ge(gemm_done[w], used_before(FILLS[f], w))
                for k in range(blocks):
                    if q is not None:
                        if KT * q + k >= 2:
                            act.wait_ge(s["sq_summed"], KT * q + k - 1)
                        op(sqr[:, k % 2, 0:width], src[:, k, :], ACT.Square, s["squared"], KT * q + k + 1)
                    if f is not None:
                        if gain:
                            act.wait_ge(s["staged"], KT * GAINED[f] + k + 1)
                        op(a_hi[:, k, 0:width], stage[:, k % 4, 0:width] if gain else src[:, k, :], ACT.Copy,
                           act_hi, CUT_AT[f] + k + 1)
                if q is not None:
                    act.wait_ge(s["sq_summed"], KT * q + KT)
                    op(root[:, 0:width], bankA[:, 0, 0:width], ACT.Sqrt, s["root_ready"], q + 1,
                       bias=eps[:, :], scale=1.0 / D)

            act.dma_start(src_mem, memT).then_inc(s["src_loaded"], 16)
            act.dma_start(par[:, :], params).then_inc(const_loaded, 16)
            act.dma_start(con[:, 0:4, :], consts[:, 0:4, :]).then_inc(const_loaded, 16)
            act.dma_start(con[:, 4:4 + 2 * LEVELS, :], consts[:, 4:4 + 2 * LEVELS, :]).then_inc(const_loaded, 16)
            act.wait_ge(filled, 2)
            act.wait_ge(s["src_loaded"], 16)
            squares_and_high(0, 0, src_mem, M)
            act.wait_ge(s["squared"], KT)
            act.wait_ge(s["staged"], KT)
            act.dma_start(src0, xT).then_inc(s["src_loaded"], 16)
            for h in range(XH):
                act.wait_ge(evicted[1], h + 1)
                if h >= 2:
                    act.wait_ge(s["kv_sum"], h - 1)
                op(sqr[:, h % 2, :], kv[:, 2 * h:2 * h + 2, :].rearrange("p c m -> p (c m)"), ACT.Square,
                   s["kv_sq"], h + 1)
            act.wait_ge(s["kv_sum"], XH)
            for h in range(XH):
                op(stage[:, h, 0:M], bankA[:, h // 2, h % 2 * M:h % 2 * M + M], ACT.Sqrt, s["kv_root"], h + 1,
                   bias=eps[:, :], scale=1.0 / (2 * P))
            act.wait_ge(s["vT_done"], 1)
            for b, bank in enumerate((bankB, bankC)):
                op(vmem[:, :, b * T:b * T + T], bank[:, :, :], ACT.Copy, s["v_done"], b + 1)

            act.wait_ge(s["src_loaded"], 32)
            squares_and_high(1, 1, src0)
            act.wait_ge(s["ab_x"], 1)
            op(ab[32:32 + VH, 2, :], ab[32:32 + VH, 0, :], ACT.Sigmoid)
            act.wait_ge(s["ab_x"], 2)
            op(ab[0:VH, 1, :], ab[0:VH, 1, :], ACT.Exp, s["ab_exp"], 1, scale=-1.0)
            op(ab[0:VH, 4, 0:1], par[0:VH, C_ALOG:C_ALOG + 1], ACT.Exp, s["ab_exp"], 2)
            act.wait_ge(s["ab_x"], 3)
            op(ab[0:VH, 1, :], ab[0:VH, 1, :], ACT.Ln, s["ab_exp"], 3)
            op(ab[0:VH, 4, 1:2], ab[0:VH, 4, 0:1], ACT.Copy, s["ab_exp"], 4)
            act.wait_ge(s["ab_x"], 4)
            act.dma_start(gc_dram[:, :], ab[0:VH, 3, :]).then_inc(s["gc_stored"], 16)
            op(ab[0:VH, 1, :], ab[0:VH, 1, :], ACT.Exp, s["ab_exp"], 5)
            act.wait_ge(s["gc_stored"], 16)

            for h in range(XH):
                for step in XA_ORDER:
                    if step[0] == "evict" and step[1] >= 2:
                        slot, n = tile_at(W_XA + 4 * h, step[1])
                        act.wait_ge(evicted[slot], n + 1)
                        op(xz[:, step[1] - 2, :], xz[:, step[1] - 2, :], ACT.Silu, s["z_silu"], 2 * h + step[1] - 1)
                    elif step[0] == "q_norm":
                        slot, n = tile_at(W_XA + 4 * h, 1)
                        act.wait_ge(evicted[slot], n + 1)
                        op(sqr[:, :, :], xq[:, :, :], ACT.Square, s["q_sq"], h + 1)
                        act.wait_ge(s["q_sum"], h + 1)
                        op(xrt[:, 0, :], bankA[:, 0, :], ACT.Sqrt, s["q_root"], h + 1, bias=eps[:, :],
                           scale=1.0 / (2 * P))
                    elif step[0] == "scores":
                        act.wait_ge(s["max_ready"], h + 1)
                        if h > 0:
                            act.wait_ge(s["pT_done"], h)
                        for n in range(NB):
                            op(xp[:, n, :], bankB[:, n // 2, n % 2 * M:n % 2 * M + M], ACT.Exp, s["p_exp"],
                               NB * h + n + 1, bias=xsm[:, 1, n:n + 1], scale=1.0 / 16, accum_out=xsm[:, 2, n:n + 1])
                    elif step[0] == "weights":
                        act.wait_ge(s["pT_done"], h + 1)
                        op(xpT[:, :, :], bankC[:, :, :], ACT.Copy, s["pT_sbuf"], h + 1)
                    elif step[0] == "values":
                        act.wait_ge(s["y_ready"], 2 * h + 2)
                        act.dma_start(y_dram[VH + 2 * h:VH + 2 * h + 2].rearrange("a p t -> p a t"),
                                      xy[:, :, :]).then_inc(s["y_stored"], 16)

            def load_decay(j):
                rows = gc_dram[bass.ds(2 * j, 2), :] if not isinstance(j, int) else gc_dram[2 * j:2 * j + 2, :]
                act.dma_start(gcb[:, :, :], rows[None, :, :].to_broadcast([P, 2, T])).then_inc(s["gc_loaded"], 16)

            def gates(g):
                for c in range(2):
                    slot, n = tile_at(W_DN, c, g, 6)
                    act.wait_ge(evicted[slot], n + 1)
                    op(z_g[:, c, :], z_in[:, c, :], ACT.Silu, s["gate"], 2 * g + c + 1)

            def dn_mix(step, j):
                if step[0] == "qk_norm":
                    for a in range(2):
                        op(sqr[:, a, :], cv[:, a, :], ACT.Square, s["dq_sq"], 2 * j + a + 1)
                    for a in range(2):
                        act.wait_ge(s["dq_sum"], 2 * j + a + 1)
                        op(T1[:, a, :, :].rearrange("p n t -> p (n t)"), bankA[:, a, :], ACT.Sqrt, s["dq_root"],
                           2 * j + a + 1, bias=eps[:, :])
                elif step[0] == "natural":
                    act.wait_ge(s["nat_v"], j + 1)
                    for a in range(2):
                        op(vn[:, a, :, :].rearrange("p n t -> p (n t)"), bankC[:, a, :], ACT.Copy, s["vn_sbuf"],
                           2 * j + a + 1)
                    act.wait_ge(s["diff"], j + 1)
                    op(dT[:, :, :, :], dT[:, :, :, :], ACT.Exp, s["expd"], 3 * j + 1)
                    op(Nm[:, :, :, :], Nm[:, :, :, :], ACT.Exp, s["expd"], 3 * j + 2, scale=-1.0)
                    op(gcb[:, :, :], gcb[:, :, :], ACT.Exp, s["expd"], 3 * j + 3)
                elif step[0] == "transposed":
                    act.wait_ge(s["nT"], j + 1)
                    op(NmT[:, :, :, :], quad(bankB), ACT.Copy, s["nT_sbuf"], j + 1)
                elif step[0] == "half":
                    act.wait_ge(s["t1"], (LEVELS - 1) * j + step[1])
                    op(T1[:, :, :, :], quad(bankA), ACT.Copy, s["t1_sbuf"], (LEVELS - 1) * j + step[1])
                elif step[0] == "update":
                    act.wait_ge(s["u"], NB * j + step[1] + 1)
                    op(uu[:, :, :], bankB[:, 0, 0:2 * P].rearrange("p (a t) -> p a t", a=2), ACT.Copy, s["u_sbuf"],
                       NB * j + step[1] + 1)
                elif step[0] == "head_out":
                    act.wait_ge(s["o"], NB * j + NB)
                    for a in range(2):
                        op(sqr[:, a, :], bankC[:, a, :], ACT.Square, s["o_sq"], 2 * j + a + 1)
                    for a in range(2):
                        act.wait_ge(s["o_sum"], 2 * j + a + 1)
                        op(ort[:, a, :], bankB[:, a, :], ACT.Sqrt, s["o_root"], 2 * j + a + 1, bias=eps[:, :],
                           scale=1.0 / P)
                    act.wait_ge(s["dy_ready"], 2 * j + 2)
                    y_rows = y_dram[bass.ds(2 * j, 2)] if not isinstance(j, int) else y_dram[2 * j:2 * j + 2]
                    act.dma_start(y_rows.rearrange("a p t -> p a t"), yo[:, :, :]).then_inc(s["dy_stored"], 16)

            def dn_trip(g, j, tiles=True, mix=True):
                for step in interleave(6 if tiles else 0, DN_STEPS if mix else []):
                    if step[0] == "evict" and step[1] >= 2:
                        act.wait_ge(s["conv"], 4 * g + step[1] - 1)
                        op(cv[:, step[1] - 2, :], cv[:, step[1] - 2, :], ACT.Silu, s["silu"], 4 * g + step[1] - 1)
                    elif step[0] not in ("gemm", "evict"):
                        dn_mix(step, j)
                if tiles:
                    gates(g)
                    load_decay(g)
                if mix:
                    act.wait_ge(s["dy_stored"], 16 * j + 16)

            dn_trip(0, None, mix=False)
            with act.Fori(0, QKH - 1) as j:
                d.enter(j, 0)
                dn_trip(j + 1, j)
            d.leave(QKH - 1)
            dn_trip(None, QKH - 1, tiles=False)

            act.wait_ge(s["y_stored"], 16 * XH)
            for half in range(2):
                if half:
                    act.wait_ge(act_lo, KT * 3)
                act.dma_start(ys, y_dram[KT * half:KT * half + KT].rearrange("a p t -> p a t")).then_inc(
                    s["ys_loaded"], 16)
                if half == 0:
                    act.dma_start(xt, xT).then_inc(s["src_loaded"], 16)
                act.wait_ge(s["ys_loaded"], 16 * half + 16)
                squares_and_high(None, 2 + half, ys, gain=False)

            for w in range(2):
                act.wait_ge(evicted[w], used_before(W_GATE, w))
            act.dma_start(x2_dram[:, :, :], xt).then_inc(s["x2_stored"], 16)
            squares_and_high(2, 4, xt)
            act.wait_ge(s["h_lb"], 1)
            op(h_tmp, h_tmp, ACT.Exp, s["h_lbexp"], 1)
            f1 = ab[32:32 + MLH, 1, :]
            act.wait_ge(s["g_x"], 1)
            op(f1, f1, ACT.Exp, s["g_exp"], 1, scale=-1.0)
            act.wait_ge(s["g_x"], 2)
            op(f1, f1, ACT.Ln, s["g_exp"], 2)
            act.wait_ge(s["g_x"], 3)
            op(ab[0:MLH, 2, :], ab[0:MLH, 2, :], ACT.Exp, s["g_exp"], 3, scale=-1.0)
            act.wait_ge(s["g_x"], 4)
            act.wait_ge(s["g_exp"], 3)
            act.dma_start(ml_dram[:, 0, :], ab[0:MLH, 3, :]).then_inc(s["ml_stored"], 16)
            act.dma_start(ml_dram[:, 1, :], ab[0:MLH, 2, :]).then_inc(s["ml_stored"], 16)
            act.wait_ge(s["ml_stored"], 32)

            def ml_mix(step, j):
                if step[0] == "ml_scores":
                    act.wait_ge(s["mvT"], j + 1)
                    op(m_vn[:, :, :, :], quad(bankB), ACT.Copy, s["m_vn"], j + 1)
                    for n in range(NB):
                        act.wait_ge(s["m_diff"], NB * j + n + 1)
                        op(m_s[:, n, n * P:T], m_s[:, n, n * P:T], ACT.Exp, s["m_expd"], NB * j + n + 1)
                elif step[0] == "ml_sums":
                    act.wait_ge(s["m_den"], j + 1)
                    op(m_den, bankB[:, 0, :], ACT.Copy, s["m_dencp"], j + 1)
                elif step[0] == "ml_out":
                    act.wait_ge(s["m_hd"], j + 1)
                    op(sqr[:, :, :], m_h[:, :, :], ACT.Square, s["m_sq"], j + 1)
                    act.wait_ge(s["m_sum"], j + 1)
                    op(m_den, bankA[:, 0, :], ACT.Sqrt, s["m_root"], j + 1, bias=eps[:, :], scale=1.0 / (2 * P))
                    act.wait_ge(s["m_yr"], j + 1)
                    y_rows = y2_dram[bass.ds(2 * j, 2)] if not isinstance(j, int) else y2_dram[2 * j:2 * j + 2]
                    act.dma_start(y_rows.rearrange("a p t -> p a t"), m_y[:, :, :]).then_inc(s["m_yst"], 16)

            def ml_trip(g, j, tiles=True, mix=True):
                for step in interleave(8 if tiles else 0, ML_STEPS if mix else []):
                    if step[0] == "evict" and step[1] in (4, 5):
                        act.wait_ge(s["m_conv"], 2 * g + step[1] - 3)
                        op(mc[:, step[1] - 4, :], mc[:, step[1] - 4, :], ACT.Silu, s["m_silu"], 2 * g + step[1] - 3)
                    elif step[0] not in ("gemm", "evict"):
                        ml_mix(step, j)
                if tiles:
                    for c in range(4):
                        slot, n = tile_at(W_ML, c, g, 8)
                        act.wait_ge(evicted[slot], n + 1)
                    op(m_z[:, :, :], m_z[:, :, :], ACT.Silu)
                    op(m_o[:, :, :], m_o[:, :, :], ACT.Sigmoid, s["m_gate"], g + 1)
                    rows = ml_dram[bass.ds(g, 1)].rearrange("h q t -> (h q) t") if not isinstance(g, int) else ml_dram[g]
                    act.dma_start(m_rows[:, :, :], rows[None, :, :].to_broadcast([P, 2, T])).then_inc(
                        s["ml_loaded"], 16)
                if mix:
                    act.wait_ge(s["m_yst"], 16 * j + 16)

            ml_trip(0, None, mix=False)
            with act.Fori(0, MLH - 1) as j:
                d.enter(j, 1)
                ml_trip(j + 1, j)
            d.leave(MLH - 1)
            ml_trip(None, MLH - 1, tiles=False)

            def hg_mix(step, j):
                if step[0] == "hg_prep":
                    slot, n = tile_at(W_HG, 2, j, 4)
                    act.wait_ge(evicted[slot], n + 1)
                    op(h_eb, hf_in, ACT.Sigmoid, s["h_sig"], 2 * j + 1)
                    op(h_d, hf_in, ACT.Sigmoid, s["h_sig"], 2 * j + 2, scale=-1.0)
                    act.wait_ge(s["h_vT"], j + 1)
                    op(h_vn, bankB[:, 0, :], ACT.Copy, s["h_vns"], j + 1)
                    act.wait_ge(s["h_fb"], j + 1)
                    op(h_eb, h_b, ACT.Ln, s["h_ln"], j + 1)
                elif step[0] == "hg_level":
                    act.wait_ge(s["h_dr"], LEVELS * j + step[1] + 1)
                    op(h_d, h_d, ACT.Exp, s["h_ex"], LEVELS * j + step[1] + 1)
                    if step[1] == 0:
                        op(h_eb, h_b, ACT.Exp, s["h_ebx"], j + 1)
                elif step[0] == "hg_state":
                    act.wait_ge(s["h_kx"], j + 1)
                    op(h_d, h_d, ACT.Exp, s["h_kxe"], j + 1)
                    act.wait_ge(s["h_kT"], j + 1)
                    op(h_kd, bankB[:, 0, :], ACT.Copy, s["h_kds"], j + 1)
                elif step[0] == "hg_out":
                    act.wait_ge(s["h_o"], j + 1)
                    op(sqr[:, 0, :], bankC[:, 0, :], ACT.Square, s["h_osq"], j + 1)
                    act.wait_ge(s["h_osum"], j + 1)
                    op(h_rt, bankC[:, 1, :], ACT.Sqrt, s["h_ort"], j + 1, bias=eps[:, :], scale=1.0 / P)
                    act.wait_ge(s["h_yr"], j + 1)
                    y_row = y2_dram[bass.ds(j + 2 * MLH, 1)] if not isinstance(j, int) else y2_dram[2 * MLH + j:2 * MLH + j + 1]
                    act.dma_start(y_row.rearrange("a p t -> p (a t)"), h_y).then_inc(s["h_yst"], 16)

            def hg_trip(g, j, tiles=True, mix=True):
                for step in interleave(4 if tiles else 0, HG_STEPS if mix else []):
                    if step[0] not in ("gemm", "evict"):
                        hg_mix(step, j)
                if tiles:
                    slot, n = tile_at(W_HG, 0, g, 4)
                    act.wait_ge(evicted[slot], n + 1)
                    op(h_gate, hg_in, ACT.Silu, s["h_gs"], g + 1)
                if mix:
                    act.wait_ge(s["h_yst"], 16 * j + 16)

            hg_trip(0, None, mix=False)
            with act.Fori(0, HGH - 1) as j:
                d.enter(j, 0)
                hg_trip(j + 1, j)
            d.leave(HGH - 1)
            hg_trip(None, HGH - 1, tiles=False)

            act.dma_start(ys, y2_dram[:, :, :].rearrange("a p t -> p a t")).then_inc(s["ys_loaded"], 16)
            act.dma_start(xt, x2_dram[:, :, :]).then_inc(s["src_loaded"], 16)
            act.wait_ge(s["src_loaded"], 64)
            act.wait_ge(s["h_yr"], HGH)
            act.dma_start(pe_src, peT).then_inc(s["src_loaded"], 16)
            act.wait_ge(s["ys_loaded"], 48)
            squares_and_high(None, 5, ys, gain=False)

            act.wait_ge(s["src_loaded"], 80)
            squares_and_high(None, 6, pe_src, gain=False, blocks=2)
            squares_and_high(3, 7, xt)

            def gate(c, base, i=0, per=0):
                slot, n = tile_at(base, c, i, per)
                act.wait_ge(evicted[slot], n + 1)
                op(stage[:, c, :], stage[:, c, :], ACT.Sigmoid, s["sg_out"], (c if per == 0 else 2 * i + 2 + c) + 1)

            for c in range(2):
                gate(c, W_PG)
            with act.Fori(0, KT // 2 - 1) as i:
                d.enter(i, 0)
                for c in range(2):
                    gate(c, W_PG + 2, i, 2)
            d.leave(KT // 2 - 1)

            act.wait_ge(s["sg_in"], 1)
            squares_and_high(4, None, xt)
            for k in range(0, KT, 4):
                act.wait_ge(s["out_ready"], k + 4)
                act.dma_start(out[:, k:k + 4, :], xt[:, k:k + 4, :]).then_inc(s["out_stored"], 16)
            act.wait_ge(s["out_stored"], 16 * (KT // 4))


XA_ORDER = ([("gemm", c, k) if k < KT else ("evict", c) for c in range(2) for k in range(KT + 1)]
            + [(x[0], x[1] + 2, *x[2:]) if x[0] in ("gemm", "evict") else x
               for x in interleave(2, [("q_norm",), ("scores",), ("weights",)])]
            + [("values",)])
DN_VECTOR_STEPS = 75


def kernel(**inputs):
    import concourse.bacc as bacc
    from concourse.bass_utils import run_bass_kernel_spmd

    f = {n: np.asarray(a) for n, a in inputs.items()}

    def tiles(w):
        k, c = w.shape
        return w.reshape(k // D, KT, P, c // P, P).transpose(0, 3, 2, 1, 4).reshape(-1, P, KT, P)

    def padded(w, at, columns):
        r = np.zeros((D, P), np.float32)
        for start, c in zip(at, columns):
            r[:, start:start + c.shape[1]] = c
        return tiles(r)

    w = f["dn_w_in"][0]
    qk, mix = QKH * P, VH * P
    c_a = 2 * qk + mix
    c_xq = c_a + 2 * VH
    c_z = c_xq + XH * 256
    q_t, k_t, v_t = tiles(w[:, :qk]), tiles(w[:, qk:2 * qk]), tiles(w[:, 2 * qk:c_a])
    xq_t, z_t = tiles(w[:, c_xq:c_z]), tiles(w[:, c_z:])
    w2 = f["w_in_2"][0]
    stream = [tiles(f["mem_w_kv"][0]), padded(w, (0, 32), (w[:, c_a:c_a + VH], w[:, c_a + VH:c_xq]))]
    for h in range(XH):
        stream += [xq_t[2 * h:2 * h + 2], z_t[VH + 2 * h:VH + 2 * h + 2]]
    for h in range(QKH):
        stream += [z_t[2 * h:2 * h + 2], q_t[h:h + 1], k_t[h:h + 1], v_t[2 * h:2 * h + 2]]
    stream += [tiles(f["w_out"][0])]
    c_if = 2 * MLH * P + 3 * MLH * 256
    ml_t, hg_t = tiles(w2[:, :c_if]), tiles(w2[:, c_if + 2 * MLH:])
    stream += [padded(w2, (0, 32), (w2[:, c_if:c_if + MLH], w2[:, c_if + MLH:c_if + 2 * MLH]))]
    for h in range(MLH):
        q, k, v, o, z = h, MLH + h, 2 * MLH + 2 * h, 4 * MLH + 2 * h, 6 * MLH + 2 * h
        stream += [ml_t[o:o + 2], ml_t[z:z + 2], ml_t[q:q + 1], ml_t[k:k + 1], ml_t[v:v + 2]]
    for h in range(HGH):
        stream += [hg_t[c * HGH + h:c * HGH + h + 1] for c in (3, 0, 1, 2)]
    stream += [tiles(f["w_out_2"][0])]
    stream += [f["w_pe_2"][0].reshape(2, P, 2, 8, P).transpose(2, 1, 3, 0, 4).reshape(2, P, KT, P)]
    stream += [tiles(f["w_pg_2"][0])]
    n = sum(len(x) for x in stream)
    stream += [np.zeros((W_END + W_END % 2 - n, P, KT, P), np.float32)]
    stream = np.concatenate(stream)

    def by_row_block(a, width):
        return np.ascontiguousarray(a.T.reshape(-1, P, width).transpose(1, 0, 2))

    params = np.zeros((P, NPAR), np.float32)
    for c, n in ((C_NORM, "norm_g"), (C_MEMN, "mem_norm_g"), (C_XQ, "xa_q_norm_g"), (C_XK, "xa_k_norm_g"),
                 (C_DNOUT, "dn_out_norm_g"), (C_NORM2, "norm_w_2"), (C_PEN, "pe_norm_w_2"), (C_FIN, "final_norm_w_2")):
        g = f[n].reshape(-1, P)
        params[:, c:c + len(g)] = g.T
    params[0:VH, C_ALOG] = f["dn_a_log"][0]
    params[0:VH, C_DT] = f["dn_dt_bias"][0]
    taps = f["dn_conv_w"][0].reshape(4, -1, P)
    for h in range(QKH):
        for c, t in enumerate((h, QKH + h, 2 * QKH + 2 * h, 2 * QKH + 2 * h + 1)):
            params[:, C_DNCONV + 16 * h + 4 * c:C_DNCONV + 16 * h + 4 * c + 4] = taps[:, t, :].T

    params[0:MLH, C_IFB], params[32:32 + MLH, C_IFB] = f["ml_b_i_2"][0], f["ml_b_f_2"][0]
    taps2, bias2, gain2 = f["conv_w_2"][0].reshape(4, -1, P), f["conv_b_2"][0].reshape(-1, P), \
        f["ml_norm_w_2"][0].reshape(-1, P)
    for h in range(MLH):
        c = C_ML + 12 * h
        params[:, c:c + 4], params[:, c + 4:c + 8] = taps2[:, h, :].T, taps2[:, MLH + h, :].T
        params[:, c + 8], params[:, c + 9] = bias2[h], bias2[MLH + h]
        params[:, c + 10], params[:, c + 11] = gain2[2 * h], gain2[2 * h + 1]
    params[:, C_HGL:C_HGL + 2 * HGH] = f["hg_lb_2"].reshape(2 * HGH, P).T
    params[:, C_HGN:C_HGN + HGH] = f["hg_norm_w_2"][0].reshape(HGH, P).T

    consts = np.zeros((P, 4 + 2 * LEVELS, P), np.float32)
    r, c = np.arange(P)[:, None], np.arange(P)[None, :]
    consts[:, 0], consts[:, 1], consts[:, 2] = 1.0, r == c, c >= r
    for n in range(LEVELS):
        m = (r >> (n + 1) == c >> (n + 1)) & (r >> n & 1 == 1) & (c >> n & 1 == 0)
        consts[:, 4 + n], consts[:, 4 + LEVELS + n] = m, m.T

    arrays = {
        "w_stream": stream,
        "x_t": by_row_block(f["x"][0], T),
        "mem_t": by_row_block(f["mem"][0], M),
        "pe_t": by_row_block(f["p_2"][0, 0], T),
        "gains": params,
        "shape_consts": consts,
    }
    nc = bacc.Bacc("TRN2", target_bir_lowering=False, num_devices=1)
    handles = [nc.dram_tensor(n, a.shape, F32, kind="ExternalInput").ap() for n, a in arrays.items()]
    out = nc.dram_tensor("y_out", (P, KT, T), F32, kind="ExternalOutput").ap()
    build(nc, *handles, out)
    got = run_bass_kernel_spmd(nc, [arrays], core_ids=[0]).results[0]["y_out"]
    return np.ascontiguousarray(got.transpose(1, 0, 2).reshape(D, T).T)[None]
```

```python
from contextlib import ExitStack

import numpy as np
import concourse.bass as bass
from concourse import mybir

F32 = mybir.dt.float32
F32R = mybir.dt.float32r
U32 = mybir.dt.uint32
ALU = mybir.AluOpType
ACT = mybir.ActivationFunctionType
AX = mybir.AxisListType

P = 128
T = 512
D = 2048
KT = D // P
NB = T // P
M = 256
EPS = 1e-6
QKH = 12
VH = 2 * QKH
XH = 4
MLH = 4
HGH = 8
LEVELS = 7

W_MEM = 0
W_AB = 2 * (XH * 256) // P
W_XA = W_AB + 1
W_DN = W_XA + 4 * XH
W_OUT = W_DN + 6 * QKH
W_GATE = W_OUT + 2 * KT
W_ML = W_GATE + 1
W_HG = W_ML + 8 * MLH
W_OUT2 = W_HG + 4 * HGH
W_PE = W_OUT2 + KT
W_PG = W_PE + 2
W_END = W_PG + KT

_o = [0]


def _cols(n):
    _o[0] += n
    return _o[0] - n


C_NORM, C_MEMN = _cols(KT), _cols(KT)
C_XQ, C_XK = _cols(2), _cols(2)
C_DNOUT = _cols(1)
C_ALOG, C_DT = _cols(1), _cols(1)
C_DNCONV = _cols(QKH * 16)
C_NORM2 = _cols(KT)
C_IFB = _cols(1)
C_ML = _cols(MLH * 12)
C_HGL = _cols(2 * HGH)
C_HGN = _cols(HGH)
C_PEN, C_FIN = _cols(KT), _cols(KT)
NPAR = _o[0]


class Steps:

    def __init__(self, eng, sem, pad):
        self.eng, self.sem, self.pad = eng, sem, pad
        self.start, self.loop, self.k, self.last = 0, 0, 0, None

    def did(self, ins, sem=None, value=None):
        if sem is None:
            self.k += 1
            sem, value = self.sem, self.start + self.loop + self.k
        ins.then_inc(sem, 1)
        self.last = (sem, value)

    def wait(self):
        if self.last is not None:
            self.eng.wait_ge(*self.last)

    def settle(self):
        self.eng.sem_inc(self.pad, 1)

    def enter(self, i, per):
        self.start, self.k, self.per, self.last = self.start + self.k, 0, per, None
        self.loop = i * per
        if self.start > 0:
            self.last = (self.sem, self.start + self.loop)

    def leave(self, trips):
        assert self.k == self.per, ("steps in a trip", self.k)
        self.start, self.loop, self.k = self.start + trips * self.per, 0, 0


def tile_at(base, c, i=0, per=0):
    return (base + c) % 2, (base + c) // 2 + (per // 2) * i


def interleave(tiles, steps):
    parts = [("gemm", c, k) for c in range(tiles) for k in range(KT)]
    whole = sum(x[-1] for x in steps)
    order, done, due = [], 0, 0
    for n, part in enumerate(parts):
        while done < len(steps) and due * len(parts) <= n * whole:
            order.append(steps[done])
            due += steps[done][-1]
            done += 1
        order.append(part)
        if part[2] == KT - 1:
            order.append(("evict", part[1]))
    return order + steps[done:]


EARLY = 6

DN_STEPS = ([("qk_norm", 36), ("natural", 6), ("transposed", 5)]
            + [(s, l, g) for l in range(1, LEVELS) for s, g in (("half", 2), ("whole", 4))]
            + [(s, n, g) for n in range(NB) for s, g in (("rest", 2), ("update", 1.5), ("output", 2))]
            + [("head_out", 5)])


ML_STEPS = [("ml_scores", 30), ("ml_sums", 30), ("ml_out", 40)]
HG_STEPS = ([("hg_start", 9), ("hg_prep", 12), ("hg_diagonal", 2)]
            + [("hg_level", l, 3.5) for l in range(LEVELS)]
            + [("hg_state", 4), ("hg_mix", 3), ("hg_out", 5)])
ML_VECTOR_STEPS = 24
HG_VECTOR_STEPS = 26


def build(nc, weights, xT, memT, peT, params, consts, out):
    ctx = ExitStack()

    def sb(name, shape, dt=F32):
        return ctx.enter_context(nc.sbuf_tensor(name, shape, dt))

    def sem(name):
        return ctx.enter_context(nc.semaphore(name))

    with ctx:
        w_raw = sb("w_raw", [P, 2, KT, P])
        w_hi = sb("w_hi", [P, 2, KT, P], F32R)
        w_lo = sb("w_lo", [P, 2, KT, P], F32R)
        a_hi = sb("a_hi", [P, KT, T], F32R)
        a_lo = sb("a_lo", [P, KT, T], F32R)
        par = sb("par", [P, NPAR])
        con = sb("con", [P, 4 + 2 * LEVELS, P])
        ones, ident, incl, reset = (con[:, n, :] for n in range(4))
        low = con[:, 4:4 + LEVELS, :].bitcast(U32)
        lowT = con[:, 4 + LEVELS:4 + 2 * LEVELS, :].bitcast(U32)
        eps = sb("eps", [P, 1])
        nul = sb("nul", [P, 1])
        arena = sb("arena", [P, 21504])

        def at(start, n=T):
            assert start + n <= 21504
            return arena[:, start:start + n]

        def halves(start, n=T):
            return at(start, 2 * n).rearrange("p (a t) -> p a t", a=2)

        stage = at(0, 4 * T).rearrange("p (s t) -> p s t", s=4)
        sqr = halves(2048)
        root, rstd = at(3072), at(3584)
        BASE = 4096
        kv = at(BASE, 16 * M).rearrange("p (c m) -> p c m", c=16)
        vmem = at(BASE + 4096, 2048).rearrange("p (m c) -> p m c", m=2)
        src0 = at(BASE + 6144, 8192).rearrange("p (k t) -> p k t", k=KT)
        src_mem = src0[:, :, 0:M]
        xq = halves(BASE + 6144)
        xz = halves(BASE + 7168)
        xp = at(BASE + 8192, 1024).rearrange("p (b m) -> p b m", b=NB)
        xpT = halves(BASE + 9216)
        xy = halves(BASE + 10240)
        xsm = at(BASE + 11264, 3 * NB).rearrange("p (s b) -> p s b", s=3)
        xrt = halves(BASE + 11776)
        ab = at(18432, 5 * T).rearrange("p (s t) -> p s t", s=5)
        cols = at(20992).rearrange("p (b q h) -> p b q h", b=NB, q=4)
        o_ = BASE
        cv = at(o_, 4 * T).rearrange("p (c t) -> p c t", c=4)
        o_ += 4 * T
        z_in, z_g = halves(o_), halves(o_ + 1024)
        o_ += 2048
        raw = at(o_, T + 3)
        o_ += 520
        gcb = halves(o_)
        o_ += 1024
        qn, kn = at(o_), at(o_ + T)
        o_ += 1024

        def units(start):
            return at(start, 1024).rearrange("p (a n t) -> p a n t", a=2, n=NB)

        Nm, dT, NmT, X, XT, T1, kd, vn = (units(o_ + 1024 * k) for k in range(8))
        ort, yo = halves(o_), halves(o_ + 6 * 1024)
        o_ += 8 * 1024
        St, rr, uu = (at(o_ + 256 * k, 256).rearrange("p (a t) -> p a t", a=2) for k in range(3))
        o_ += 768
        cb = at(o_, 32).rearrange("p (b q a) -> p b q a", b=NB, q=4)
        cw = at(o_ + 32, 16)
        ke, qd = (at(o_ + 48), kn), (at(o_ + 48 + T), qn)
        assert o_ + 48 + 2 * T <= 20992
        xt = at(BASE, 8192).rearrange("p (k t) -> p k t", k=KT)
        ys = at(BASE + 8192, 8192).rearrange("p (k t) -> p k t", k=KT)

        o_ = BASE
        m_raw = at(o_, T + 3)
        mc, mv, m_o, m_z, m_g, m_rows, m_h, m_y = (halves(o_ + 520 + 1024 * k) for k in range(8))
        o_ += 520 + 8192
        m_s = at(o_, NB * T).rearrange("p (n t) -> p n t", n=NB)
        m_vn = at(o_ + 2048, 1024).rearrange("p (a n t) -> p a n t", a=2, n=NB)
        m_den = at(o_ + 3072)
        m_conv = at(o_ + 3584, 12)
        m_gain = at(o_ + 3600, 2)
        m_cb = at(o_ + 3604, NB)
        mcols = at(20992, NB * MLH).rearrange("p (n h) -> p n h", n=NB)
        h_par = at(21024, 3 * HGH).rearrange("p (h c) -> p h c", c=3)
        h_tmp = at(21056, HGH)
        o_ = BASE
        (h_gate, h_q, h_k, h_b, h_eb) = (at(o_ + T * k) for k in range(5))
        hg_in, hq_in, hf_in, hi_in = m_o[:, 0, :], m_o[:, 1, :], m_z[:, 0, :], m_z[:, 1, :]
        o_ += 520 + 4 * 1024
        (h_d, h_w0, h_w1, h_a, h_vn, h_kdt, h_kd, h_qe, h_s, h_rt, h_y, h_d1) = (at(o_ + T * k) for k in range(12))
        h_hp = at(o_ + T * 12, 3)
        ets = ys
        pe_src = at(20480, 1024).rearrange("p (k t) -> p k t", k=2)

        gemm_ps = [ctx.enter_context(nc.psum_tensor(f"gemm_ps{i}", [P, T], F32)) for i in range(2)]
        bankA, bankB, bankC = (ctx.enter_context(nc.psum_tensor(f"bank{x}", [P, 2, T], F32)) for x in "ABC")

        def quad(bank):
            return bank[:, :, :].rearrange("p a (n t) -> p a n t", n=NB)

        y_dram = nc.dram_tensor("y_scratch", [2 * KT, P, T], F32)
        x2_dram = nc.dram_tensor("x2_scratch", [P, KT, T], F32)
        y2_dram = nc.dram_tensor("y2_scratch", [KT, P, T], F32)
        ml_dram = nc.dram_tensor("ml_scratch", [MLH, 2, T], F32)
        gc_dram = nc.dram_tensor("gc_scratch", [VH, T], F32)

        dve_step, act_step, pool_step, pad = sem("dve_step"), sem("act_step"), sem("pool_step"), sem("pad")
        const_loaded, filled = sem("const_loaded"), sem("filled")
        raw_loaded = [sem("raw_loaded0"), sem("raw_loaded1")]
        cut = [sem("cut0"), sem("cut1")]
        gemm_done = [sem("gemm_done0"), sem("gemm_done1")]
        evicted = [sem("evicted0"), sem("evicted1")]
        names = ("src_loaded staged act_hi act_lo squared sq_summed root_ready rstd_ready "
                 "kv_sq kv_sum kv_root kv_norm vT_done v_done "
                 "ab_exp ab_x rows_ready colsT cols_ready gc_stored "
                 "q_sq q_sum q_root q_norm s_done max_ready p_exp p_norm pT_done pT_sbuf o_done z_silu y_ready y_stored "
                 "conv silu dq_sq dq_sum dq_root dq_norm nat nat_v pair vn_sbuf diff expd n_ready nT nT_sbuf x_ready "
                 "t1 t1_sbuf dd lvl rk r_ready u u_sbuf o s_ready o_sq o_sum o_root dy_ready dy_stored gate gc_loaded "
                 "ys_loaded out_ready out_stored "
                 "g_x g_exp g_rowsT mcols_ready ml_stored h_lb h_lbexp x2_stored "
                 "m_conv m_silu m_gated m_gate ml_loaded mvT m_vn m_diff m_expd m_sc m_scd m_den m_num m_dencp m_hd m_sq "
                 "m_sum m_root m_yr m_yst "
                 "h_cut h_sig h_fb h_ln h_vT h_vns h_qk h_diag h_dr h_ex h_wr h_pr h_pred h_ebx h_kx h_kxe h_kdr h_kT "
                 "h_kds h_st h_sr h_o h_osq h_osum h_ort h_yr h_yst h_gs "
                 "e_done e_out sg_out sq_run sq_acc run_summed x_new kd_ready mem_hi0 mem_hi1 early_y0 early_y1 early_x x2_loaded").split()
        s = {n: sem(n) for n in names}
        act_hi, act_lo = s["act_hi"], s["act_lo"]
        block = ctx.enter_context(nc.Block())

        def gains(c, n=1):
            return par[:, c:c + n]

        def used_before(tile, slot):
            return (tile + 1 - slot) // 2

        FILLS = [W_MEM, W_AB, W_OUT, W_OUT + KT, W_GATE, W_OUT2, W_PE, W_PG]
        CUT_AT = [0, KT, 2 * KT, 3 * KT, 4 * KT, 5 * KT, 6 * KT, 6 * KT + 2]
        GAINED = {0: 0, 1: 1, 4: 2, 7: 3}

        @block.sync
        def _(sp):
            for w in range(2):
                sp.dma_start(w_raw[:, w, :, :], weights[w]).then_inc(raw_loaded[w], 16)
            with sp.Fori(0, (W_END + 1) // 2 - 1) as i:
                for w in range(2):
                    sp.wait_ge(cut[w], i + 1)
                    sp.dma_start(w_raw[:, w, :, :], weights[bass.ds(2 * i + 2 + w, 1)].rearrange(
                        "a p k c -> p (a k) c")).then_inc(raw_loaded[w], 16)
            for w in range(2):
                sp.wait_ge(raw_loaded[w], 16 * ((W_END + 1) // 2))

        @block.gpsimd
        def _(pool):
            def low_tile(w, n):
                pool.wait_ge(s[f"mem_hi{w}"], n + 1)
                pool.tensor_tensor(w_lo[:, w, :, :], w_raw[:, w, :, :], w_hi[:, w, :, :].bitcast(F32),
                                   ALU.subtract).then_inc(cut[w], 1)

            def cut_tile(w, n, i):
                pool.wait_ge(raw_loaded[w], 16 * n + 16)
                if True:
                    pool.wait_ge(gemm_done[w], n)
                pool.tensor_tensor(w_hi[:, w, :, :].rearrange("p k c -> p (k c)"),
                                   w_raw[:, w, :, :].rearrange("p k c -> p (k c)"),
                                   nul[:, 0:1].to_broadcast([P, KT * P]), ALU.add).then_inc(pool_step, 1)
                pool.wait_ge(pool_step, 2 * i + w + 1)
                pool.tensor_tensor(w_lo[:, w, :, :], w_raw[:, w, :, :], w_hi[:, w, :, :].bitcast(F32),
                                   ALU.subtract).then_inc(cut[w], 1)

            pool.wait_ge(filled, 2)
            with pool.Fori(0, W_AB // 2) as i:
                for w in range(2):
                    low_tile(w, i)
            with pool.Fori(0, (W_END - W_AB) // 2) as i:
                for w in range(2):
                    cut_tile(w, i + W_AB // 2, i)

        @block.tensor
        def _(pe):
            def gemm(base, c, k, fill=None, i=0, per=0, width=T):
                slot, n = tile_at(base, c, i, per)
                if k == 0:
                    pe.wait_ge(cut[slot], n + 1)
                    if not (isinstance(n, int) and n == 0):
                        pe.wait_ge(evicted[slot], n)
                if fill is not None:
                    pe.wait_ge(act_lo, CUT_AT[fill] + k + 1)
                o = gemm_ps[slot][:, 0:width]
                hi, lo = w_hi[:, slot, k, :], w_lo[:, slot, k, :]
                pe.matmul(o, hi, a_hi[:, k, 0:width], start=(k == 0), stop=False)
                pe.matmul(o, hi, a_lo[:, k, 0:width], start=False, stop=False)
                last = pe.matmul(o, lo, a_hi[:, k, 0:width], start=False, stop=(k == KT - 1))
                if k == KT - 1:
                    last.then_inc(gemm_done[slot], 1)

            def square_sums(q, width=T):
                for k in range(KT):
                    pe.wait_ge(s["squared"], KT * q + k + 1)
                    pe.matmul(bankA[:, 0, 0:width], ones, sqr[:, k % 2, 0:width], start=(k == 0),
                              stop=(k == KT - 1)).then_inc(s["sq_summed"], 1)

            pe.wait_ge(const_loaded, 48)
            square_sums(0, M)
            for c in range(W_AB):
                for k in range(KT):
                    gemm(W_MEM, c, k, 0 if c == 0 else None, width=M)
            for h in range(XH):
                pe.wait_ge(s["kv_sq"], h + 1)
                for d in range(2):
                    last = pe.matmul(bankA[:, h // 2, h % 2 * M:h % 2 * M + M], ones,
                                     sqr[:, h % 2, d * M:d * M + M], start=(d == 0), stop=(d == 1))
                last.then_inc(s["kv_sum"], 1)
            pe.wait_ge(evicted[1], W_AB // 2)
            for c in range(8):
                bank = bankB if c < 4 else bankC
                for m in range(2):
                    last = pe.transpose(bank[:, m, c % 4 * P:c % 4 * P + P], kv[:, 8 + c, m * P:m * P + P],
                                        ident)
            last.then_inc(s["vT_done"], 1)

            pe.wait_ge(s["kv_root"], XH)
            square_sums(1)
            for k in range(KT):
                gemm(W_AB, 0, k, 1)
            pe.wait_ge(s["rows_ready"], 1)
            for n in range(NB):
                last = pe.transpose(bankB[:, 0, n * P:n * P + P], ab[:, 3, n * P:n * P + P], ident)
            last.then_inc(s["colsT"], 1)

            for h in range(XH):
                for step in XA_ORDER:
                    if step[0] == "gemm":
                        gemm(W_XA + 4 * h, step[1], step[2])
                    elif step[0] == "q_norm":
                        pe.wait_ge(s["q_sq"], h + 1)
                        for d in range(2):
                            last = pe.matmul(bankA[:, 0, :], ones, sqr[:, d, :], start=(d == 0), stop=(d == 1))
                        last.then_inc(s["q_sum"], 1)
                    elif step[0] == "scores":
                        pe.wait_ge(s["q_norm"], h + 1)
                        if h == 0:
                            pe.wait_ge(s["kv_norm"], XH)
                            pe.wait_ge(s["cols_ready"], 1)
                        else:
                            pe.wait_ge(s["y_ready"], 2 * h)
                        for n in range(NB):
                            o = bankB[:, n // 2, n % 2 * M:n % 2 * M + M]
                            for d in range(2):
                                last = pe.matmul(o, xq[:, d, n * P:n * P + P], kv[:, 2 * h + d, :],
                                                 start=(d == 0), stop=(d == 1))
                        last.then_inc(s["s_done"], 1)
                    elif step[0] == "weights":
                        pe.wait_ge(s["p_norm"], h + 1)
                        if h == 0:
                            pe.wait_ge(s["v_done"], 2)
                        for n in range(NB):
                            for m in range(2):
                                last = pe.transpose(bankC[:, m, n * P:n * P + P], xp[:, n, m * P:m * P + P], ident)
                        last.then_inc(s["pT_done"], 1)
                    elif step[0] == "values":
                        pe.wait_ge(s["pT_sbuf"], h + 1)
                        for d in range(2):
                            for m in range(2):
                                last = pe.matmul(bankB[:, d, :], vmem[:, m, (2 * h + d) * P:(2 * h + d) * P + P],
                                                 xpT[:, m, :], start=(m == 0), stop=(m == 1))
                        last.then_inc(s["o_done"], 1)

            def dn_mix(step, j):
                if step[0] == "qk_norm":
                    for a in range(2):
                        pe.wait_ge(s["dq_sq"], 2 * j + a + 1)
                        pe.matmul(bankA[:, a, :], ones, sqr[:, a, :], start=True, stop=True).then_inc(s["dq_sum"], 1)
                elif step[0] == "natural":
                    pe.wait_ge(s["dq_norm"], 2 * j + 2)
                    for n in range(NB):
                        last = pe.transpose(bankB[:, 0, n * P:n * P + P], kn[:, n * P:n * P + P], ident)
                    last.then_inc(s["nat"], 1)
                    pe.wait_ge(s["silu"], 4 * j + 4)
                    for a in range(2):
                        for n in range(NB):
                            last = pe.transpose(bankC[:, a, n * P:n * P + P], cv[:, 2 + a, n * P:n * P + P], ident)
                    last.then_inc(s["nat_v"], 1)
                    for n in range(NB):
                        b = slice(n * P, n * P + P)
                        pe.matmul(bankA[:, 0, b], kn[:, b], kn[:, b], start=True, stop=True)
                        last = pe.matmul(bankA[:, 1, b], kn[:, b], qn[:, b], start=True, stop=True)
                    last.then_inc(s["pair"], 1)
                elif step[0] == "transposed":
                    pe.wait_ge(s["n_ready"], j + 1)
                    pe.wait_ge(s["vn_sbuf"], 2 * j + 2)
                    for a in range(2):
                        for n in range(NB):
                            last = pe.transpose(quad(bankC)[:, a, n, :], Nm[:, a, n, :], ident)
                    last.then_inc(s["nT"], 1)
                elif step[0] == "half":
                    pe.wait_ge(s["x_ready"], j + 1)
                    if step[1] > 1:
                        pe.wait_ge(s["lvl"], (LEVELS - 1) * j + step[1] - 1)
                    else:
                        pe.wait_ge(s["nT_sbuf"], j + 1)
                    for a in range(2):
                        for n in range(NB):
                            last = pe.matmul(quad(bankA)[:, a, n, :], NmT[:, a, n, :], X[:, a, n, :],
                                             start=True, stop=True)
                    last.then_inc(s["t1"], 1)
                elif step[0] == "whole":
                    pe.wait_ge(s["t1_sbuf"], (LEVELS - 1) * j + step[1])
                    if step[1] == 1:
                        pe.wait_ge(s["kd_ready"], j + 1)
                    for a in range(2):
                        for n in range(NB):
                            if step[1] < LEVELS - 1:
                                pe.matmul(quad(bankB)[:, a, n, :], XT[:, a, n, :], T1[:, a, n, :],
                                          start=True, stop=True)
                            last = pe.matmul(quad(bankC)[:, a, n, :], T1[:, a, n, :], XT[:, a, n, :],
                                             start=True, stop=True)
                    last.then_inc(s["dd"], 1)
                elif step[0] == "rest":
                    if step[1] > 0:
                        pe.wait_ge(s["s_ready"], 3 * j + step[1])
                        for a in range(2):
                            last = pe.matmul(bankA[:, 0, a * P:a * P + P], ke[a][:, step[1] * P:step[1] * P + P],
                                             St[:, a, :], start=True, stop=True)
                        last.then_inc(s["rk"], 1)
                elif step[0] == "update":
                    pe.wait_ge(s["r_ready"], NB * j + step[1] + 1)
                    for a in range(2):
                        last = pe.matmul(bankB[:, 0, a * P:a * P + P], XT[:, a, step[1], :], rr[:, a, :],
                                         start=True, stop=True)
                    last.then_inc(s["u"], 1)
                elif step[0] == "output":
                    n = step[1]
                    pe.wait_ge(s["u_sbuf"], NB * j + n + 1)
                    for a in range(2):
                        o = bankC[:, a, n * P:n * P + P]
                        if n > 0:
                            pe.matmul(o, St[:, a, :], qd[a][:, n * P:n * P + P], start=True, stop=False)
                        last = pe.matmul(o, uu[:, a, :], dT[:, a, n, :], start=(n == 0), stop=True)
                    if n < NB - 1:
                        for a in range(2):
                            last = pe.matmul(bankA[:, 1, a * P:a * P + P], kd[:, a, n, :], uu[:, a, :],
                                             start=True, stop=True)
                    last.then_inc(s["o"], 1)
                elif step[0] == "head_out":
                    for a in range(2):
                        pe.wait_ge(s["o_sq"], 2 * j + a + 1)
                        pe.matmul(bankB[:, a, :], ones, sqr[:, a, :], start=True, stop=True).then_inc(s["o_sum"], 1)

            def dn_trip(g, j, tiles=True, mix=True):
                for step in interleave(6 if tiles else 0, DN_STEPS if mix else []):
                    if step[0] == "gemm":
                        gemm(W_DN, step[1], step[2], None, g, 6)
                    elif step[0] != "evict":
                        dn_mix(step, j)

            dn_trip(0, None, mix=False)
            with pe.Fori(0, QKH - 1) as j:
                dn_trip(j + 1, j)
            for step in interleave(EARLY, DN_STEPS):
                if step[0] == "gemm":
                    gemm(W_OUT, step[1], step[2], 2 if step[1] == 0 else None)
                elif step[0] != "evict":
                    dn_mix(step, QKH - 1)

            with pe.Fori(0, (KT - EARLY) // 2) as i:
                for c in range(2):
                    for k in range(KT):
                        gemm(W_OUT + EARLY, c, k, None, i, 2)
            for k in range(KT):
                gemm(W_OUT + KT, 0, k, 3)
            for k in range(KT):
                gemm(W_OUT + KT, 1, k)
            with pe.Fori(0, KT // 2 - 1) as i:
                for c in range(2):
                    for k in range(KT):
                        gemm(W_OUT + KT + 2, c, k, None, i, 2)

            def run_sum(q):
                pe.wait_ge(s["sq_acc"], KT * (q - 1))
                pe.matmul(bankA[:, 0, :], ones, root, start=True, stop=True).then_inc(s["run_summed"], 1)

            pe.wait_ge(s["o_root"], 2 * QKH)
            run_sum(2)
            for k in range(KT):
                gemm(W_GATE, 0, k, 4)
            pe.wait_ge(s["g_x"], 4)
            for n in range(NB):
                last = pe.transpose(bankB[:, 0, n * MLH:n * MLH + MLH], ab[0:MLH, 1, n * P:n * P + P],
                                    ident[0:MLH, 0:MLH])
            last.then_inc(s["g_rowsT"], 1)

            def ml_mix(step, j):
                if step[0] == "ml_scores":
                    for a in range(2):
                        slot, n = tile_at(W_ML, 6 + a, j, 8)
                        pe.wait_ge(evicted[slot], n + 1)
                    for a in range(2):
                        for n in range(NB):
                            last = pe.transpose(bankB[:, a, n * P:n * P + P], mv[:, a, n * P:n * P + P], ident)
                    last.then_inc(s["mvT"], 1)
                    pe.wait_ge(s["m_silu"], 2 * j + 2)
                    for n in range(NB):
                        o = (bankA, bankC)[n // 2][:, n % 2, n * P:T]
                        last = pe.matmul(o, mc[:, 1, n * P:n * P + P], mc[:, 0, n * P:T], start=True, stop=True)
                    last.then_inc(s["m_sc"], 1)
                elif step[0] == "ml_sums":
                    pe.wait_ge(s["m_scd"], j + 1)
                    pe.wait_ge(s["m_vn"], j + 1)
                    for n in range(NB):
                        last = pe.matmul(bankB[:, 0, n * P:T], ones, m_s[:, n, n * P:T], start=(n == 0),
                                         stop=(n == NB - 1))
                    last.then_inc(s["m_den"], 1)
                    for a in range(2):
                        for n in range(NB):
                            last = pe.matmul(bankC[:, a, n * P:T], m_vn[:, a, n, :], m_s[:, n, n * P:T],
                                             start=(n == 0), stop=(n == NB - 1))
                    last.then_inc(s["m_num"], 1)
                elif step[0] == "ml_out":
                    pe.wait_ge(s["m_sq"], j + 1)
                    for a in range(2):
                        last = pe.matmul(bankA[:, 0, :], ones, sqr[:, a, :], start=(a == 0), stop=(a == 1))
                    last.then_inc(s["m_sum"], 1)

            def ml_trip(g, j, tiles=True, mix=True):
                for step in interleave(8 if tiles else 0, ML_STEPS if mix else []):
                    if step[0] == "gemm":
                        gemm(W_ML, step[1], step[2], None, g, 8)
                    elif step[0] != "evict":
                        ml_mix(step, j)

            ml_trip(0, None, mix=False)
            with pe.Fori(0, MLH - 1) as j:
                ml_trip(j + 1, j)
            for step in interleave(4, ML_STEPS):
                if step[0] == "gemm":
                    gemm(W_HG, step[1], step[2])
                elif step[0] != "evict":
                    ml_mix(step, MLH - 1)

            def hg_mix(step, j):
                if step[0] == "hg_prep":
                    pe.wait_ge(s["h_cut"], j + 1)
                    for n in range(NB):
                        last = pe.transpose(bankB[:, 0, n * P:n * P + P], hi_in[:, n * P:n * P + P], ident)
                    last.then_inc(s["h_vT"], 1)
                elif step[0] == "hg_diagonal":
                    pe.wait_ge(s["h_qk"], j + 1)
                    pe.matmul(bankB[:, 1, :], ones, h_w1, start=True, stop=True).then_inc(s["h_diag"], 1)
                elif step[0] == "hg_level":
                    l = step[1]
                    pe.wait_ge(s["h_wr"], LEVELS * j + l + 1)
                    w = (h_w0, h_w1)[l % 2]
                    for n in range(NB):
                        b = slice(n * P, n * P + P)
                        last = pe.matmul(bankA[:, l % 2, b], w[:, b], w[:, b], start=True, stop=True)
                    last.then_inc(s["h_pr"], 1)
                elif step[0] == "hg_state":
                    pe.wait_ge(s["h_kdr"], j + 1)
                    for n in range(NB):
                        last = pe.transpose(bankB[:, 0, n * P:n * P + P], h_kdt[:, n * P:n * P + P], ident)
                    last.then_inc(s["h_kT"], 1)
                elif step[0] == "hg_mix":
                    pe.wait_ge(s["h_kds"], j + 1)
                    for n in range(NB - 1):
                        b = slice(n * P, n * P + P)
                        last = pe.matmul(bankB[:, 1, b], h_kd[:, b], h_vn[:, b], start=True, stop=True)
                    last.then_inc(s["h_st"], 1)
                elif step[0] == "hg_out":
                    pe.wait_ge(s["h_sr"], j + 1)
                    pe.wait_ge(s["h_pred"], LEVELS * j + LEVELS)
                    for n in range(NB):
                        b = slice(n * P, n * P + P)
                        last = pe.matmul(bankC[:, 0, b], h_vn[:, b], h_a[:, b], start=True, stop=(n == 0))
                        if n > 0:
                            last = pe.matmul(bankC[:, 0, b], h_s[:, (n - 1) * P:n * P], h_qe[:, b],
                                             start=False, stop=True)
                    last.then_inc(s["h_o"], 1)
                    pe.wait_ge(s["h_osq"], j + 1)
                    pe.matmul(bankC[:, 1, :], ones, sqr[:, 0, :], start=True, stop=True).then_inc(s["h_osum"], 1)

            def hg_trip(g, j, tiles=True, mix=True):
                for step in interleave(4 if tiles else 0, HG_STEPS if mix else []):
                    if step[0] == "gemm":
                        gemm(W_HG, step[1], step[2], None, g, 4)
                    elif step[0] != "evict":
                        hg_mix(step, j)

            with pe.Fori(0, HGH - 1) as j:
                hg_trip(j + 1, j)
            for step in interleave(2, HG_STEPS):
                if step[0] == "gemm":
                    if step[2] < KT - 1:
                        gemm(W_OUT2, step[1], step[2], 5 if step[1] == 0 else None)
                elif step[0] != "evict":
                    hg_mix(step, HGH - 1)

            for c in range(2):
                gemm(W_OUT2, c, KT - 1, 5)
            with pe.Fori(0, KT // 2 - 1) as i:
                for c in range(2):
                    for k in range(KT):
                        gemm(W_OUT2 + 2, c, k, None, i, 2)

            for t in range(2):
                slot, n = tile_at(W_PE, t)
                pe.wait_ge(cut[slot], n + 1)
                for c in range(8):
                    e = 8 * t + c
                    if t == 0 and c < 2:
                        pe.wait_ge(act_lo, CUT_AT[6] + 2)
                        pe.wait_ge(evicted[c], used_before(W_PE, c))
                    else:
                        pe.wait_ge(s["e_out"], e - 1)
                    o = gemm_ps[e % 2][:, :]
                    for k in range(2):
                        hi, lo = w_hi[:, slot, 2 * c + k, :], w_lo[:, slot, 2 * c + k, :]
                        pe.matmul(o, hi, a_hi[:, k, :], start=(k == 0), stop=False)
                        pe.matmul(o, hi, a_lo[:, k, :], start=False, stop=False)
                        last = pe.matmul(o, lo, a_hi[:, k, :], start=False, stop=(k == 1))
                    if c < 7:
                        last.then_inc(s["e_done"], 1)
                    else:
                        last.then_inc(gemm_done[slot], 1)

            pe.wait_ge(s["h_yr"], HGH)
            run_sum(3)
            pe.wait_ge(s["e_out"], 16)
            for c in range(2):
                for k in range(KT):
                    gemm(W_PG, c, k, 7 if c == 0 else None)
            with pe.Fori(0, KT // 2 - 1) as i:
                for c in range(2):
                    for k in range(KT):
                        gemm(W_PG + 2, c, k, None, i, 2)
            run_sum(4)

        @block.vector
        def _(v):
            d = Steps(v, dve_step, pad)

            def op(make, *args, sem=None, value=None):
                d.wait()
                d.did(make(*args), sem, value)

            def copy_after(make, *args, sem=None, value=None):
                d.wait()
                d.settle()
                d.did(make(*args), sem, value)

            def scaled(dst, base, c, i=0, per=0, width=T, rows=P):
                slot, n = tile_at(base, c, i, per)
                v.wait_ge(gemm_done[slot], n + 1)
                op(v.tensor_tensor, dst, gemm_ps[slot][0:rows, 0:width], rstd[0:rows, 0:width], ALU.mult,
                   sem=evicted[slot], value=n + 1)

            def reciprocal_root(q, width=T):
                v.wait_ge(s["root_ready"], q + 1)
                op(v.reciprocal, rstd[:, 0:width], root[:, 0:width], sem=s["rstd_ready"], value=q + 1)

            def fill(f, src, gain, width=T, blocks=KT):
                for w in range(2):
                    if used_before(FILLS[f], w):
                        v.wait_ge(gemm_done[w], used_before(FILLS[f], w))

                def product(k):
                    op(v.tensor_scalar, stage[:, k % 4, 0:width], src[:, k, :], gains(gain + k), None, ALU.mult,
                       sem=s["staged"], value=KT * GAINED[f] + k + 1)

                for k in range(blocks):
                    if gain is not None:
                        for kk in ((0, 1, 2) if k == 0 else (k + 2,)):
                            if kk < KT:
                                product(kk)
                    v.wait_ge(act_hi, CUT_AT[f] + k + 1)
                    op(v.tensor_tensor, a_lo[:, k, 0:width],
                       stage[:, k % 4, 0:width] if gain is not None else src[:, k, :],
                       a_hi[:, k, 0:width].bitcast(F32), ALU.subtract, sem=act_lo, value=CUT_AT[f] + k + 1)

            op(v.memset, eps[:, :], EPS, sem=filled, value=1)
            op(v.memset, nul[:, :], 0.0, sem=filled, value=2)
            op(v.memset, ab[:, 3, :], 0.0)
            v.wait_ge(const_loaded, 48)

            v.wait_ge(s["src_loaded"], 16)
            fill(0, src_mem, C_MEMN, M)
            reciprocal_root(0, M)
            for c in range(W_AB):
                scaled(kv[:, c, :], W_MEM, c, width=M)
            for h in range(XH):
                v.wait_ge(s["kv_root"], h + 1)
                op(v.reciprocal, stage[:, h, 0:M], stage[:, h, 0:M])
                for e in range(2):
                    op(v.scalar_tensor_tensor, kv[:, 2 * h + e, :], kv[:, 2 * h + e, :], gains(C_XK + e),
                       stage[:, h, 0:M], ALU.mult, ALU.mult, sem=s["kv_norm"] if e else None, value=h + 1)

            v.wait_ge(s["src_loaded"], 32)
            fill(1, src0, C_NORM)
            reciprocal_root(1)
            scaled(ab[0:64, 0, :], W_AB, 0, rows=64)
            op(v.tensor_scalar, ab[0:64, 0, :], ab[0:64, 0, :], par[0:64, C_DT:C_DT + 1], None, ALU.add,
               sem=s["ab_x"], value=1)
            op(v.scalar_tensor_tensor, ab[0:VH, 1, :], ab[0:VH, 0, :], -1.0, ab[0:VH, 0, :], ALU.mult, ALU.max,
               sem=s["ab_x"], value=2)
            v.wait_ge(s["ab_exp"], 1)
            op(v.tensor_scalar, ab[0:VH, 1, :], ab[0:VH, 1, :], 1.0, None, ALU.add, sem=s["ab_x"], value=3)
            v.wait_ge(s["ab_exp"], 4)
            op(v.scalar_tensor_tensor, ab[0:VH, 0, :], ab[0:VH, 0, :], 0.0, ab[0:VH, 1, :], ALU.max, ALU.add)
            op(v.tensor_scalar, ab[0:VH, 0, :], ab[0:VH, 0, :], ab[0:VH, 4, 0:1], -1.0, ALU.mult, ALU.mult)
            for n in range(NB):
                b = slice(n * P, n * P + P)
                op(v.tensor_tensor_scan, ab[0:VH, 3, b], ones[0:VH, :], ab[0:VH, 0, b], 0.0, ALU.mult, ALU.add)
            gc_rows = ab[0:VH, 3, :].rearrange("p (n t) -> p n t", n=NB)
            op(v.tensor_tensor, ab[0:VH, 1, :].rearrange("p (n t) -> p n t", n=NB),
               gc_rows[:, :, P - 1:P].to_broadcast([VH, NB, P]), gc_rows, ALU.subtract, sem=s["ab_x"], value=4)
            op(v.tensor_scalar, ab[32:32 + VH, 3, :], ab[32:32 + VH, 2, :], -1.0, None, ALU.mult)
            op(v.tensor_copy, ab[96:96 + VH, 3, :], ab[32:32 + VH, 2, :])
            v.wait_ge(s["ab_exp"], 5)
            op(v.tensor_copy, ab[64:64 + VH, 3, :], ab[0:VH, 1, :], sem=s["rows_ready"], value=1)
            v.wait_ge(s["colsT"], 1)
            op(v.tensor_copy, at(20992), bankB[:, 0, :], sem=s["cols_ready"], value=1)

            for h in range(XH):
                for step in XA_ORDER:
                    if step[0] == "evict":
                        c = step[1]
                        if c >= 2 and h > 0:
                            v.wait_ge(s["y_ready"], 2 * h)
                        scaled((xq, xz)[c // 2][:, c % 2, :], W_XA + 4 * h, c)
                    elif step[0] == "q_norm":
                        v.wait_ge(s["q_root"], h + 1)
                        op(v.reciprocal, xrt[:, 0, :], xrt[:, 0, :])
                        for e in range(2):
                            op(v.scalar_tensor_tensor, xq[:, e, :], xq[:, e, :], gains(C_XQ + e), xrt[:, 0, :],
                               ALU.mult, ALU.mult, sem=s["q_norm"] if e else None, value=h + 1)
                    elif step[0] == "scores":
                        v.wait_ge(s["s_done"], h + 1)
                        op(v.tensor_reduce, xsm[:, 0, :], bankB[:, :, :].rearrange("p a (b m) -> p (a b) m", m=M),
                           AX.X, ALU.max)
                        op(v.tensor_scalar, xsm[:, 1, :], xsm[:, 0, :], -1.0 / 16, None, ALU.mult,
                           sem=s["max_ready"], value=h + 1)
                        v.wait_ge(s["p_exp"], NB * (h + 1))
                        op(v.reciprocal, xsm[:, 2, :], xsm[:, 2, :])
                        for n in range(NB):
                            op(v.tensor_scalar, xp[:, n, :], xp[:, n, :], xsm[:, 2, n:n + 1], None, ALU.mult,
                               sem=s["p_norm"] if n == NB - 1 else None, value=h + 1)
                    elif step[0] == "values":
                        v.wait_ge(s["o_done"], h + 1)
                        v.wait_ge(s["z_silu"], 2 * h + 2)
                        if h > 0:
                            v.wait_ge(s["y_stored"], 16 * h)
                        for e in range(2):
                            op(v.tensor_tensor, xy[:, e, :], bankB[:, e, :], xz[:, e, :], ALU.mult,
                               sem=s["y_ready"], value=2 * h + e + 1)

            def dn_evict(c, g):
                if c < 2:
                    if not (isinstance(g, int) and g == 0):
                        v.wait_ge(s["gate"], 2 * g)
                    scaled(z_in[:, c, :], W_DN, c, g, 6)
                    return
                if c == 2:
                    v.wait_ge(evicted[1], 1)
                    if not isinstance(g, int):
                        d.wait()
                        d.settle()
                    v.tensor_copy(cw, par[:, bass.ds(C_DNCONV + 16 * g, 16)] if not isinstance(g, int)
                                  else par[:, C_DNCONV + 16 * g:C_DNCONV + 16 * g + 16]).then_inc(dve_step, 1)
                    d.k += 1
                    d.last = (dve_step, d.start + d.loop + d.k)
                scaled(raw[:, 3:T + 3], W_DN, c, g, 6)
                o = cv[:, c - 2, :]
                tap = 4 * (c - 2)
                op(v.tensor_scalar, o, raw[:, 0:T], cw[:, tap:tap + 1], None, ALU.mult)
                for t in range(1, 4):
                    op(v.scalar_tensor_tensor, o, raw[:, t:t + T], cw[:, tap + t:tap + t + 1], o, ALU.mult, ALU.add,
                       sem=s["conv"] if t == 3 else None, value=4 * g + c - 1)

            def dn_mix(step, j):
                if step[0] == "qk_norm":
                    d.wait()
                    d.settle()
                    d.did(v.tensor_copy(cb, cols[:, :, :, bass.ds(2 * j, 2)] if not isinstance(j, int)
                                        else cols[:, :, :, 2 * j:2 * j + 2]))
                    for a, (dst, scale) in enumerate(((qn, P ** -0.5), (kn, 1.0))):
                        v.wait_ge(s["dq_root"], 2 * j + a + 1)
                        op(v.reciprocal, T1[:, a, 0:NB, :].rearrange("p n t -> p (n t)"),
                           T1[:, a, 0:NB, :].rearrange("p n t -> p (n t)"))
                        op(v.scalar_tensor_tensor, dst, cv[:, a, :], scale,
                           T1[:, a, 0:NB, :].rearrange("p n t -> p (n t)"), ALU.mult, ALU.mult,
                           sem=s["dq_norm"], value=2 * j + a + 1)
                    v.wait_ge(s["gc_loaded"], 16 * j + 16)
                    for a in range(2):
                        for n in range(NB):
                            g_row = gcb[:, a, n * P:n * P + P]
                            op(v.tensor_scalar, dT[:, a, n, :], g_row, cb[:, n, 0, a:a + 1], 0.0,
                               ALU.subtract, ALU.min)
                            op(v.tensor_scalar, Nm[:, a, n, :], g_row, cb[:, n, 0, a:a + 1], 0.0,
                               ALU.subtract, ALU.max,
                               sem=s["diff"] if (a, n) == (1, NB - 1) else None, value=j + 1)
                elif step[0] == "natural":
                    v.wait_ge(s["pair"], j + 1)
                    v.wait_ge(s["expd"], 3 * j + 2)
                    for a in range(2):
                        for n in range(NB):
                            op(v.scalar_tensor_tensor, Nm[:, a, n, :], bankA[:, 0, n * P:n * P + P],
                               cb[:, n, 1, a:a + 1], Nm[:, a, n, :], ALU.mult, ALU.mult,
                               sem=s["n_ready"] if (a, n) == (1, NB - 1) else None, value=j + 1)
                    for a in range(2):
                        op(v.tensor_tensor, dT[:, a, :, :], dT[:, a, :, :], quad(bankA)[:, 1, :, :], ALU.mult)
                elif step[0] == "transposed":
                    flat = "p a n t -> p (a n) t"
                    for dst in (X, XT):
                        op(v.tensor_copy, dst[:, :, :, :].rearrange(flat), ident[:, None, :].to_broadcast([P, 8, P]))
                    copy_after(v.copy_predicated, X[:, :, :, :].rearrange(flat),
                               low[:, 0:1, :].to_broadcast([P, 8, P]), Nm[:, :, :, :].rearrange(flat))
                    v.wait_ge(s["nT_sbuf"], j + 1)
                    copy_after(v.copy_predicated, XT[:, :, :, :].rearrange(flat),
                               lowT[:, 0:1, :].to_broadcast([P, 8, P]), quad(bankC).rearrange(flat),
                               sem=s["x_ready"], value=j + 1)
                    op(v.tensor_tensor, dT[:, :, :, :].rearrange(flat), dT[:, :, :, :].rearrange(flat),
                       incl[:, None, :].to_broadcast([P, 8, P]), ALU.mult)
                    v.wait_ge(s["dy_stored"], 16 * j + 16)
                    for a in range(2):
                        for n in range(NB):
                            op(v.tensor_scalar, kd[:, a, n, :], bankB[:, 0, n * P:n * P + P],
                               cb[:, n, 2, a:a + 1], None, ALU.mult,
                               sem=s["kd_ready"] if (a, n) == (1, NB - 1) else None, value=j + 1)
                elif step[0] == "half" and step[1] == 2:
                    v.wait_ge(s["expd"], 3 * j + 3)
                    for a in range(2):
                        op(v.tensor_tensor, ke[a], kn, gcb[:, a, :], ALU.mult)
                        op(v.tensor_tensor, qd[a], qn, gcb[:, a, :], ALU.mult)
                elif step[0] == "whole":
                    flat = "p a n t -> p (a n) t"
                    v.wait_ge(s["dd"], (LEVELS - 1) * j + step[1])
                    if step[1] < LEVELS - 1:
                        copy_after(v.copy_predicated, X[:, :, :, :].rearrange(flat),
                                   low[:, step[1]:step[1] + 1, :].to_broadcast([P, 8, P]), quad(bankB).rearrange(flat))
                    copy_after(v.copy_predicated, XT[:, :, :, :].rearrange(flat),
                               lowT[:, step[1]:step[1] + 1, :].to_broadcast([P, 8, P]), quad(bankC).rearrange(flat),
                               sem=s["lvl"], value=(LEVELS - 1) * j + step[1])
                elif step[0] == "rest":
                    n = step[1]
                    if n == 0:
                        v.wait_ge(s["vn_sbuf"], 2 * j + 2)
                        for a in range(2):
                            op(v.tensor_scalar, rr[:, a, :], vn[:, a, 0, :], cb[:, 0, 3, a:a + 1], None, ALU.mult,
                               sem=s["r_ready"] if a else None, value=NB * j + 1)
                    else:
                        v.wait_ge(s["rk"], 3 * j + n)
                        op(v.tensor_tensor, rr[:, :, :], vn[:, :, n, :],
                           bankA[:, 0, 0:2 * P].rearrange("p (a t) -> p a t", a=2), ALU.subtract)
                        for a in range(2):
                            op(v.tensor_scalar, rr[:, a, :], rr[:, a, :], cb[:, n, 3, a:a + 1], None, ALU.mult,
                               sem=s["r_ready"] if a else None, value=NB * j + n + 1)
                elif step[0] == "output":
                    n = step[1]
                    if n < NB - 1:
                        v.wait_ge(s["o"], NB * j + n + 1)
                        for a in range(2):
                            dS = bankA[:, 1, a * P:a * P + P]
                            mark = dict(sem=s["s_ready"] if a else None, value=3 * j + n + 1)
                            if n == 0:
                                op(v.tensor_copy, St[:, a, :], dS, **mark)
                            else:
                                op(v.scalar_tensor_tensor, St[:, a, :], St[:, a, :],
                                   gcb[:, a, n * P + P - 1:n * P + P], dS, ALU.mult, ALU.add, **mark)
                elif step[0] == "head_out":
                    v.wait_ge(s["gate"], 2 * j + 2)
                    for a in range(2):
                        v.wait_ge(s["o_root"], 2 * j + a + 1)
                        op(v.reciprocal, ort[:, a, :], ort[:, a, :])
                        op(v.scalar_tensor_tensor, yo[:, a, :], bankC[:, a, :], gains(C_DNOUT), ort[:, a, :],
                           ALU.mult, ALU.mult)
                        op(v.tensor_tensor, yo[:, a, :], yo[:, a, :], z_g[:, a, :], ALU.mult,
                           sem=s["dy_ready"], value=2 * j + a + 1)

            def dn_trip(g, j, tiles=True, mix=True):
                for step in interleave(6 if tiles else 0, DN_STEPS if mix else []):
                    if step[0] == "evict":
                        dn_evict(step[1], g)
                    elif step[0] != "gemm":
                        dn_mix(step, j)

            op(v.memset, raw[:, 0:3], 0.0)
            v.sem_inc(s["dy_stored"], 16)
            dn_trip(0, None, mix=False)
            with v.Fori(0, QKH - 1) as j:
                d.enter(j, DN_VECTOR_STEPS)
                dn_trip(j + 1, j)
            d.leave(QKH - 1)

            def add_tile(dst, base, c, i=0, per=0, q=None):
                slot, n = tile_at(base, c, i, per)
                v.wait_ge(gemm_done[slot], n + 1)
                op(v.tensor_tensor, dst, gemm_ps[slot][:, :], dst, ALU.add, sem=evicted[slot], value=n + 1)
                if q is not None:
                    add_squares(q, c if per == 0 else 2 * i + 2 + c, c)

            def add_squares(q, k, c):
                done = KT * (q - 2) + k + 1
                v.wait_ge(s["sq_run"], done)
                if isinstance(k, int) and k == 0:
                    op(v.tensor_copy, root, sqr[:, c, :], sem=s["sq_acc"], value=done)
                else:
                    op(v.tensor_tensor, root, root, sqr[:, c, :], ALU.add, sem=s["sq_acc"], value=done)

            for w in range(2):
                v.wait_ge(gemm_done[w], used_before(W_OUT, w))
            for step in interleave(EARLY, DN_STEPS):
                if step[0] == "gemm":
                    if step[1] == 0:
                        k = step[2]
                        v.wait_ge(act_hi, CUT_AT[2] + k + 1)
                        op(v.tensor_tensor, a_lo[:, k, :], stage[:, k % 4, :], a_hi[:, k, :].bitcast(F32),
                           ALU.subtract, sem=act_lo, value=CUT_AT[2] + k + 1)
                elif step[0] == "evict":
                    if step[1] == 1:
                        v.wait_ge(s["early_x"], 16)
                        add_tile(xt[:, 0, :], W_OUT, 0)
                    if step[1] > 0:
                        add_tile(xt[:, step[1], :], W_OUT, step[1])
                else:
                    dn_mix(step, QKH - 1)
            v.wait_ge(s["src_loaded"], 48)
            with v.Fori(0, (KT - EARLY) // 2) as i:
                d.enter(i, 0)
                for c in range(2):
                    add_tile(xt[:, bass.ds(2 * i + EARLY + c, 1), :].rearrange("p k t -> p (k t)"),
                             W_OUT + EARLY, c, i, 2)
            d.leave((KT - EARLY) // 2)
            v.wait_ge(s["ys_loaded"], 16)
            fill(3, ys, None)
            for c in range(2):
                add_tile(xt[:, c, :], W_OUT + KT, c, q=2)
            with v.Fori(0, KT // 2 - 1) as i:
                d.enter(i, 0)
                for c in range(2):
                    add_tile(xt[:, bass.ds(2 * i + 2 + c, 1), :].rearrange("p k t -> p (k t)"),
                             W_OUT + KT + 2, c, i, 2, 2)
            d.leave(KT // 2 - 1)

            fill(4, xt, C_NORM2)
            reciprocal_root(2)
            op(v.tensor_tensor, h_tmp, par[:, C_HGL + HGH:C_HGL + 2 * HGH], par[:, C_HGL:C_HGL + HGH], ALU.subtract,
               sem=s["h_lb"], value=1)
            v.wait_ge(s["h_lbexp"], 1)
            op(v.tensor_scalar, h_tmp, h_tmp, 1.0, None, ALU.add)
            op(v.reciprocal, h_par[:, :, 0], h_tmp)
            op(v.tensor_scalar, h_par[:, :, 1], h_par[:, :, 0], -1.0, 1.0, ALU.mult, ALU.add)
            op(v.tensor_copy, h_par[:, :, 2], par[:, C_HGN:C_HGN + HGH])
            scaled(ab[0:64, 0, :], W_GATE, 0, rows=64)
            op(v.tensor_scalar, ab[0:64, 0, :], ab[0:64, 0, :], par[0:64, C_IFB:C_IFB + 1], None, ALU.add)
            f_ = ab[32:32 + MLH, 0, :]
            f1 = ab[32:32 + MLH, 1, :]
            op(v.scalar_tensor_tensor, f1, f_, -1.0, f_, ALU.mult, ALU.max, sem=s["g_x"], value=1)
            v.wait_ge(s["g_exp"], 1)
            op(v.tensor_scalar, f1, f1, 1.0, None, ALU.add, sem=s["g_x"], value=2)
            v.wait_ge(s["g_exp"], 2)
            op(v.scalar_tensor_tensor, f1, f_, 0.0, f1, ALU.min, ALU.subtract)
            op(v.tensor_copy, ab[0:MLH, 2, :], f1)
            for n in range(NB):
                b = slice(n * P, n * P + P)
                op(v.tensor_tensor_scan, ab[0:MLH, 3, b], ones[0:MLH, :], ab[0:MLH, 2, b],
                   0.0 if n == 0 else ab[0:MLH, 3, n * P - 1:n * P], ALU.mult, ALU.add)
            op(v.tensor_tensor, ab[0:MLH, 1, :], ab[0:MLH, 0, :], ab[0:MLH, 3, :], ALU.subtract)
            for n in range(NB):
                b = slice(n * P, n * P + P)
                op(v.tensor_tensor_scan, ab[0:MLH, 4, b], ones[0:MLH, :], ab[0:MLH, 1, b],
                   0.0 if n == 0 else ab[0:MLH, 4, n * P - 1:n * P], ALU.mult, ALU.max)
            op(v.tensor_tensor, ab[0:MLH, 2, :], ab[0:MLH, 3, :], ab[0:MLH, 4, :], ALU.add, sem=s["g_x"], value=3)
            op(v.tensor_scalar, ab[0:MLH, 3, :], ab[0:MLH, 4, :], -1.0, None, ALU.mult, sem=s["g_x"], value=4)
            v.wait_ge(s["g_rowsT"], 1)
            op(v.tensor_copy, at(20992, NB * MLH), bankB[:, 0, 0:NB * MLH], sem=s["mcols_ready"], value=1)

            v.wait_ge(s["x2_stored"], 16)
            op(v.memset, m_raw[:, 0:3], 0.0)

            def head_copy(dst, src, at0, i, n):
                d.wait()
                d.settle()
                d.did(v.tensor_copy(dst, src[:, at0 + n * i:at0 + n * i + n] if isinstance(i, int)
                                    else src[:, bass.ds(at0 + n * i, n)]))

            def ml_evict(c, g):
                if c < 4:
                    if not (isinstance(g, int) and g == 0):
                        v.wait_ge(s["m_gated"], g)
                    scaled((m_o, m_z)[c // 2][:, c % 2, :], W_ML, c, g, 8)
                    return
                if c == 4:
                    head_copy(m_conv, par, C_ML, g, 12)
                if c >= 6:
                    scaled(mv[:, c - 6, :], W_ML, c, g, 8)
                    return
                scaled(m_raw[:, 3:T + 3], W_ML, c, g, 8)
                o, tap = mc[:, c - 4, :], 4 * (c - 4)
                op(v.tensor_scalar, o, m_raw[:, 0:T], m_conv[:, tap:tap + 1], m_conv[:, 8 + c - 4:9 + c - 4],
                   ALU.mult, ALU.add)
                for t in range(1, 4):
                    op(v.scalar_tensor_tensor, o, m_raw[:, t:t + T], m_conv[:, tap + t:tap + t + 1], o,
                       ALU.mult, ALU.add, sem=s["m_conv"] if t == 3 else None, value=2 * g + c - 3)

            def ml_mix(step, j):
                if step[0] == "ml_scores":
                    d.wait()
                    d.settle()
                    d.did(v.tensor_copy(m_cb, mcols[:, :, j] if isinstance(j, int)
                                        else mcols[:, :, bass.ds(j, 1)].rearrange("p n h -> p (n h)")))
                    d.wait()
                    d.settle()
                    d.did(v.tensor_copy(m_gain, par[:, C_ML + 12 * j + 10:C_ML + 12 * j + 12] if isinstance(j, int)
                                        else par[:, bass.ds(C_ML + 10 + 12 * j, 2)]))
                    v.wait_ge(s["ml_loaded"], 16 * j + 16)
                    for n in range(NB):
                        op(v.tensor_scalar, m_s[:, n, n * P:T], m_rows[:, 0, n * P:T], m_cb[:, n:n + 1], 0.0,
                           ALU.add, ALU.min, sem=s["m_diff"], value=NB * j + n + 1)
                    v.wait_ge(s["m_sc"], j + 1)
                    for n in range(NB):
                        v.wait_ge(s["m_expd"], NB * j + n + 1)
                        op(v.scalar_tensor_tensor, m_s[:, n, n * P:T], (bankA, bankC)[n // 2][:, n % 2, n * P:T],
                           P ** -0.5, m_s[:, n, n * P:T], ALU.mult, ALU.mult)
                        b = slice(n * P, n * P + P)
                        op(v.tensor_tensor, m_s[:, n, b], m_s[:, n, b], incl, ALU.mult,
                           sem=s["m_scd"] if n == NB - 1 else None, value=j + 1)
                elif step[0] == "ml_sums":
                    v.wait_ge(s["m_dencp"], j + 1)
                    op(v.scalar_tensor_tensor, m_den, m_den, -1.0, m_den, ALU.mult, ALU.max)
                    op(v.tensor_tensor, m_den, m_den, m_rows[:, 1, :], ALU.max)
                    op(v.reciprocal, m_den, m_den)
                    v.wait_ge(s["m_num"], j + 1)
                    for a in range(2):
                        op(v.tensor_tensor, m_h[:, a, :], bankC[:, a, :], m_den, ALU.mult,
                           sem=s["m_hd"] if a else None, value=j + 1)
                elif step[0] == "ml_out":
                    v.wait_ge(s["m_root"], j + 1)
                    op(v.reciprocal, m_den, m_den)
                    v.wait_ge(s["m_gated"], j + 1)
                    for a in range(2):
                        op(v.scalar_tensor_tensor, m_h[:, a, :], m_h[:, a, :], m_gain[:, a:a + 1], m_den,
                           ALU.mult, ALU.mult)
                        op(v.tensor_tensor, m_y[:, a, :], m_h[:, a, :], m_g[:, a, :], ALU.mult,
                           sem=s["m_yr"] if a else None, value=j + 1)

            def ml_trip(g, j, tiles=True, mix=True):
                for step in interleave(8 if tiles else 0, ML_STEPS if mix else []):
                    if step[0] == "evict":
                        ml_evict(step[1], g)
                    elif step[0] != "gemm":
                        ml_mix(step, j)
                if tiles:
                    v.wait_ge(s["m_gate"], g + 1)
                    op(v.tensor_tensor, m_g[:, :, :], m_o[:, :, :], m_z[:, :, :], ALU.mult,
                       sem=s["m_gated"], value=g + 1)
                d.wait()

            ml_trip(0, None, mix=False)
            with v.Fori(0, MLH - 1) as j:
                d.enter(j, ML_VECTOR_STEPS)
                ml_trip(j + 1, j)
            d.leave(MLH - 1)

            def hg_evict(c, g):
                first = isinstance(g, int) and g == 0
                if c == 0 and not first:
                    v.wait_ge(s["h_gs"], g)
                if c == 3 and not first:
                    v.wait_ge(s["h_vT"], g)
                scaled((hg_in, hq_in, hf_in, hi_in)[c], W_HG, c, g, 4)

            v.wait_ge(s["m_gated"], MLH)
            for step in interleave(4, ML_STEPS):
                if step[0] == "evict":
                    hg_evict(step[1], 0)
                elif step[0] != "gemm":
                    ml_mix(step, MLH - 1)
            v.wait_ge(s["m_yst"], 16 * MLH)

            def by_pair(x, l):
                return x.rearrange("p (b t) -> p b t", t=2 << l)

            blocks = "p (n t) -> p n t"

            def exponents(l, j):
                h = 1 << l
                bv, dv = by_pair(h_b, l), by_pair((h_d, h_d1)[l % 2], l)
                ref = bv[:, :, h - 1:h].to_broadcast([P, T // (2 * h), h])
                op(v.tensor_tensor, dv[:, :, h:2 * h], bv[:, :, h:2 * h], ref, ALU.subtract)
                op(v.tensor_tensor, dv[:, :, 0:h], ref, bv[:, :, 0:h], ALU.subtract,
                   sem=s["h_dr"], value=LEVELS * j + l + 1)

            def merge(l, j):
                v.wait_ge(s["h_pr"], LEVELS * j + l + 1)
                d.wait()
                d.settle()
                d.did(v.copy_predicated(h_a.rearrange(blocks, n=NB), lowT[:, l:l + 1, :].to_broadcast([P, NB, P]),
                                        bankA[:, l % 2, :].rearrange(blocks, n=NB)),
                      s["h_pred"], LEVELS * j + l + 1)

            def hg_mix(step, j):
                if step[0] == "hg_prep":
                    d.wait()
                    d.settle()
                    d.did(v.tensor_copy(h_hp, h_par[:, j, :] if isinstance(j, int)
                                        else h_par[:, bass.ds(j, 1), :].rearrange("p h c -> p (h c)")))
                    op(v.tensor_copy, h_q, hq_in, sem=s["h_cut"], value=j + 1)
                    v.wait_ge(s["h_sig"], 2 * j + 2)
                    op(v.tensor_scalar, h_b, h_eb, h_hp[:, 1:2], h_hp[:, 0:1], ALU.mult, ALU.add,
                       sem=s["h_fb"], value=j + 1)
                    op(v.tensor_scalar, h_k, h_d, h_hp[:, 1:2], None, ALU.mult)
                    v.wait_ge(s["h_ln"], j + 1)
                    for n in range(NB):
                        b = slice(n * P, n * P + P)
                        op(v.tensor_tensor_scan, h_b[:, b], ones, h_eb[:, b], 0.0, ALU.mult, ALU.add)
                    op(v.tensor_tensor, h_w1, h_q, h_k, ALU.mult, sem=s["h_qk"], value=j + 1)
                elif step[0] == "hg_diagonal":
                    v.wait_ge(s["h_diag"], j + 1)
                    op(v.tensor_tensor, h_a.rearrange(blocks, n=NB), bankB[:, 1, :].rearrange(blocks, n=NB),
                       ident[:, None, :].to_broadcast([P, NB, P]), ALU.mult)
                elif step[0] == "hg_level":
                    l = step[1]
                    h = 1 << l
                    w = (h_w0, h_w1)[l % 2]
                    dv = by_pair((h_d, h_d1)[l % 2], l)
                    if l == 0:
                        exponents(0, j)
                    if l + 1 < LEVELS:
                        exponents(l + 1, j)
                    v.wait_ge(s["h_ex"], LEVELS * j + l + 1)
                    op(v.tensor_tensor, by_pair(w, l)[:, :, h:2 * h], by_pair(h_q, l)[:, :, h:2 * h],
                       dv[:, :, h:2 * h], ALU.mult)
                    op(v.tensor_tensor, by_pair(w, l)[:, :, 0:h], by_pair(h_k, l)[:, :, 0:h],
                       dv[:, :, 0:h], ALU.mult, sem=s["h_wr"], value=LEVELS * j + l + 1)
                    if l > 0:
                        merge(l - 1, j)
                elif step[0] == "hg_state":
                    merge(LEVELS - 1, j)
                    b3 = h_b.rearrange(blocks, n=NB)
                    op(v.tensor_tensor, h_d.rearrange(blocks, n=NB), b3[:, :, P - 1:P].to_broadcast([P, NB, P]), b3,
                       ALU.subtract, sem=s["h_kx"], value=j + 1)
                    v.wait_ge(s["h_kxe"], j + 1)
                    op(v.tensor_tensor, h_kdt, h_k, h_d, ALU.mult, sem=s["h_kdr"], value=j + 1)
                    v.wait_ge(s["h_ebx"], j + 1)
                    op(v.tensor_tensor, h_qe, h_q, h_eb, ALU.mult)
                elif step[0] == "hg_mix":
                    v.wait_ge(s["h_st"], j + 1)
                    op(v.tensor_copy, h_s[:, 0:P], bankB[:, 1, 0:P])
                    for n in range(1, NB - 1):
                        b = slice(n * P, n * P + P)
                        op(v.scalar_tensor_tensor, h_s[:, b], h_s[:, (n - 1) * P:n * P],
                           h_eb[:, n * P + P - 1:n * P + P], bankB[:, 1, b], ALU.mult, ALU.add,
                           sem=s["h_sr"] if n == NB - 2 else None, value=j + 1)
                elif step[0] == "hg_out":
                    v.wait_ge(s["h_ort"], j + 1)
                    v.wait_ge(s["h_gs"], j + 1)
                    op(v.reciprocal, h_rt, h_rt)
                    op(v.scalar_tensor_tensor, h_rt, bankC[:, 0, :], h_hp[:, 2:3], h_rt, ALU.mult, ALU.mult)
                    op(v.tensor_tensor, h_y, h_rt, h_gate, ALU.mult, sem=s["h_yr"], value=j + 1)

            def hg_trip(g, j, tiles=True, mix=True):
                for step in interleave(4 if tiles else 0, HG_STEPS if mix else []):
                    if step[0] == "evict":
                        hg_evict(step[1], g)
                    elif step[0] != "gemm":
                        hg_mix(step, j)

            with v.Fori(0, HGH - 1) as j:
                d.enter(j, HG_VECTOR_STEPS)
                hg_trip(j + 1, j)
            d.leave(HGH - 1)
            def low_part(f, k, src):
                v.wait_ge(act_hi, CUT_AT[f] + k + 1)
                op(v.tensor_tensor, a_lo[:, k, :], src, a_hi[:, k, :].bitcast(F32), ALU.subtract,
                   sem=act_lo, value=CUT_AT[f] + k + 1)

            for w in range(2):
                v.wait_ge(gemm_done[w], used_before(W_OUT2, w))
            for step in interleave(2, HG_STEPS):
                if step[0] == "gemm":
                    if step[1] == 0 and step[2] < KT - 1:
                        low_part(5, step[2], stage[:, step[2] % 4, :])
                elif step[0] != "evict":
                    hg_mix(step, HGH - 1)
            low_part(5, KT - 1, h_y)

            v.wait_ge(s["x2_loaded"], 16)
            for c in range(2):
                add_tile(xt[:, c, :], W_OUT2, c, q=3)
            v.wait_ge(s["src_loaded"], 64)
            with v.Fori(0, KT // 2 - 1) as i:
                d.enter(i, 0)
                for c in range(2):
                    add_tile(xt[:, bass.ds(2 * i + 2 + c, 1), :].rearrange("p k t -> p (k t)"),
                             W_OUT2 + 2, c, i, 2, 3)
            d.leave(KT // 2 - 1)

            v.wait_ge(s["src_loaded"], 80)
            fill(6, pe_src, None, blocks=2)
            for e in range(16):
                slot, n = tile_at(W_PE, e // 8)
                if e % 8 < 7:
                    v.wait_ge(s["e_done"], 7 * (e // 8) + e % 8 + 1)
                else:
                    v.wait_ge(gemm_done[slot], n + 1)
                op(v.tensor_copy, ets[:, e, :], gemm_ps[e % 2][:, :], sem=s["e_out"], value=e + 1)

            for w in range(2):
                v.sem_inc(evicted[w], 1)

            fill(7, xt, C_PEN)
            reciprocal_root(3)

            def gated(c, base, i=0, per=0):
                slot, n = tile_at(base, c, i, per)
                k = c if per == 0 else 2 * i + 2 + c
                x_, e_ = ((xt[:, k, :], ets[:, k, :]) if isinstance(k, int) else
                          (a[:, bass.ds(k, 1), :].rearrange("p k t -> p (k t)") for a in (xt, ets)))
                v.wait_ge(gemm_done[slot], n + 1)
                op(v.tensor_tensor, stage[:, c, :], gemm_ps[slot][:, :], rstd, ALU.mult, sem=evicted[slot],
                   value=n + 1)
                v.wait_ge(s["sg_out"], k + 1)
                op(v.tensor_tensor, stage[:, c, :], stage[:, c, :], e_, ALU.mult)
                op(v.tensor_tensor, x_, x_, stage[:, c, :], ALU.add, sem=s["x_new"], value=k + 1)
                add_squares(4, k, c)

            for c in range(2):
                gated(c, W_PG)
            with v.Fori(0, KT // 2 - 1) as i:
                d.enter(i, 2)
                for c in range(2):
                    gated(c, W_PG + 2, i, 2)
            d.leave(KT // 2 - 1)

            reciprocal_root(4)
            for k in range(KT):
                op(v.scalar_tensor_tensor, xt[:, k, :], xt[:, k, :], gains(C_FIN + k), rstd, ALU.mult, ALU.mult,
                   sem=s["out_ready"], value=k + 1)

        @block.scalar
        def _(act):
            d = Steps(act, act_step, pad)

            def op(dst, src, func, sem=None, value=None, **kw):
                d.wait()
                d.did(act.activation(dst, src, func, **kw), sem, value)

            def squares_and_high(q, f, src, width=T, gain=True, blocks=KT):
                if f is not None:
                    for w in range(2):
                        if used_before(FILLS[f], w):
                            act.wait_ge(gemm_done[w], used_before(FILLS[f], w))
                for k in range(blocks):
                    if q is not None:
                        if KT * q + k >= 2:
                            act.wait_ge(s["sq_summed"], KT * q + k - 1)
                        op(sqr[:, k % 2, 0:width], src[:, k, :], ACT.Square, s["squared"], KT * q + k + 1)
                    if f is not None:
                        if gain:
                            act.wait_ge(s["staged"], KT * GAINED[f] + k + 1)
                        op(a_hi[:, k, 0:width], stage[:, k % 4, 0:width] if gain else src[:, k, :], ACT.Copy,
                           act_hi, CUT_AT[f] + k + 1)
                if q is not None:
                    act.wait_ge(s["sq_summed"], KT * q + KT)
                    op(root[:, 0:width], bankA[:, 0, 0:width], ACT.Sqrt, s["root_ready"], q + 1,
                       bias=eps[:, :], scale=1.0 / D)

            act.dma_start(src_mem, memT).then_inc(s["src_loaded"], 16)
            act.dma_start(par[:, :], params).then_inc(const_loaded, 16)
            act.dma_start(con[:, 0:4, :], consts[:, 0:4, :]).then_inc(const_loaded, 16)
            act.dma_start(con[:, 4:4 + 2 * LEVELS, :], consts[:, 4:4 + 2 * LEVELS, :]).then_inc(const_loaded, 16)
            def high_tile(t):
                w, n = tile_at(W_MEM, t)
                act.wait_ge(raw_loaded[w], 16 * n + 16)
                if n > 0:
                    act.wait_ge(gemm_done[w], n)
                op(w_hi[:, w, :, :], w_raw[:, w, :, :], ACT.Copy, s[f"mem_hi{w}"], n + 1)

            act.wait_ge(filled, 2)
            for t in range(2):
                high_tile(t)
            act.wait_ge(s["src_loaded"], 16)
            squares_and_high(0, 0, src_mem, M)
            for t in range(2, W_AB):
                high_tile(t)
            act.wait_ge(s["squared"], KT)
            act.wait_ge(s["staged"], KT)
            act.dma_start(src0, xT).then_inc(s["src_loaded"], 16)
            for h in range(XH):
                act.wait_ge(evicted[1], h + 1)
                if h >= 2:
                    act.wait_ge(s["kv_sum"], h - 1)
                op(sqr[:, h % 2, :], kv[:, 2 * h:2 * h + 2, :].rearrange("p c m -> p (c m)"), ACT.Square,
                   s["kv_sq"], h + 1)
            act.wait_ge(s["kv_sum"], XH)
            for h in range(XH):
                op(stage[:, h, 0:M], bankA[:, h // 2, h % 2 * M:h % 2 * M + M], ACT.Sqrt, s["kv_root"], h + 1,
                   bias=eps[:, :], scale=1.0 / (2 * P))
            act.wait_ge(s["vT_done"], 1)
            for b, bank in enumerate((bankB, bankC)):
                op(vmem[:, :, b * T:b * T + T], bank[:, :, :], ACT.Copy, s["v_done"], b + 1)

            act.wait_ge(s["src_loaded"], 32)
            squares_and_high(1, 1, src0)
            act.wait_ge(s["ab_x"], 1)
            op(ab[32:32 + VH, 2, :], ab[32:32 + VH, 0, :], ACT.Sigmoid)
            act.wait_ge(s["ab_x"], 2)
            op(ab[0:VH, 1, :], ab[0:VH, 1, :], ACT.Exp, s["ab_exp"], 1, scale=-1.0)
            op(ab[0:VH, 4, 0:1], par[0:VH, C_ALOG:C_ALOG + 1], ACT.Exp, s["ab_exp"], 2)
            act.wait_ge(s["ab_x"], 3)
            op(ab[0:VH, 1, :], ab[0:VH, 1, :], ACT.Ln, s["ab_exp"], 3)
            op(ab[0:VH, 4, 1:2], ab[0:VH, 4, 0:1], ACT.Copy, s["ab_exp"], 4)
            act.wait_ge(s["ab_x"], 4)
            act.dma_start(gc_dram[:, :], ab[0:VH, 3, :]).then_inc(s["gc_stored"], 16)
            op(ab[0:VH, 1, :], ab[0:VH, 1, :], ACT.Exp, s["ab_exp"], 5)
            act.wait_ge(s["gc_stored"], 16)

            for h in range(XH):
                for step in XA_ORDER:
                    if step[0] == "evict" and step[1] >= 2:
                        slot, n = tile_at(W_XA + 4 * h, step[1])
                        act.wait_ge(evicted[slot], n + 1)
                        op(xz[:, step[1] - 2, :], xz[:, step[1] - 2, :], ACT.Silu, s["z_silu"], 2 * h + step[1] - 1)
                    elif step[0] == "q_norm":
                        slot, n = tile_at(W_XA + 4 * h, 1)
                        act.wait_ge(evicted[slot], n + 1)
                        op(sqr[:, :, :], xq[:, :, :], ACT.Square, s["q_sq"], h + 1)
                        act.wait_ge(s["q_sum"], h + 1)
                        op(xrt[:, 0, :], bankA[:, 0, :], ACT.Sqrt, s["q_root"], h + 1, bias=eps[:, :],
                           scale=1.0 / (2 * P))
                    elif step[0] == "scores":
                        act.wait_ge(s["max_ready"], h + 1)
                        if h > 0:
                            act.wait_ge(s["pT_done"], h)
                        for n in range(NB):
                            op(xp[:, n, :], bankB[:, n // 2, n % 2 * M:n % 2 * M + M], ACT.Exp, s["p_exp"],
                               NB * h + n + 1, bias=xsm[:, 1, n:n + 1], scale=1.0 / 16, accum_out=xsm[:, 2, n:n + 1])
                    elif step[0] == "weights":
                        act.wait_ge(s["pT_done"], h + 1)
                        op(xpT[:, :, :], bankC[:, :, :], ACT.Copy, s["pT_sbuf"], h + 1)
                    elif step[0] == "values":
                        act.wait_ge(s["y_ready"], 2 * h + 2)
                        act.dma_start(y_dram[VH + 2 * h:VH + 2 * h + 2].rearrange("a p t -> p a t"),
                                      xy[:, :, :]).then_inc(s["y_stored"], 16)

            def load_decay(j):
                rows = gc_dram[bass.ds(2 * j, 2), :] if not isinstance(j, int) else gc_dram[2 * j:2 * j + 2, :]
                act.dma_start(gcb[:, :, :], rows[None, :, :].to_broadcast([P, 2, T])).then_inc(s["gc_loaded"], 16)

            def gates(g):
                for c in range(2):
                    slot, n = tile_at(W_DN, c, g, 6)
                    act.wait_ge(evicted[slot], n + 1)
                    op(z_g[:, c, :], z_in[:, c, :], ACT.Silu, s["gate"], 2 * g + c + 1)

            def qk_roots(g):
                for a in range(2):
                    op(sqr[:, a, :], cv[:, a, :], ACT.Square, s["dq_sq"], 2 * g + a + 1)
                for a in range(2):
                    act.wait_ge(s["dq_sum"], 2 * g + a + 1)
                    op(T1[:, a, :, :].rearrange("p n t -> p (n t)"), bankA[:, a, :], ACT.Sqrt, s["dq_root"],
                       2 * g + a + 1, bias=eps[:, :])

            def dn_mix(step, j, g=None):
                if step[0] == "qk_norm":
                    act.wait_ge(s["diff"], j + 1)
                    op(dT[:, :, :, :], dT[:, :, :, :], ACT.Exp, s["expd"], 3 * j + 1)
                    op(Nm[:, :, :, :], Nm[:, :, :, :], ACT.Exp, s["expd"], 3 * j + 2, scale=-1.0)
                    op(gcb[:, :, :], gcb[:, :, :], ACT.Exp, s["expd"], 3 * j + 3)
                elif step[0] == "natural":
                    act.wait_ge(s["nat_v"], j + 1)
                    for a in range(2):
                        op(vn[:, a, :, :].rearrange("p n t -> p (n t)"), bankC[:, a, :], ACT.Copy, s["vn_sbuf"],
                           2 * j + a + 1)
                elif step[0] == "transposed":
                    act.wait_ge(s["nT"], j + 1)
                    op(NmT[:, :, :, :], quad(bankC), ACT.Copy, s["nT_sbuf"], j + 1)
                elif step[0] == "half":
                    act.wait_ge(s["t1"], (LEVELS - 1) * j + step[1])
                    op(T1[:, :, :, :], quad(bankA), ACT.Copy, s["t1_sbuf"], (LEVELS - 1) * j + step[1])
                elif step[0] == "update":
                    act.wait_ge(s["u"], NB * j + step[1] + 1)
                    op(uu[:, :, :], bankB[:, 0, 0:2 * P].rearrange("p (a t) -> p a t", a=2), ACT.Copy, s["u_sbuf"],
                       NB * j + step[1] + 1)
                    if step[1] == NB - 1 and g is not None:
                        act.wait_ge(s["s_ready"], 3 * j + 3)
                        load_decay(g)
                elif step[0] == "head_out":
                    act.wait_ge(s["o"], NB * j + NB)
                    for a in range(2):
                        op(sqr[:, a, :], bankC[:, a, :], ACT.Square, s["o_sq"], 2 * j + a + 1)
                    for a in range(2):
                        act.wait_ge(s["o_sum"], 2 * j + a + 1)
                        op(ort[:, a, :], bankB[:, a, :], ACT.Sqrt, s["o_root"], 2 * j + a + 1, bias=eps[:, :],
                           scale=1.0 / P)
                    if g is not None:
                        qk_roots(g)
                    act.wait_ge(s["dy_ready"], 2 * j + 2)
                    y_rows = y_dram[bass.ds(2 * j, 2)] if not isinstance(j, int) else y_dram[2 * j:2 * j + 2]
                    act.dma_start(y_rows.rearrange("a p t -> p a t"), yo[:, :, :]).then_inc(s["dy_stored"], 16)

            def dn_trip(g, j, mix=True):
                for step in interleave(6, DN_STEPS if mix else []):
                    if step[0] == "evict" and step[1] >= 2:
                        act.wait_ge(s["conv"], 4 * g + step[1] - 1)
                        op(cv[:, step[1] - 2, :], cv[:, step[1] - 2, :], ACT.Silu, s["silu"], 4 * g + step[1] - 1)
                    elif step[0] not in ("gemm", "evict"):
                        dn_mix(step, j, g)
                if not mix:
                    qk_roots(g)
                    load_decay(g)
                gates(g)

            dn_trip(0, None, mix=False)
            with act.Fori(0, QKH - 1) as j:
                d.enter(j, 0)
                dn_trip(j + 1, j)
            d.leave(QKH - 1)

            def load_early(k):
                act.dma_start(stage[:, k % 4:k % 4 + 2, :], y_dram[k:k + 2].rearrange("a p t -> p a t")).then_inc(
                    s[f"early_y{k // 2 % 2}"], 16)

            act.wait_ge(s["dy_stored"], 16 * QKH)
            for k in range(0, 4, 2):
                load_early(k)
            for w in range(2):
                act.wait_ge(gemm_done[w], used_before(W_OUT, w))
            for step in interleave(EARLY, DN_STEPS):
                if step[0] == "gemm":
                    if step[1] == 0:
                        k = step[2]
                        act.wait_ge(s[f"early_y{k // 2 % 2}"], 16 * (k // 4) + 16)
                        op(a_hi[:, k, :], stage[:, k % 4, :], ACT.Copy, act_hi, CUT_AT[2] + k + 1)
                        if k % 2 == 0 and 2 <= k < KT - 2:
                            act.wait_ge(act_hi, CUT_AT[2] + k)
                            act.wait_ge(act_lo, CUT_AT[2] + k)
                            load_early(k + 2)
                elif step[0] != "evict":
                    dn_mix(step, QKH - 1)
                    if step[0] == "natural":
                        act.wait_ge(s["dq_norm"], 2 * QKH)
                        act.wait_ge(s["gate"], 2 * QKH)
                        act.dma_start(xt[:, 0:EARLY, :], xT[:, 0:EARLY, :]).then_inc(s["early_x"], 16)
            act.wait_ge(s["dy_stored"], 16 * QKH + 16)

            act.dma_start(xt[:, EARLY:KT, :], xT[:, EARLY:KT, :]).then_inc(s["src_loaded"], 16)
            act.wait_ge(s["y_stored"], 16 * XH)
            act.dma_start(ys, y_dram[KT:2 * KT].rearrange("a p t -> p a t")).then_inc(s["ys_loaded"], 16)
            act.wait_ge(s["ys_loaded"], 16)
            squares_and_high(None, 3, ys, gain=False)

            def run_square(q, k, c):
                if not isinstance(k, int) or KT * (q - 2) + k >= 2:
                    act.wait_ge(s["sq_acc"], KT * (q - 2) + k - 1)
                src = xt[:, k, :] if isinstance(k, int) else xt[:, bass.ds(k, 1), :].rearrange("p k t -> p (k t)")
                d.wait()
                d.settle()
                d.did(act.activation(sqr[:, c, :], src, ACT.Square), s["sq_run"], KT * (q - 2) + k + 1)

            def run_squares(q, base):
                def one(k, c, slot, n):
                    act.wait_ge(evicted[slot], n + 1)
                    run_square(q, k, c)

                for c in range(2):
                    one(c, c, *tile_at(base, c))
                with act.Fori(0, KT // 2 - 1) as i:
                    d.enter(i, 0)
                    for c in range(2):
                        one(2 * i + 2 + c, c, *tile_at(base + 2, c, i, 2))
                d.leave(KT // 2 - 1)

            def run_root(q):
                act.wait_ge(s["run_summed"], q - 1)
                op(root, bankA[:, 0, :], ACT.Sqrt, s["root_ready"], q + 1, bias=eps[:, :], scale=1.0 / D)

            run_squares(2, W_OUT + KT)

            for w in range(2):
                act.wait_ge(evicted[w], used_before(W_GATE, w))
            act.dma_start(x2_dram[:, :, :], xt).then_inc(s["x2_stored"], 16)
            run_root(2)
            squares_and_high(None, 4, xt)
            act.wait_ge(s["h_lb"], 1)
            op(h_tmp, h_tmp, ACT.Exp, s["h_lbexp"], 1)
            f1 = ab[32:32 + MLH, 1, :]
            act.wait_ge(s["g_x"], 1)
            op(f1, f1, ACT.Exp, s["g_exp"], 1, scale=-1.0)
            act.wait_ge(s["g_x"], 2)
            op(f1, f1, ACT.Ln, s["g_exp"], 2)
            act.wait_ge(s["g_x"], 3)
            op(ab[0:MLH, 2, :], ab[0:MLH, 2, :], ACT.Exp, s["g_exp"], 3, scale=-1.0)
            act.wait_ge(s["g_x"], 4)
            act.wait_ge(s["g_exp"], 3)
            act.dma_start(ml_dram[:, 0, :], ab[0:MLH, 3, :]).then_inc(s["ml_stored"], 16)
            act.dma_start(ml_dram[:, 1, :], ab[0:MLH, 2, :]).then_inc(s["ml_stored"], 16)
            act.wait_ge(s["ml_stored"], 32)

            def ml_mix(step, j):
                if step[0] == "ml_scores":
                    act.wait_ge(s["mvT"], j + 1)
                    op(m_vn[:, :, :, :], quad(bankB), ACT.Copy, s["m_vn"], j + 1)
                    for n in range(NB):
                        act.wait_ge(s["m_diff"], NB * j + n + 1)
                        op(m_s[:, n, n * P:T], m_s[:, n, n * P:T], ACT.Exp, s["m_expd"], NB * j + n + 1)
                elif step[0] == "ml_sums":
                    act.wait_ge(s["m_den"], j + 1)
                    op(m_den, bankB[:, 0, :], ACT.Copy, s["m_dencp"], j + 1)
                elif step[0] == "ml_out":
                    act.wait_ge(s["m_hd"], j + 1)
                    op(sqr[:, :, :], m_h[:, :, :], ACT.Square, s["m_sq"], j + 1)
                    act.wait_ge(s["m_sum"], j + 1)
                    op(m_den, bankA[:, 0, :], ACT.Sqrt, s["m_root"], j + 1, bias=eps[:, :], scale=1.0 / (2 * P))
                    act.wait_ge(s["m_yr"], j + 1)
                    y_rows = y2_dram[bass.ds(2 * j, 2)] if not isinstance(j, int) else y2_dram[2 * j:2 * j + 2]
                    act.dma_start(y_rows.rearrange("a p t -> p a t"), m_y[:, :, :]).then_inc(s["m_yst"], 16)

            def ml_trip(g, j, tiles=True, mix=True):
                for step in interleave(8 if tiles else 0, ML_STEPS if mix else []):
                    if step[0] == "evict" and step[1] in (4, 5):
                        act.wait_ge(s["m_conv"], 2 * g + step[1] - 3)
                        op(mc[:, step[1] - 4, :], mc[:, step[1] - 4, :], ACT.Silu, s["m_silu"], 2 * g + step[1] - 3)
                    elif step[0] not in ("gemm", "evict"):
                        ml_mix(step, j)
                if tiles:
                    for c in range(4):
                        slot, n = tile_at(W_ML, c, g, 8)
                        act.wait_ge(evicted[slot], n + 1)
                    op(m_z[:, :, :], m_z[:, :, :], ACT.Silu)
                    op(m_o[:, :, :], m_o[:, :, :], ACT.Sigmoid, s["m_gate"], g + 1)
                    rows = ml_dram[bass.ds(g, 1)].rearrange("h q t -> (h q) t") if not isinstance(g, int) else ml_dram[g]
                    act.dma_start(m_rows[:, :, :], rows[None, :, :].to_broadcast([P, 2, T])).then_inc(
                        s["ml_loaded"], 16)
                if mix:
                    act.wait_ge(s["m_yst"], 16 * j + 16)

            ml_trip(0, None, mix=False)
            with act.Fori(0, MLH - 1) as j:
                d.enter(j, 1)
                ml_trip(j + 1, j)
            d.leave(MLH - 1)
            for step in ML_STEPS:
                ml_mix(step, MLH - 1)
            act.wait_ge(s["m_yst"], 16 * MLH)

            def hg_mix(step, j):
                if step[0] == "hg_prep":
                    slot, n = tile_at(W_HG, 2, j, 4)
                    act.wait_ge(evicted[slot], n + 1)
                    op(h_eb, hf_in, ACT.Sigmoid, s["h_sig"], 2 * j + 1)
                    op(h_d, hf_in, ACT.Sigmoid, s["h_sig"], 2 * j + 2, scale=-1.0)
                    act.wait_ge(s["h_vT"], j + 1)
                    op(h_vn, bankB[:, 0, :], ACT.Copy, s["h_vns"], j + 1)
                    act.wait_ge(s["h_fb"], j + 1)
                    op(h_eb, h_b, ACT.Ln, s["h_ln"], j + 1)
                elif step[0] == "hg_level":
                    act.wait_ge(s["h_dr"], LEVELS * j + step[1] + 1)
                    x = (h_d, h_d1)[step[1] % 2]
                    op(x, x, ACT.Exp, s["h_ex"], LEVELS * j + step[1] + 1)
                    if step[1] == 0:
                        op(h_eb, h_b, ACT.Exp, s["h_ebx"], j + 1)
                elif step[0] == "hg_state":
                    act.wait_ge(s["h_kx"], j + 1)
                    op(h_d, h_d, ACT.Exp, s["h_kxe"], j + 1)
                    act.wait_ge(s["h_kT"], j + 1)
                    op(h_kd, bankB[:, 0, :], ACT.Copy, s["h_kds"], j + 1)
                elif step[0] == "hg_out":
                    act.wait_ge(s["h_o"], j + 1)
                    op(sqr[:, 0, :], bankC[:, 0, :], ACT.Square, s["h_osq"], j + 1)
                    act.wait_ge(s["h_osum"], j + 1)
                    op(h_rt, bankC[:, 1, :], ACT.Sqrt, s["h_ort"], j + 1, bias=eps[:, :], scale=1.0 / P)
                    act.wait_ge(s["h_yr"], j + 1)
                    y_row = y2_dram[bass.ds(j + 2 * MLH, 1)] if not isinstance(j, int) else y2_dram[2 * MLH + j:2 * MLH + j + 1]
                    act.dma_start(y_row.rearrange("a p t -> p (a t)"), h_y).then_inc(s["h_yst"], 16)

            def hg_trip(g, j, tiles=True, mix=True):
                for step in interleave(4 if tiles else 0, HG_STEPS if mix else []):
                    if step[0] not in ("gemm", "evict"):
                        hg_mix(step, j)
                if tiles:
                    slot, n = tile_at(W_HG, 0, g, 4)
                    act.wait_ge(evicted[slot], n + 1)
                    op(h_gate, hg_in, ACT.Silu, s["h_gs"], g + 1)
                if mix:
                    act.wait_ge(s["h_yst"], 16 * j + 16)

            hg_trip(0, None, mix=False)
            with act.Fori(0, HGH - 1) as j:
                d.enter(j, 0)
                hg_trip(j + 1, j)
            d.leave(HGH - 1)

            def load_y2(k):
                n = min(2, KT - 1 - k)
                act.dma_start(stage[:, k % 4:k % 4 + n, :], y2_dram[k:k + n].rearrange("a p t -> p a t")).then_inc(
                    s[f"early_y{k // 2 % 2}"], 16)

            for k in range(0, 4, 2):
                load_y2(k)
            for w in range(2):
                act.wait_ge(gemm_done[w], used_before(W_OUT2, w))
            for step in interleave(2, HG_STEPS):
                if step[0] == "gemm":
                    if step[1] == 0 and step[2] < KT - 1:
                        k = step[2]
                        act.wait_ge(s[f"early_y{k // 2 % 2}"], 16 * (KT // 4 + k // 4) + 16)
                        op(a_hi[:, k, :], stage[:, k % 4, :], ACT.Copy, act_hi, CUT_AT[5] + k + 1)
                        if k % 2 == 0 and 2 <= k < KT - 2:
                            act.wait_ge(act_hi, CUT_AT[5] + k)
                            act.wait_ge(act_lo, CUT_AT[5] + k)
                            load_y2(k + 2)
                elif step[0] != "evict":
                    hg_mix(step, HGH - 1)
            act.wait_ge(s["h_yr"], HGH)
            act.dma_start(xt[:, 0:4, :], x2_dram[:, 0:4, :]).then_inc(s["x2_loaded"], 16)
            op(a_hi[:, KT - 1, :], h_y, ACT.Copy, act_hi, CUT_AT[5] + KT)
            act.wait_ge(act_hi, CUT_AT[5] + KT)
            act.wait_ge(act_lo, CUT_AT[5] + KT)
            act.wait_ge(s["h_yst"], 16 * HGH)

            act.dma_start(xt[:, 4:KT, :], x2_dram[:, 4:KT, :]).then_inc(s["src_loaded"], 16)
            act.wait_ge(s["src_loaded"], 64)
            act.dma_start(pe_src, peT).then_inc(s["src_loaded"], 16)
            run_squares(3, W_OUT2)

            act.wait_ge(s["src_loaded"], 80)
            squares_and_high(None, 6, pe_src, gain=False, blocks=2)
            run_root(3)
            squares_and_high(None, 7, xt)

            def gate(c, base, i=0, per=0):
                slot, n = tile_at(base, c, i, per)
                k = c if per == 0 else 2 * i + 2 + c
                act.wait_ge(evicted[slot], n + 1)
                op(stage[:, c, :], stage[:, c, :], ACT.Sigmoid, s["sg_out"], k + 1)
                act.wait_ge(s["x_new"], k + 1)
                run_square(4, k, c)

            for c in range(2):
                gate(c, W_PG)
            with act.Fori(0, KT // 2 - 1) as i:
                d.enter(i, 0)
                for c in range(2):
                    gate(c, W_PG + 2, i, 2)
            d.leave(KT // 2 - 1)

            run_root(4)
            for k in range(0, KT, 4):
                act.wait_ge(s["out_ready"], k + 4)
                act.dma_start(out[:, k:k + 4, :], xt[:, k:k + 4, :]).then_inc(s["out_stored"], 16)
            act.wait_ge(s["out_stored"], 16 * (KT // 4))


XA_ORDER = ([("gemm", c, k) if k < KT else ("evict", c) for c in range(2) for k in range(KT + 1)]
            + [(x[0], x[1] + 2, *x[2:]) if x[0] in ("gemm", "evict") else x
               for x in interleave(2, [("q_norm", 10), ("scores", 12), ("weights", 4)])]
            + [("values", 0)])
DN_VECTOR_STEPS = 74


def kernel(**inputs):
    import concourse.bacc as bacc
    from concourse.bass_utils import run_bass_kernel_spmd

    f = {n: np.asarray(a) for n, a in inputs.items()}

    def tiles(w):
        k, c = w.shape
        return w.reshape(k // D, KT, P, c // P, P).transpose(0, 3, 2, 1, 4).reshape(-1, P, KT, P)

    def padded(w, at, columns):
        r = np.zeros((D, P), np.float32)
        for start, c in zip(at, columns):
            r[:, start:start + c.shape[1]] = c
        return tiles(r)

    w = f["dn_w_in"][0]
    qk, mix = QKH * P, VH * P
    c_a = 2 * qk + mix
    c_xq = c_a + 2 * VH
    c_z = c_xq + XH * 256
    q_t, k_t, v_t = tiles(w[:, :qk]), tiles(w[:, qk:2 * qk]), tiles(w[:, 2 * qk:c_a])
    xq_t, z_t = tiles(w[:, c_xq:c_z]), tiles(w[:, c_z:])
    w2 = f["w_in_2"][0]
    stream = [tiles(f["mem_w_kv"][0]), padded(w, (0, 32), (w[:, c_a:c_a + VH], w[:, c_a + VH:c_xq]))]
    for h in range(XH):
        stream += [xq_t[2 * h:2 * h + 2], z_t[VH + 2 * h:VH + 2 * h + 2]]
    for h in range(QKH):
        stream += [z_t[2 * h:2 * h + 2], q_t[h:h + 1], k_t[h:h + 1], v_t[2 * h:2 * h + 2]]
    stream += [tiles(f["w_out"][0])]
    c_if = 2 * MLH * P + 3 * MLH * 256
    ml_t, hg_t = tiles(w2[:, :c_if]), tiles(w2[:, c_if + 2 * MLH:])
    stream += [padded(w2, (0, 32), (w2[:, c_if:c_if + MLH], w2[:, c_if + MLH:c_if + 2 * MLH]))]
    for h in range(MLH):
        q, k, v, o, z = h, MLH + h, 2 * MLH + 2 * h, 4 * MLH + 2 * h, 6 * MLH + 2 * h
        stream += [ml_t[o:o + 2], ml_t[z:z + 2], ml_t[q:q + 1], ml_t[k:k + 1], ml_t[v:v + 2]]
    for h in range(HGH):
        stream += [hg_t[c * HGH + h:c * HGH + h + 1] for c in (3, 0, 1, 2)]
    stream += [tiles(f["w_out_2"][0])]
    stream += [f["w_pe_2"][0].reshape(2, P, 2, 8, P).transpose(2, 1, 3, 0, 4).reshape(2, P, KT, P)]
    stream += [tiles(f["w_pg_2"][0])]
    n = sum(len(x) for x in stream)
    stream += [np.zeros((W_END + W_END % 2 - n, P, KT, P), np.float32)]
    stream = np.concatenate(stream)

    def by_row_block(a, width):
        return np.ascontiguousarray(a.T.reshape(-1, P, width).transpose(1, 0, 2))

    params = np.zeros((P, NPAR), np.float32)
    for c, n in ((C_NORM, "norm_g"), (C_MEMN, "mem_norm_g"), (C_XQ, "xa_q_norm_g"), (C_XK, "xa_k_norm_g"),
                 (C_DNOUT, "dn_out_norm_g"), (C_NORM2, "norm_w_2"), (C_PEN, "pe_norm_w_2"), (C_FIN, "final_norm_w_2")):
        g = f[n].reshape(-1, P)
        params[:, c:c + len(g)] = g.T
    params[0:VH, C_ALOG] = f["dn_a_log"][0]
    params[0:VH, C_DT] = f["dn_dt_bias"][0]
    taps = f["dn_conv_w"][0].reshape(4, -1, P)
    for h in range(QKH):
        for c, t in enumerate((h, QKH + h, 2 * QKH + 2 * h, 2 * QKH + 2 * h + 1)):
            params[:, C_DNCONV + 16 * h + 4 * c:C_DNCONV + 16 * h + 4 * c + 4] = taps[:, t, :].T

    params[0:MLH, C_IFB], params[32:32 + MLH, C_IFB] = f["ml_b_i_2"][0], f["ml_b_f_2"][0]
    taps2, bias2, gain2 = f["conv_w_2"][0].reshape(4, -1, P), f["conv_b_2"][0].reshape(-1, P), \
        f["ml_norm_w_2"][0].reshape(-1, P)
    for h in range(MLH):
        c = C_ML + 12 * h
        params[:, c:c + 4], params[:, c + 4:c + 8] = taps2[:, h, :].T, taps2[:, MLH + h, :].T
        params[:, c + 8], params[:, c + 9] = bias2[h], bias2[MLH + h]
        params[:, c + 10], params[:, c + 11] = gain2[2 * h], gain2[2 * h + 1]
    params[:, C_HGL:C_HGL + 2 * HGH] = f["hg_lb_2"].reshape(2 * HGH, P).T
    params[:, C_HGN:C_HGN + HGH] = f["hg_norm_w_2"][0].reshape(HGH, P).T

    consts = np.zeros((P, 4 + 2 * LEVELS, P), np.float32)
    r, c = np.arange(P)[:, None], np.arange(P)[None, :]
    consts[:, 0], consts[:, 1], consts[:, 2] = 1.0, r == c, c >= r
    for n in range(LEVELS):
        m = (r >> (n + 1) == c >> (n + 1)) & (r >> n & 1 == 1) & (c >> n & 1 == 0)
        consts[:, 4 + n], consts[:, 4 + LEVELS + n] = m, m.T

    arrays = {
        "w_stream": stream,
        "x_t": by_row_block(f["x"][0], T),
        "mem_t": by_row_block(f["mem"][0], M),
        "pe_t": by_row_block(f["p_2"][0, 0], T),
        "gains": params,
        "shape_consts": consts,
    }
    nc = bacc.Bacc("TRN2", target_bir_lowering=False, num_devices=1)
    handles = [nc.dram_tensor(n, a.shape, F32, kind="ExternalInput").ap() for n, a in arrays.items()]
    out = nc.dram_tensor("y_out", (P, KT, T), F32, kind="ExternalOutput").ap()
    build(nc, *handles, out)
    got = run_bass_kernel_spmd(nc, [arrays], core_ids=[0]).results[0]["y_out"]
    return np.ascontiguousarray(got.transpose(1, 0, 2).reshape(D, T).T)[None]
```
